# Optimizing a Trainium2 kernel written in Bass

```python
import math
import jax, jax.numpy as jnp
from jax import lax
import numpy as np

D_MODEL = 2048
BATCH = 1
SEQ = 256
DEPTH = 2
DEC_BATCH = 8
DEC_SEQ = 8
PAST_LEN = 2048
PAGE_SIZE = 128

N_A = DEPTH // 2
N_B = DEPTH - N_A
CONV_CH = D_MODEL
CONV_W = 3
N_HEADS = 16
N_KV = 4
GRP = N_HEADS // N_KV
HEAD_DIM = D_MODEL // N_HEADS
N_BRANCH = 3
BLK = 64
N_SEL = 16
WINDOW = 512
Q_BLK = 64
ROPE_THETA = 10000.0
EPS = 1e-6
NEG = -1e30
FORCE = 1e3

kernel_name = 'yoco_shortconv_nsa_step'

def rms_norm(x, g):
    xf = x.astype(jnp.float32)
    y = xf * lax.rsqrt(jnp.mean(xf * xf, axis=-1, keepdims=True) + EPS)
    return (y * g.astype(jnp.float32)).astype(x.dtype)

def rope(x, pos):
    half = x.shape[-1] // 2
    inv = ROPE_THETA ** (-jnp.arange(half, dtype=jnp.float32) / half)
    ang = pos.astype(jnp.float32)[:, None] * inv[None, :]
    shp = (pos.shape[0],) + (1,) * (x.ndim - 3) + (half,)
    c = jnp.cos(ang).reshape(shp)
    s = jnp.sin(ang).reshape(shp)
    xf = x.astype(jnp.float32)
    x1, x2 = xf[..., :half], xf[..., half:]
    return jnp.concatenate([x1 * c - x2 * s, x2 * c + x1 * s], axis=-1).astype(x.dtype)

def masked_softmax(s, mask):
    p = jax.nn.softmax(jnp.where(mask, s.astype(jnp.float32), NEG), axis=-1)
    return jnp.where(mask, p, 0.0)

def short_conv_layer(x, prev, g, w_in, w_conv, w_out):
    T = x.shape[1]
    u = rms_norm(x, g) @ w_in
    b_gate, c_gate, h, z = jnp.split(u, 4, axis=-1)
    c = c_gate * h
    cp = jnp.concatenate([prev.astype(c.dtype), c], axis=1)
    conv = w_conv[0] * cp[:, 0:T]
    for j in range(1, CONV_W):
        conv = conv + w_conv[j] * cp[:, j:j + T]
    y = jax.nn.silu(z) * (b_gate * conv)
    return x + y @ w_out, cp[:, T:]

def shared_kv(h, pos, g_kv, w_kv, g_k):
    B, T, _ = h.shape
    kv = (rms_norm(h, g_kv) @ w_kv).reshape(B, T, N_BRANCH, 2, N_KV, HEAD_DIM)
    k = rope(rms_norm(kv[:, :, :, 0], g_k[:, None, :]), pos)
    kv = jnp.stack([k, kv[:, :, :, 1]], axis=3)
    rows = kv[:, :, :2].reshape(B, T, 4, N_KV, HEAD_DIM)
    return rows, kv[:, :, 2]

def compress(rows, w_cmp):
    B, T = rows.shape[:2]
    nb = -(-T // BLK)
    rows = jnp.pad(rows, ((0, 0), (0, nb * BLK - T), (0, 0), (0, 0), (0, 0)))
    blocks = rows.reshape(B, nb, BLK, 2, N_KV, HEAD_DIM)
    kvc = jnp.einsum('bnlcgd,lcg->bncgd', blocks, w_cmp.astype(rows.dtype))
    blk_end = jnp.arange(nb, dtype=jnp.int32) * BLK + (BLK - 1)
    return kvc, blk_end

def nsa_branches(q, qpos, kvc, blk_end, gather_sel, kvw, kwpos):
    scale = HEAD_DIM ** -0.5
    s = jnp.einsum('bqgrd,bngd->bqgrn', q, kvc[:, :, 0]) * scale
    cmask = (blk_end[None, :] <= qpos[:, None])[None, :, None, None, :]
    p = masked_softmax(s, cmask)
    o_cmp = jnp.einsum('bqgrn,bngd->bqgrd', p.astype(q.dtype), kvc[:, :, 1])
    nb = kvc.shape[1]
    cur = (qpos // BLK)[None, :, None, None]
    j = jnp.arange(nb, dtype=jnp.int32)
    forced = ((j == 0) | (j == cur) | (j == cur - 1)).astype(jnp.float32)
    score = jnp.where(j <= cur, p.sum(axis=3) + FORCE * forced, NEG)
    _, idx = lax.top_k(score, min(N_SEL, nb))
    valid = idx <= cur
    ksv = gather_sel(idx)
    kpos = idx[..., None] * BLK + jnp.arange(BLK, dtype=jnp.int32)
    smask = valid[..., None] & (kpos <= qpos[None, :, None, None, None])
    s = jnp.einsum('bqgrd,bqgkld->bqgrkl', q, ksv[..., 0, :]) * scale
    Bq, Q, G, R = s.shape[:4]
    p = masked_softmax(s.reshape(Bq, Q, G, R, -1), smask.reshape(Bq, Q, G, 1, -1)).reshape(s.shape)
    o_sel = jnp.einsum('bqgrkl,bqgkld->bqgrd', p.astype(q.dtype), ksv[..., 1, :])
    s = jnp.einsum('bqgrd,bngd->bqgrn', q, kvw[:, :, 0]) * scale
    dpos = qpos[:, None] - kwpos[None, :]
    wmask = ((dpos >= 0) & (dpos < WINDOW) & (kwpos[None, :] >= 0))[None, :, None, None, :]
    p = masked_softmax(s, wmask)
    o_win = jnp.einsum('bqgrn,bngd->bqgrd', p.astype(q.dtype), kvw[:, :, 1])
    return jnp.stack([o_cmp, o_sel, o_win], axis=2)

def nsa_query(x, pos, g, w_qz, g_q):
    B, T, _ = x.shape
    HD = N_HEADS * HEAD_DIM
    u = rms_norm(x, g) @ w_qz
    q = rope(rms_norm(u[..., :HD].reshape(B, T, N_KV, GRP, HEAD_DIM), g_q), pos)
    z = jax.nn.silu(u[..., HD:4 * HD]).reshape(B, T, N_BRANCH, N_HEADS, HEAD_DIM)
    gate = jax.nn.sigmoid(u[..., 4 * HD:]).reshape(B, T, N_BRANCH, N_HEADS, 1)
    return q, z * gate

def nsa_out(x, o3, zg, w_out):
    B, T = x.shape[:2]
    o = (o3.reshape(B, T, N_BRANCH, N_HEADS, HEAD_DIM) * zg).sum(axis=2)
    return x + o.reshape(B, T, N_HEADS * HEAD_DIM) @ w_out

def prompt_forward(x, g_a, w_in_a, conv_w, w_out_a, g_kv, w_kv, g_k, w_cmp, g_b, w_qz, g_q, w_out_b):
    B, S, _ = x.shape
    pos = jnp.arange(S, dtype=jnp.int32)
    conv_states = []
    for layer in range(DEPTH):
        if layer < N_A:
            prev = jnp.zeros((B, CONV_W - 1, CONV_CH), x.dtype)
            x, st = short_conv_layer(x, prev, g_a[layer], w_in_a[layer], conv_w[layer], w_out_a[layer])
            conv_states.append(st)
            continue
        if layer == N_A:
            rows, win = shared_kv(x, pos, g_kv, w_kv, g_k)
            kvc, blk_end = compress(rows[:, :, 0:2], w_cmp)
            nb = kvc.shape[1]
            sel_blocks = rows[:, :, 2:4].reshape(B, nb, BLK, 2, N_KV, HEAD_DIM)
            win_pad = jnp.pad(win, ((0, 0), (WINDOW, 0), (0, 0), (0, 0), (0, 0)))
            n_qb = S // Q_BLK
            b_ids = jnp.repeat(jnp.arange(B, dtype=jnp.int32), n_qb)
            i_ids = jnp.tile(jnp.arange(n_qb, dtype=jnp.int32), B)
            gidx = jnp.arange(N_KV, dtype=jnp.int32)[None, None, :, None]

            def item(args):
                qi, b, i = args
                qpos = i * Q_BLK + jnp.arange(Q_BLK, dtype=jnp.int32)
                sel_b = sel_blocks[b]
                gather = lambda idx: sel_b[idx, :, :, gidx]
                kvw = lax.dynamic_slice_in_dim(win_pad[b], i * Q_BLK, WINDOW + Q_BLK, axis=0)[None]
                kwpos = i * Q_BLK - WINDOW + jnp.arange(WINDOW + Q_BLK, dtype=jnp.int32)
                return nsa_branches(qi[None], qpos, kvc[b][None], blk_end, gather, kvw, kwpos)[0]
        lb = layer - N_A
        q, zg = nsa_query(x, pos, g_b[lb], w_qz[lb], g_q[lb])
        q_items = q.reshape(B * n_qb, Q_BLK, N_KV, GRP, HEAD_DIM)
        o3 = lax.map(item, (q_items, b_ids, i_ids)).reshape(B, S, N_BRANCH, N_KV, GRP, HEAD_DIM)
        x = nsa_out(x, o3, zg, w_out_b[lb])
    win_state = win[:, S - min(WINDOW, S):]
    return x, jnp.stack(conv_states), rows, win_state

def sample_forward(x, state_conv, cache_kv, state_win, page_table, g_a, w_in_a, conv_w, w_out_a,
                   g_kv, w_kv, g_k, w_cmp, g_b, w_qz, g_q, w_out_b):
    Bd, T, _ = x.shape
    page = cache_kv.shape[1]
    past = page_table.shape[1] * page
    pos = past + jnp.arange(T, dtype=jnp.int32)
    conv_states = []
    for layer in range(DEPTH):
        if layer < N_A:
            x, st = short_conv_layer(x, state_conv[layer], g_a[layer], w_in_a[layer], conv_w[layer], w_out_a[layer])
            conv_states.append(st)
            continue
        if layer == N_A:
            rows, win = shared_kv(x, pos, g_kv, w_kv, g_k)
            past_cmp = cache_kv[page_table, :, 0:2].reshape(Bd, past, 2, N_KV, HEAD_DIM)
            kvc, blk_end = compress(jnp.concatenate([past_cmp.astype(rows.dtype), rows[:, :, 0:2]], axis=1), w_cmp)
            nb_past = past // BLK
            nb_new = kvc.shape[1] - nb_past
            bpp = page // BLK
            pool_blocks = cache_kv.reshape(cache_kv.shape[0], bpp, BLK, 4, N_KV, HEAD_DIM)
            new_sel = jnp.pad(rows[:, :, 2:4], ((0, 0), (0, nb_new * BLK - T), (0, 0), (0, 0), (0, 0)))
            new_sel = new_sel.reshape(Bd, nb_new, BLK, 2, N_KV, HEAD_DIM)
            bidx = jnp.arange(Bd, dtype=jnp.int32)[:, None, None, None]
            gidx = jnp.arange(N_KV, dtype=jnp.int32)[None, None, :, None]

            def gather(idx):
                jp = jnp.minimum(idx, nb_past - 1)
                phys = page_table[bidx, jp // bpp]
                old = pool_blocks[phys, jp % bpp, :, 2:4, gidx].astype(new_sel.dtype)
                new = new_sel[bidx, jnp.clip(idx - nb_past, 0, nb_new - 1), :, :, gidx]
                return jnp.where((idx >= nb_past)[..., None, None, None], new, old)
            kvw = jnp.concatenate([state_win.astype(win.dtype), win], axis=1)
            kwpos = past - state_win.shape[1] + jnp.arange(kvw.shape[1], dtype=jnp.int32)
        lb = layer - N_A
        q, zg = nsa_query(x, pos, g_b[lb], w_qz[lb], g_q[lb])
        o3 = nsa_branches(q, pos, kvc, blk_end, gather, kvw, kwpos)
        x = nsa_out(x, o3, zg, w_out_b[lb])
    win_state = kvw[:, kvw.shape[1] - min(WINDOW, kvw.shape[1]):]
    return x, jnp.stack(conv_states), rows, win_state

def setup_inputs(seed: int = 0) -> dict:
    key = jax.random.key(seed)
    ks = jax.random.split(key, 18)
    n_pages = PAST_LEN // PAGE_SIZE
    n_used = DEC_BATCH * n_pages
    n_pool = n_used + max(1, n_used // 4)
    win_buf = min(WINDOW, PAST_LEN)
    HD = N_HEADS * HEAD_DIM

    def nrm(k, shape, scale=1.0):
        return jax.random.normal(k, shape, jnp.float32) * scale

    return {
        'x_prompt': nrm(ks[0], (BATCH, SEQ, D_MODEL)),
        'x_sample': nrm(ks[1], (DEC_BATCH, DEC_SEQ, D_MODEL)),
        'state_conv': nrm(ks[2], (N_A, DEC_BATCH, CONV_W - 1, CONV_CH)),
        'cache_kv': nrm(ks[3], (n_pool, PAGE_SIZE, 4, N_KV, HEAD_DIM)),
        'state_win': nrm(ks[4], (DEC_BATCH, win_buf, 2, N_KV, HEAD_DIM)),
        'page_table': jax.random.permutation(ks[5], n_pool)[:n_used].reshape(DEC_BATCH, n_pages).astype(jnp.int32),
        'g_a': 1.0 + nrm(ks[6], (N_A, D_MODEL), 0.02),
        'w_in_a': nrm(ks[7], (N_A, D_MODEL, 4 * CONV_CH), D_MODEL ** -0.5),
        'conv_w': nrm(ks[8], (N_A, CONV_W, CONV_CH), CONV_W ** -0.5),
        'w_out_a': nrm(ks[9], (N_A, CONV_CH, D_MODEL), CONV_CH ** -0.5),
        'g_kv': 1.0 + nrm(ks[10], (D_MODEL,), 0.02),
        'w_kv': nrm(ks[11], (D_MODEL, N_BRANCH * 2 * N_KV * HEAD_DIM), D_MODEL ** -0.5),
        'g_k': 1.0 + nrm(ks[12], (N_BRANCH, HEAD_DIM), 0.02),
        'w_cmp': (1.0 + nrm(ks[13], (BLK, 2, N_KV), 0.1)) / BLK,
        'g_b': 1.0 + nrm(ks[14], (N_B, D_MODEL), 0.02),
        'w_qz': nrm(ks[15], (N_B, D_MODEL, 4 * HD + N_BRANCH * N_HEADS), D_MODEL ** -0.5),
        'g_q': 1.0 + nrm(ks[16], (N_B, HEAD_DIM), 0.02),
        'w_out_b': nrm(ks[17], (N_B, HD, D_MODEL), HD ** -0.5),
    }

def reference(x_prompt, x_sample, state_conv, cache_kv, state_win, page_table, g_a, w_in_a, conv_w,
              w_out_a, g_kv, w_kv, g_k, w_cmp, g_b, w_qz, g_q, w_out_b):
    y_prompt, conv_p, rows_p, win_p = prompt_forward(
        x_prompt, g_a, w_in_a, conv_w, w_out_a, g_kv, w_kv, g_k, w_cmp, g_b, w_qz, g_q, w_out_b)
    y_sample, conv_s, rows_s, win_s = sample_forward(
        x_sample, state_conv, cache_kv, state_win, page_table, g_a, w_in_a, conv_w, w_out_a,
        g_kv, w_kv, g_k, w_cmp, g_b, w_qz, g_q, w_out_b)
    return (y_prompt, y_sample, conv_p, conv_s, rows_p, rows_s, win_p, win_s)


_drawn_inputs = setup_inputs


def setup_inputs(seed=0):
    import zlib

    import numpy as np

    out = dict(_drawn_inputs(seed))
    spreads = {}
    factors = {'cache_kv': 3.613, 'g_kv': 2.858, 'g_k': 4.137, 'w_cmp': 8.0, 'g_b': 8.0, 'g_q': 8.0}
    for name, (base, spread) in spreads.items():
        noise = np.random.default_rng([zlib.crc32(name.encode()), seed]).standard_normal(out[name].shape)
        drawn = base * np.exp(spread * noise) if base else spread * noise
        out[name] = __import__('jax').numpy.asarray(drawn.astype(out[name].dtype))
    for name, factor in factors.items():
        out[name] = (out[name] * factor).astype(out[name].dtype)
    return out
```

```python
from contextlib import ExitStack

import numpy as np

import concourse.bass as bass
import concourse.mybir as mybir

F32 = mybir.dt.float32
BF16 = mybir.dt.bfloat16
I32 = mybir.dt.int32
ACT = mybir.ActivationFunctionType
ALU = mybir.AluOpType
AX = mybir.AxisListType

P = 128
D = 2048
KT = D // P
NP = 256
B, T = 8, 8
NS = B * T
NT = NP + NS
H, G = 16, 4
R = H // G
HD = 128
PAST, PAGE, BLK, WIN = 2048, 128, 64, 512
N_SEL = 16
NPG = PAST // PAGE
NBK = PAST // BLK
PBK = NP // BLK
MID = NBK - 2
KEEP = N_SEL - 3
EPS = 1e-6
NEG = -1e30
SCALE = HD ** -0.5
UNIT = 256
GATES = 3 * H

WS = 8
WSZ = KT // 2 * UNIT
ZS = 4
ZSZ = KT // 4 * UNIT
CS = 8
VS = 10
VSZ = 2 * G * HD

TOK = ((0, P), (P, P), (NP, NS))


class Chain:

    def __init__(self, eng, sem):
        self.eng, self.sem, self.base, self.n = eng, sem, 0, 0

    def __call__(self, ins):
        self.n += 1
        ins.then_inc(self.sem, 1)
        self.eng.wait_ge(self.sem, self.base + self.n)

    def enter(self, i, per):
        self.start, self.per = self.base + self.n, per
        self.base, self.n = i * per + self.start, 0

    def leave(self, trips):
        assert self.n == self.per, (self.n, self.per)
        self.base, self.n = self.start + trips * self.per, 0


T_USES = ([("keys", c, g) for c in range(2) for g in range(G)] + [("probs_win", 0, 0)]
          + [("keys", c, g) for c in range(2, 5) for g in range(G)]
          + [("probs_sel", c, 0) for c in range(4)] + [("probs_new", 0, 0)]
          + [("prompt", c, 0) for c in range(3)] + [("prompt_cmp", 0, 0)])
NTU = len(T_USES)
assert NTU % 2 == 0
CHUNKS = 1 + PAST // 512
NSU = CHUNKS + 4
NMU = 12
KEY_USE = (0, 2, 6, 8, 10)
VWIN_USE, VSEL_USE, V_USES = 4, 12, 20


def build(nc, ins, consts, outs, scratch):
    (x_prompt, x_sample, state_conv, cache_kv, state_win, page_table, g_a, w_in_a, conv_w, w_out_a,
     g_kv, w_kv, g_k, w_cmp, g_b, w_qz, g_q, w_out_b) = ins
    y_p, y_s, conv_p, conv_s, rows_p, rows_s, win_p, win_s = outs
    gates_dram, x1_dram = scratch

    with ExitStack() as ctx:
        def sem(name):
            return ctx.enter_context(nc.semaphore(name))

        ps = ctx.enter_context(nc.psum_tensor("ps", [P, 8, 512], F32))

        def sb(name, *shape, dt=F32):
            return ctx.enter_context(nc.sbuf_tensor(name, [P, *shape], dt))

        ident, ones, group, causal = (sb(n, P) for n in ("ident", "ones", "group", "causal"))
        cosT, sinT = sb("cosT", NT), sb("sinT", NT)
        newmask = sb("newmask", B, NS)
        winmask = sb("winmask", T)
        tri = sb("tri", MID, MID, dt=BF16)
        pcmask, pckeep = sb("pcmask", 2, PBK), sb("pckeep", 2, PBK)
        vecT = sb("vecT", 100)
        w2 = sb("w2", 2, G, 2)
        ptab = sb("ptab", B * NPG, dt=I32)
        pcvT = sb("pcvT", G, PBK)
        kcT, vcT = sb("kcT", B, G, NBK), sb("vcT", B, G, NBK)
        wring = sb("wring", WS * WSZ)
        hn = sb("hn", KT, NT)
        BIG = 30720
        big = sb("big", BIG)

        class Region:
            def __init__(self, lo, hi):
                self.at, self.hi = lo, hi

            def take(self, *shape):
                n = int(np.prod(shape))
                v = big[:, self.at:self.at + n]
                self.at += n
                assert self.at <= self.hi, ("region", self.at, self.hi)
                if len(shape) > 1:
                    names = "abcd"[:len(shape)]
                    v = v.rearrange(f"p ({' '.join(names)}) -> p {' '.join(names)}", **dict(zip(names, shape)))
                return v

        slot = [wring[:, s * WSZ:(s + 1) * WSZ].rearrange("p (k c) -> p k c", c=UNIT) for s in range(WS)]
        zslot = [wring[:, s * ZSZ:(s + 1) * ZSZ].rearrange("p (k c) -> p k c", c=UNIT) for s in range(ZS)]
        Sp = wring[:, ZS * ZSZ:ZS * ZSZ + 2048].rearrange("p (q a k) -> p q a k", q=2, a=4)
        VLO = WS * WSZ - VS * VSZ
        assert ZS * ZSZ + 2048 <= VLO
        vslot = [wring[:, VLO + s * VSZ:VLO + (s + 1) * VSZ].rearrange("p (k c) -> p k c", k=2) for s in range(VS)]

        XLO = BIG - KT * NT
        xT = big[:, XLO:BIG].rearrange("p (k t) -> p k t", k=KT)
        rstd = big[:, XLO - NT:XLO]
        keep = Region(0, BIG)
        qS = keep.take(B, H * T)
        qP = keep.take(H, NP)
        kTs = keep.take(2, G, NT)
        vts = keep.take(2, 3, G * HD)
        pcK = keep.take(G, PBK)
        pcV = keep.take(G, HD)
        tmp = Region(keep.at, XLO - NT)
        kro = tmp.take(G, NT)
        vto, kto = tmp.take(3, 3, G * HD), tmp.take(3, 3, G * HD)
        raw, sq, rs, kn, ra = (tmp.take(2, NT) for _ in range(5))
        wgt = kto.rearrange("p a b c -> p (a b c)")[:, 0:KT * GATES].rearrange("p (k c) -> p k c", c=GATES)
        gd = rs[:, 0, :]
        early = Region(0, XLO - NT)
        yT = early.take(KT, NT)
        pgs = early.take(CS, 2 * G * HD)
        pg = [pgs[:, s, :] for s in range(CS)]
        xin = big[:, KT * NT:KT * NT + 3 * D].rearrange("p (t d) -> p t d", t=3)
        cpad = early.take(2, NP + 2)
        spad = early.take(2, B, T + 2)
        csb, ez, bc = (early.take(2, NT) for _ in range(3))
        stT = early.take(KT, 2 * B)
        cso = early.take(KT, 2 + 2 * B)
        ssum = early.take(NT)
        xsq = early.take(KT, NT)
        xsqf = xsq.rearrange("p k t -> p (k t)")
        vecs, stin, crow = xsqf[:, 0:P], xsqf[:, P:P + D], xsqf[:, P:P + D]
        trif = xsqf[:, P + D:P + D + MID * MID].rearrange("p (j i) -> p j i", i=MID)
        main = Region(keep.at, BIG)
        zS = main.take(3, H, NS)
        oS = main.take(3, B, H * T)
        LATE = main.at
        KTb = main.take(G, 512)
        Pp = KTb.rearrange("p g k -> p (g k)")[:, 0:4 * 384].rearrange("p (a q) -> p a q", a=4)
        S = main.take(WIN + NS + PAST + NS)
        PT = [main.take(4, P) for _ in range(2)]
        gt, eq = (PT[n].rearrange("p a b -> p (a b)")[:, 0:MID * MID // 2].bitcast(BF16)
                  .rearrange("p (j i) -> p j i", i=MID) for n in range(2))
        PTn = main.take(2, P)
        gbc = [main.take(2, NT) for _ in range(2)]
        ezm = main.take(2, NT)
        zgP = main.take(3, 2, NP)
        vst = main.take(2, 2, HD)
        pvst = main.take(HD)
        qst = main.take(2, NP)
        qSb = main.take(H * T)
        vcst, kcst = main.take(G, NBK), main.take(G, NBK)
        vcb = main.take(G * HD)
        msb = main.take(192)
        pcm, psc, bmask = main.take(NBK), main.take(NBK), main.take(NBK)
        pcT = main.take(H * T)
        pcTp = main.take(2, NP)
        pcs = main.take(4, PBK)
        stat = main.take(64)
        otmp = main.take(2, NP)
        late = Region(LATE, XLO)
        oTs = late.take(H, NS)
        oadd = late.take(H, NS)
        xst = [late.take(2, NT) for _ in range(2)]
        ysb = [late.take(3, UNIT) for _ in range(2)]

        WN, SL, SN = WIN, WIN + NS, WIN + NS + PAST

        x_in, misc_in, consts_in = sem("x_in"), sem("misc_in"), sem("consts_in")
        w2_zero, w2_done, consts_used = sem("w2_zero"), sem("w2_done"), sem("consts_used")
        tp_full, tpd_free, tpa_free = sem("tp_full"), sem("tpd_free"), sem("tpa_free")
        vec_full, vec_out = sem("vec_full"), sem("vec_out")
        sq_out, sum_out, sum_full, var_out, sd_out, hn_out = (sem(n) for n in (
            "sq_out", "sum_out", "sum_full", "var_out", "sd_out", "hn_out"))
        w_full, w_used = [sem(f"w_full{s}") for s in range(WS)], sem("w_used")
        w_asked = sem("w_asked")
        z_full, z_used = [sem(f"z_full{s}") for s in range(ZS)], sem("z_used")
        v_full, v_used = [sem(f"v_full{s}") for s in range(VS)], sem("v_used")
        pg_full, pg_used = [sem(f"pg_full{s}") for s in range(CS)], sem("pg_used")
        c_out, h_used, e_out, zc_used, b_used, y_out = (sem(n) for n in (
            "c_out", "h_used", "e_out", "zc_used", "b_used", "y_out"))
        kc_out, vc_out = sem("kc_out"), sem("vc_out")
        cs_full, cs_out = sem("cs_full"), sem("cs_out")
        x1_out = sem("x1_out")
        dchain, achain = sem("dchain"), sem("achain")
        cs_store, x1_store, kv_store, wcopy = (sem(n) for n in ("cs_store", "x1_store", "kv_store", "wcopy"))
        sqr_out, hs_full, hv_out, hsd_out, rope_out, kcp_out = (sem(n) for n in (
            "sqr_out", "hs_full", "hv_out", "hsd_out", "rope_out", "kcp_out"))
        kt_full, kt_out, vt_out = sem("kt_full"), sem("kt_out"), sem("vt_out")
        pc_full, pc_out, pv_full, pv_out, vts_out = (sem(n) for n in ("pc_full", "pc_out", "pv_full", "pv_out", "vts_out"))
        wg_in, g_full, ge_out, gd_out, gates_out = (sem(n) for n in ("wg_in", "g_full", "ge_out", "gd_out", "gates_out"))
        gb_full, gb_used = [sem("gb_full0"), sem("gb_full1")], sem("gb_used")
        st_sample, st_prompt = sem("st_sample"), sem("st_prompt")
        t_full, td_free, ta_free = sem("t_full"), sem("td_free"), sem("ta_free")
        s_full, s_free, m_full, m_free = sem("s_full"), sem("s_free"), sem("m_full"), sem("m_free")
        ze_out, zu_free = sem("ze_out"), sem("zu_free")
        cexp_in, cexp_out, wexp_in, wexp_out, sexp_in, sexp_out, pexp_in, pexp_out = (sem(n) for n in (
            "cexp_in", "cexp_out", "wexp_in", "wexp_out", "sexp_in", "sexp_out", "pexp_in", "pexp_out"))
        p_ready, w_ready, sel_ready, pp_ready = sem("p_ready"), sem("w_ready"), sem("sel_ready"), sem("pp_ready")
        x1_back = sem("x1_back")
        ots_out, xst_out, y_full, y_free = sem("ots_out"), sem("xst_out"), sem("y_full"), sem("y_free")
        y_stored = [sem("y_stored0"), sem("y_stored1")]

        U_MIX, U_KV, U_QUERY, U_OUT = 64, 80, 104, 120
        HDALL = H * HD

        def wload(sp, w, half, col, use, s):
            col = sp.snap(col)
            sp.wait_ge(w_used, use + 1)
            sp.sem_inc(w_asked, 1)
            sp.dma_start(slot[s], w[half * D // 2:(half + 1) * D // 2, bass.ds(col, UNIT)]
                         .rearrange("(k p) c -> p k c", p=P)).then_inc(w_full[s], 16)

        def empty_t(eng, copy, n, i):
            kind, c, g = T_USES[n]
            bank, free = 4 + n % 2, (td_free, ta_free)[n % 2]
            if kind == "keys":
                eng.wait_ge(*((s_full, i * NSU + c) if c else (m_full, i * NMU + 1)))
            eng.wait_ge(t_full, i * NTU + n + 1)
            four = ps[:, bank, :].rearrange("p (a q) -> p a q", a=4)
            if kind == "keys":
                ins = copy(KTb[:, g, :], ps[:, bank, :])
            elif kind in ("probs_win", "probs_sel"):
                ins = copy(PT[c % 2], four)
            elif kind == "probs_new":
                ins = copy(PTn[0:NS, 0, :], ps[0:NS, bank, 0:P])
            elif kind == "prompt":
                ins = copy(Pp[:, :, c * P:(c + 1) * P], four)
            else:
                ins = copy(pcTp[0:PBK], ps[0:PBK, bank, :].rearrange("p (t q) -> p t q", t=2))
            ins.then_inc(free, 1)

        block = ctx.enter_context(nc.Block())

        @block.sync
        def _(sp):
            for tt, (t0, n) in enumerate(TOK[:2]):
                sp.dma_start(xin[:, tt, :], x_prompt[0, t0:t0 + n, :]).then_inc(x_in, 16)
            sp.dma_start(xin[0:NS, 2, :], x_sample.rearrange("b t d -> (b t) d")).then_inc(x_in, 16)
            sp.dma_start(ident[:], consts["ident"]).then_inc(x_in, 16)
            sp.dma_start(vecs[0:16, :], g_a.rearrange("l (k p) -> (l k) p", p=P)).then_inc(misc_in, 16)
            sp.dma_start(vecs[16:32, :], g_kv.rearrange("(k p) -> k p", p=P)).then_inc(misc_in, 16)
            sp.dma_start(vecs[32:48, :], g_b.rearrange("l (k p) -> (l k) p", p=P)).then_inc(misc_in, 16)
            sp.dma_start(vecs[48:96, :], conv_w.rearrange("l w (k p) -> (l w k) p", p=P)).then_inc(misc_in, 16)
            sp.dma_start(vecs[96:99, :], g_k).then_inc(misc_in, 16)
            sp.dma_start(vecs[99:100, :], g_q).then_inc(misc_in, 16)
            sp.dma_start(stin[0:2 * B, :], state_conv.rearrange("l b w d -> (l b w) d")).then_inc(misc_in, 16)
            for t, name in ((ones, "ones"), (group, "group"), (causal, "causal"), (cosT, "cosT"), (sinT, "sinT"),
                            (newmask, "newmask"), (winmask, "winmask"), (trif, "tri"), (pcmask, "pcmask"), (pckeep, "pckeep")):
                sp.dma_start(t[:] if t is not trif else t, consts[name]).then_inc(consts_in, 16)
            sp.dma_start(ptab[0:1, :], page_table.rearrange("(o b) n -> o (b n)", o=1)).then_inc(consts_in, 16)
            for lo in (0, BLK):
                sp.dma_start(csb[lo:lo + BLK, 0, 0:2 * G], w_cmp.rearrange("l c g -> l (c g)")).then_inc(consts_in, 16)
            sp.wait_ge(consts_in, 16 * 13)

            def conv_step(i, first):
                for n in range(8):
                    quarter, half = (1, 2, 3, 0)[n // 2], n % 2
                    wload(sp, w_in_a[0], half, i * UNIT + quarter * D, i * 8 + n, n)
                    if first and n == 0:
                        sp.wait_ge(tp_full, KT)
                    for j in (2 * n, 2 * n + 1):
                        page = sp.value_load(ptab[0:1, bass.ds(i * NPG + j, 1)], min_val=0, max_val=cache_kv.shape[0] - 1)
                        sp.wait_ge(pg_used, i * NPG + j + 1)
                        sp.dma_start(pg[j % CS], cache_kv[bass.ds(page, 1), :, 0:2].rearrange(
                            "o l c g d -> (o l) (c g d)")).then_inc(pg_full[j % CS], 16)

            conv_step(0, True)
            with sp.Fori(1, B) as i:
                conv_step(i, False)
            with sp.Fori(0, 2) as i:
                for n in range(8):
                    wload(sp, w_out_a[0], n % 2, i * (4 * UNIT) + n // 2 * UNIT, i * 8 + U_MIX + n, n)

            def window_copy(b):
                sp.dma_start(win_s[bass.ds(b, 1), 0:WIN - T].rearrange("o l c g d -> o (l c g d)"),
                             state_win[bass.ds(b, 1), T:WIN].rearrange("o l c g d -> o (l c g d)")).then_inc(wcopy, 16)

            with sp.Fori(0, 3) as i:
                for n in range(8):
                    wload(sp, w_kv, n % 2, i * (8 * HD) + n // 2 * UNIT, i * 8 + U_KV + n, n)
                    if n % 4 == 3:
                        window_copy(i * 2 + n // 4)
            with sp.Fori(0, 2) as i:
                for n in range(8):
                    wload(sp, w_qz[0], n % 2, i * (4 * UNIT) + n // 2 * UNIT, i * 8 + U_QUERY + n, n)
                window_copy(i + 6)

            def zload(i, use, first):
                u, kq, s = use // 4, use % 4, use % ZS
                if first:
                    sp.wait_ge(w_used, WS + U_OUT - WS + s * ZSZ // WSZ + 1)
                col = sp.snap(i * UNIT + (1 + u) * HDALL)
                sp.wait_ge(z_used, i * 12 + use + 1)
                sp.dma_start(zslot[s], w_qz[0, kq * D // 4:(kq + 1) * D // 4, bass.ds(col, UNIT)]
                             .rearrange("(k p) c -> p k c", p=P)).then_inc(z_full[s], 16)

            def vload(i, use, first, window, chunk, part, which):
                s = use % VS
                if first:
                    sp.wait_ge(w_used, WS + U_OUT - WS + (VLO + s * VSZ) // WSZ + 1)
                srcs = []
                for k in range(2):
                    j = 4 * chunk + 2 * part + k
                    if window:
                        src = state_win[bass.ds(i, 1), j * P:(j + 1) * P, which].rearrange("o l g d -> (o l) (g d)")
                    else:
                        page = sp.value_load(ptab[0:1, bass.ds(i * NPG + j, 1)], min_val=0, max_val=cache_kv.shape[0] - 1)
                        src = cache_kv[bass.ds(page, 1), :, 2 + which].rearrange("o l g d -> (o l) (g d)")
                    srcs.append(src)
                sp.wait_ge(v_used, i * V_USES + use + 1)
                for k in range(2):
                    sp.dma_start(vslot[s][:, k, :], srcs[k]).then_inc(v_full[s], 16)

            def gload(i, u):
                row = sp.snap(i * 2 + u * H)
                sp.wait_ge(gb_used, i * 3 + (1 if u == 2 else 0))
                sp.dma_start(gbc[u % 2], gates_dram[bass.ds(row, 2), :].rearrange("(o h) t -> o h t", o=1)
                             .to_broadcast([P, 2, NT])).then_inc(gb_full[u % 2], 16)

            def main_step(i, first):
                for c in range(CHUNKS):
                    for part in range(2):
                        vload(i, KEY_USE[c] + part, first, c == 0, max(c - 1, 0), part, 0)
                        zload(i, 2 * c + part, first and c < 2)
                    if c == 1:
                        for part in range(2):
                            vload(i, VWIN_USE + part, first, True, 0, part, 1)
                    if c == 2:
                        if first:
                            sp.wait_ge(gates_out, 16)
                        gload(i, 0)
                    if c == 3:
                        gload(i, 1)
                for part in range(2):
                    zload(i, 10 + part, False)
                for n in range(8):
                    vload(i, VSEL_USE + n, False, False, n // 2, n % 2, 1)
                gload(i, 2)

            main_step(0, True)
            with sp.Fori(1, B) as i:
                main_step(i, False)

            def out_load(i, n, first):
                if first and n == 0:
                    sp.wait_ge(z_used, ZS + B * 12)
                if first and n == 2:
                    sp.wait_ge(m_full, B * NMU + 1)
                    sp.wait_ge(ots_out, 1)
                    sp.dma_start(xT, x1_dram.rearrange("p (k t) -> p k t", k=KT)).then_inc(x1_back, 16)
                wload(sp, w_out_b[0], n % 2, i * (4 * UNIT) + n // 2 * UNIT, i * 8 + U_OUT + n, n)

            for i in range(2):
                for n in range(8):
                    out_load(i, n, i == 0)
            sp.wait_ge(wcopy, 16 * B)
            sp.wait_ge(cs_store, 32)
            sp.wait_ge(x1_store, 16)
            sp.wait_ge(kv_store, 16 * 12)
            for q in y_stored:
                sp.wait_ge(q, 32 * 4)

        @block.gpsimd
        def _(pool):
            pool.sem_inc(w_used, WS)
            pool.sem_inc(pg_used, CS)
            pool.sem_inc(x1_out, 2)
            pool.sem_inc(sqr_out, 2)
            pool.sem_inc(kt_out, 3)
            pool.sem_inc(z_used, ZS)
            pool.sem_inc(v_used, VS)
            pool.sem_inc(td_free, 1)
            pool.sem_inc(ta_free, 1)
            pool.sem_inc(s_free, 1)
            pool.sem_inc(m_free, 1)
            pool.sem_inc(y_free, 2)
            for count in (zc_used, b_used, kc_out, vc_out, vt_out, zu_free, m_full, kcp_out, kt_full, h_used, y_out, rope_out):
                pool.sem_inc(count, 1)
            nc.gpsimd.memset(w2[:], 0.0).then_inc(w2_zero, 1)

            with pool.Fori(0, 3) as i:
                pool.wait_ge(rope_out, i * 2 + 2 + 1)
                nc.gpsimd.tensor_copy(kTs[:, bass.ds(i // 2, 1)].rearrange("p o g t -> p (o g) t"), kro).then_inc(kcp_out, 1)
            pool.wait_ge(vt_out, 10)
            nc.gpsimd.tensor_copy(vts[:, :, 0:2, :], vto[:, 1:3, 0:2, :]).then_inc(vts_out, 1)
            nc.gpsimd.tensor_copy(vts[0:NS, :, 2, :], vto[0:NS, 1:3, 2, :]).then_inc(vts_out, 1)
            pool.wait_ge(rope_out, 15)
            pool.wait_ge(vts_out, 2)
            pool.wait_ge(pv_out, 1)
            pool.wait_ge(gd_out, 1)
            pool.wait_ge(gates_out, 16)
            pool.wait_ge(x1_store, 16)
            with pool.Fori(0, B) as i:
                pool.wait_ge(m_full, i * NMU + 1)
                nc.gpsimd.tensor_copy(qSb, qS[:, bass.ds(i, 1), :].rearrange("p o c -> p (o c)")).then_inc(st_sample, 1)
                nc.gpsimd.tensor_copy(vcst, vcT[:, bass.ds(i, 1)].rearrange("p o g n -> p (o g) n")).then_inc(st_sample, 1)
                nc.gpsimd.tensor_copy(kcst, kcT[:, bass.ds(i, 1)].rearrange("p o g n -> p (o g) n")).then_inc(st_sample, 1)
                nc.gpsimd.tensor_copy(qst, qP[:, bass.ds(i * 2, 2), :]).then_inc(st_prompt, 1)
                for br in range(2):
                    nc.gpsimd.tensor_copy(vst[:, br], vts[:, br, 0:2, bass.ds(i // 2 * HD, HD)]).then_inc(st_prompt, 1)
                nc.gpsimd.tensor_copy(pvst[0:PBK, :], pcV[0:PBK, bass.ds(i // 2, 1), :].rearrange("p o d -> p (o d)")).then_inc(st_prompt, 1)
            pool.wait_ge(x1_back, 16)
            for n in range(8):
                pool.wait_ge(y_free, n + 1)
                nc.gpsimd.tensor_copy(xst[n % 2], xT[:, 2 * n:2 * n + 2, :]).then_inc(xst_out, 1)

        @block.tensor
        def _(pe):
            def mm(out, lhsT, rhs, start=True, stop=True, **kw):
                return nc.tensor.matmul(out, lhsT, rhs, start=start, stop=stop, **kw)

            def tr(out, in_):
                n = in_.shape[0]
                return nc.tensor.transpose(out, in_, ident[0:n, 0:n])

            pe.wait_ge(x_in, 64)
            for kt in range(KT):
                if kt >= 8:
                    pe.wait_ge((tpd_free, tpa_free)[kt % 2], (kt - 8) // 2 + 1)
                for tt, (t0, n) in enumerate(TOK):
                    last = tr(ps[:, kt % 8, t0:t0 + n], xin[0:n, tt, kt * P:(kt + 1) * P])
                last.then_inc(tp_full, 1)
            pe.wait_ge(misc_in, 16 * 7)
            pe.wait_ge(tpd_free, 8)
            pe.wait_ge(tpa_free, 8)
            tr(ps[:, 0, 0:100], vecs[0:100, :]).then_inc(vec_full, 1)
            for kt in range(KT):
                last = tr(ps[:, 1, kt * 2 * B:(kt + 1) * 2 * B], stin[0:2 * B, kt * P:(kt + 1) * P])
            last.then_inc(vec_full, 1)
            pe.wait_ge(consts_in, 16 * 13)
            pe.wait_ge(sum_out, 1)
            mm(ps[:, 2, 0:NT], ones[:], ssum).then_inc(sum_full, 1)
            pe.wait_ge(var_out, 1)
            pe.wait_ge(vec_out, 2)

            def half_unit(s, cnt, bank, half, rhs):
                pe.wait_ge(w_full[s], cnt)
                for t in range(2):
                    for k in range(KT // 2):
                        last = mm(ps[:, bank + t, 0:NT], slot[s][:, k, t * P:(t + 1) * P], rhs[:, half * 8 + k, :],
                                  start=half == 0 and k == 0, stop=half == 1 and k == 7)
                return last

            pe.wait_ge(hn_out, KT)
            pe.wait_ge(w2_done, 2)
            with pe.Fori(0, B) as i:
                for n in range(8):
                    u, half = n // 2, n % 2
                    if half == 0:
                        if u == 0:
                            pe.wait_ge(zc_used, i + 1)
                        if u == 1:
                            pe.wait_ge(b_used, i + 1)
                        if u == 2:
                            pe.wait_ge(c_out, i + 1)
                        if u == 3:
                            pe.wait_ge(h_used, i + 1 + 1)
                    last = half_unit(n, i * 16 + 16, 2 * (u % 2), half, hn)
                    last.then_inc(w_used, 1)
                    for j in (2 * n, 2 * n + 1):
                        if j == 0:
                            pe.wait_ge(kc_out, i + 1)
                            pe.wait_ge(vc_out, i + 1)
                        pe.wait_ge(pg_full[j % CS], i * 32 + 16 * (j // CS + 1))
                        for c in range(2):
                            for g in range(G):
                                last = mm(ps[:, 6 + c, g * NBK + 2 * j:g * NBK + 2 * j + 2],
                                          pg[j % CS][:, (c * G + g) * HD:(c * G + g + 1) * HD], w2[:, c, g, :])
                        last.then_inc(pg_used, 1)

            pe.wait_ge(y_out, B + 1)
            for n in range(4):
                if n >= 2:
                    pe.wait_ge(cs_out, n - 1)
                for k in range(4):
                    last = tr(ps[0:18, 4 + n % 2, k * P:(k + 1) * P], cso[:, 4 * n + k, :])
                last.then_inc(cs_full, 1)

            pe.wait_ge(zc_used, B + 1)
            pe.wait_ge(b_used, B + 1)
            with pe.Fori(0, 2) as i:
                for n in range(8):
                    u, half = n // 2, n % 2
                    if half == 0:
                        pe.wait_ge(x1_out, i * 4 + u + 1)
                    last = half_unit(n, i * 16 + 16 * (U_MIX // WS + 1), 2 * (u % 2), half, yT)
                    last.then_inc(w_used, 1)
            pe.wait_ge(sum_out, 2)
            mm(ps[:, 4, 0:NT], ones[:], ssum).then_inc(sum_full, 1)
            pe.wait_ge(hn_out, 2 * KT)
            pe.wait_ge(x1_out, 2 + 8)

            def head_sums(q):
                pe.wait_ge(sqr_out, 2 + q + 1)
                mm(ps[:, 4, 0:NT], ones[:], sq[:, 0, :])
                mm(ps[:, 5, 0:NT], ones[:], sq[:, 1, :]).then_inc(hs_full, 1)

            with pe.Fori(0, 3) as i:
                for n in range(8):
                    half = n % 2
                    cnt = i * 16 + 16 * (U_KV // WS + 1)
                    if n < 4:
                        if n % 2 == 0:
                            pe.wait_ge(vt_out, i * 3 + 1)
                            pe.wait_ge(kt_out, i * 3 + 3)
                            pe.wait_ge(sqr_out, i * 2 + n // 2 + 1)
                        last = half_unit(n, cnt, 2 * (n // 2), half, hn)
                        last.then_inc(w_used, 1)
                    else:
                        if n == 4:
                            pe.wait_ge(sqr_out, i * 2 + 4)
                        hf = (n - 4) // 2
                        pe.wait_ge(w_full[n], cnt)
                        for tt, (t0, nt) in enumerate(TOK):
                            for k in range(8):
                                last = mm(ps[0:nt, tt, hf * UNIT:(hf + 1) * UNIT], hn[:, half * 8 + k, t0:t0 + nt],
                                          slot[n][:, k, :], start=half == 0 and k == 0, stop=half == 1 and k == 7)
                        last.then_inc(w_used, 1)
                    if n == 3:
                        head_sums(i * 2)
                    if n == 4:
                        head_sums(i * 2 + 1)
                    if n == 6:
                        pe.wait_ge(rope_out, i * 2 + 2 + 1)
                        pe.wait_ge(kt_out, i * 3 + 3)
                        for tt, (t0, nt) in enumerate(TOK):
                            for g in range(G):
                                last = tr(ps[0:nt, (6, 7, 3)[tt], g * HD:(g + 1) * HD], kro[:, g, t0:t0 + nt])
                            last.then_inc(kt_full, 1)
            pe.wait_ge(kt_out, 3 + 9)
            pe.wait_ge(vt_out, 10)
            for c, src in ((0, kto), (1, vto)):
                for tt in range(2):
                    for g in range(G):
                        last = mm(ps[:, 6 + c, g * PBK + 2 * tt:g * PBK + 2 * tt + 2], src[:, 0, tt, g * HD:(g + 1) * HD], w2[:, c, g, :])
            last.then_inc(pc_full, 1)

            pe.wait_ge(hn_out, 3 * KT)
            with pe.Fori(0, 2) as i:
                for n in range(8):
                    u, half = n // 2, n % 2
                    if half == 0:
                        pe.wait_ge(sqr_out, i * 4 + 6 + u + 1)
                    last = half_unit(n, i * 16 + 16 * (U_QUERY // WS + 1), 2 * (u % 2), half, hn)
                    last.then_inc(w_used, 1)
                    if half == 0 and u >= 1:
                        head_sums(i * 4 + 6 + u - 1)
                head_sums(i * 4 + 6 + 3)
            pe.wait_ge(pc_out, 2)
            for g in range(G):
                last = tr(ps[0:PBK, 6, g * HD:(g + 1) * HD], pcvT[:, g, :])
            last.then_inc(pv_full, 1)
            pe.wait_ge(wg_in, 16)
            for kt in range(KT):
                last = mm(ps[0:GATES, 0, 0:NT], wgt[:, kt, :], hn[:, kt, :], start=kt == 0, stop=kt == KT - 1)
            last.then_inc(g_full, 1)
            pe.wait_ge(ge_out, 1)
            pe.wait_ge(pv_out, 1)
            pe.wait_ge(hv_out, 14)

            with pe.Fori(0, B) as i:
                t_at = [0]

                def t_bank(known_free=False):
                    n = t_at[0]
                    t_at[0] += 1
                    if not known_free:
                        pe.wait_ge((td_free, ta_free)[n % 2], i * (NTU // 2) + n // 2 + 1)
                    return 4 + n % 2

                def t_emptied(kind, c, g):
                    n = T_USES.index((kind, c, g))
                    pe.wait_ge((td_free, ta_free)[n % 2], i * (NTU // 2) + n // 2 + 2)

                def m_bank(n):
                    pe.wait_ge(m_free, i * NMU + n)

                def z_part(part):
                    u, kq, t = part // 8, part % 8 // 2, part % 2
                    if part % 8 == 0:
                        pe.wait_ge(zu_free, i * 3 + (1 if u == 2 else 0) + 1)
                    s = (4 * u + kq) % ZS
                    if t == 0:
                        pe.wait_ge(z_full[s], i * 48 + 16 * (u + 1))
                    for k in range(4):
                        last = mm(ps[:, 2 * (u % 2) + t, 0:NT], zslot[s][:, k, t * P:(t + 1) * P], hn[:, kq * 4 + k, :],
                                  start=kq == 0 and k == 0, stop=kq == 3 and k == 3, skip_group_check=True)
                    if t == 1:
                        last.then_inc(z_used, 1)

                def keys(c, g):
                    for h in range(2):
                        use = KEY_USE[c] + h
                        if g == 0:
                            pe.wait_ge(v_full[use % VS], i * 64 + 32 * (use // VS + 1))
                    bank = t_bank()
                    for p in range(4):
                        last = tr(ps[:, bank, p * P:(p + 1) * P], vslot[(KEY_USE[c] + p // 2) % VS][:, p % 2, g * HD:(g + 1) * HD])
                        if g == G - 1 and p == 1:
                            last.then_inc(v_used, 1)
                    last.then_inc(t_full, 1)

                def scores(c):
                    pe.wait_ge(s_free, i * NSU + c + 1)
                    for g in range(G):
                        t_emptied("keys", c, g)
                        last = mm(ps[32 * g:32 * g + 32, 6, :], qSb[:, 32 * g:32 * g + 32], KTb[:, g, :])
                        if g == 0:
                            last.then_inc(v_used, 1)
                    last.then_inc(s_full, 1)

                def pv(use, probs, start):
                    for p in range(4):
                        s = (use + p // 2) % VS
                        if p % 2 == 0:
                            pe.wait_ge(v_full[s], i * 64 + 32 * ((use + p // 2) // VS + 1))
                        for g in range(G):
                            last = mm(ps[:, 7, 32 * g:32 * g + 32], vslot[s][:, p % 2, g * HD:(g + 1) * HD],
                                      probs[:, p, 32 * g:32 * g + 32], start=start and p == 0 and g == 0, stop=False, skip_group_check=True)
                        if p % 2 == 1:
                            last.then_inc(v_used, 1)

                def pv_new(br):
                    for g in range(G):
                        last = mm(ps[:, 7, 32 * g:32 * g + 32], vts[0:NS, br, 2, g * HD:(g + 1) * HD],
                                  PTn[0:NS, br, 32 * g:32 * g + 32], start=False, stop=True, skip_group_check=True)
                    last.then_inc(m_full, 1)

                def prompt_scores(qt, t):
                    pe.wait_ge(s_free, i * NSU + CHUNKS + qt * 2 + t + 1)
                    nk = (qt + 1) * P
                    for br in range(2):
                        last = mm(ps[:, 6, br * 256:br * 256 + nk], qst[:, t, qt * P:(qt + 1) * P],
                                  kTs[:, br, bass.ds(i // 2, 1), 0:nk].rearrange("p o k -> p (o k)"))
                    last.then_inc(s_full, 1)

                pe.wait_ge(st_sample, i * 3 + 3)
                for g in range(G):
                    keys(0, g)
                    z_part(g)
                    if g == 0:
                        m_bank(1)
                        for gg in range(G):
                            q = qSb[:, 32 * gg:32 * gg + 32]
                            mm(ps[32 * gg:32 * gg + 32, 7, 0:NBK], q, kcst[:, gg, :])
                            mm(ps[32 * gg:32 * gg + 32, 7, 64:128], q, kTs[:, 1, gg, NP:NT])
                            last = mm(ps[32 * gg:32 * gg + 32, 7, 128:192], q, kTs[:, 0, gg, NP:NT])
                        last.then_inc(m_full, 1)
                    if g == 1:
                        m_bank(2)
                        pe.wait_ge(p_ready, i + 1)
                        mm(ps[:, 7, 0:NBK], group[:], pcm).then_inc(m_full, 1)
                    if g == 2:
                        m_bank(3)
                        for gg in range(G):
                            last = tr(ps[0:NBK, 7, gg * HD:(gg + 1) * HD], vcst[:, gg, :])
                        last.then_inc(m_full, 1)
                    if g == 3:
                        m_bank(4)
                        tr(ps[0:NBK, 7, 0:P], pcm).then_inc(m_full, 1)
                scores(0)
                m_bank(5)
                for g in range(G):
                    last = mm(ps[:, 7, 32 * g:32 * g + 32], vcb[0:NBK, g * HD:(g + 1) * HD], pcT[0:NBK, 32 * g:32 * g + 32])
                last.then_inc(m_full, 1)
                for g in range(G):
                    keys(1, g)
                    z_part(4 + g)
                scores(1)
                pe.wait_ge(w_ready, i + 1)
                m_bank(6)
                bank = t_bank()
                for p in range(4):
                    last = tr(ps[:, bank, p * P:(p + 1) * P], S[:, p * P:(p + 1) * P])
                last.then_inc(t_full, 1)
                tr(ps[0:NS, 7, 0:P], S[:, WN:WN + NS]).then_inc(m_full, 1)
                for c in range(2, CHUNKS):
                    for g in range(G):
                        keys(c, g)
                        z_part(4 * c + g)
                        if c == 2 and g == 0:
                            m_bank(7)
                            t_emptied("probs_win", 0, 0)
                            pv(VWIN_USE, PT[0], True)
                            pv_new(1)
                    scores(c)
                pe.wait_ge(st_prompt, i * 4 + 4)
                for n in range(4):
                    z_part(20 + n)
                    prompt_scores(n // 2, n % 2)
                m_bank(8)
                for qt in range(2):
                    for t in range(2):
                        last = mm(ps[:, 7, (qt * 2 + t) * PBK:(qt * 2 + t + 1) * PBK], qst[:, t, qt * P:(qt + 1) * P],
                                  pcK[:, bass.ds(i // 2, 1), :].rearrange("p o n -> p (o n)"))
                last.then_inc(m_full, 1)
                pe.wait_ge(sel_ready, i + 1)
                for c in range(5):
                    bank = t_bank(c == 4)
                    if c < 4:
                        for p in range(4):
                            last = tr(ps[:, bank, p * P:(p + 1) * P], S[:, SL + (4 * c + p) * P:SL + (4 * c + p + 1) * P])
                    else:
                        last = tr(ps[0:NS, bank, 0:P], S[:, SN:SN + NS])
                    last.then_inc(t_full, 1)
                    if c == 0:
                        m_bank(9)
                    if c >= 1:
                        t_emptied("probs_sel", c - 1, 0)
                        pv(VSEL_USE + 2 * (c - 1), PT[(c - 1) % 2], c == 1)
                t_emptied("probs_new", 0, 0)
                pv_new(0)
                for c, (kt, qt) in enumerate(((0, 0), (0, 1), (1, 1))):
                    pe.wait_ge(pp_ready, i * 3 + qt + 1)
                    bank = t_bank()
                    for a in range(4):
                        last = tr(ps[:, bank, a * P:(a + 1) * P], Sp[:, qt, a, kt * P:(kt + 1) * P])
                    last.then_inc(t_full, 1)
                pe.wait_ge(pp_ready, i * 3 + 3)
                bank = t_bank()
                for t in range(2):
                    for qt in range(2):
                        last = tr(ps[0:PBK, bank, (t * 2 + qt) * P:(t * 2 + qt + 1) * P], pcs[:, qt * 2 + t, :])
                last.then_inc(t_full, 1)
                for br in range(2):
                    m_bank(10 + br)
                    if br == 0:
                        for c in range(3):
                            t_emptied("prompt", c, 0)
                    for t in range(2):
                        a = 2 * t + br
                        mm(ps[:, 7, t * NP:(t + 1) * NP], vst[:, br, 0, :], Pp[:, a, 0:NP], stop=False, skip_group_check=True)
                        last = mm(ps[:, 7, t * NP + P:(t + 1) * NP], vst[:, br, 1, :], Pp[:, a, NP:NP + P], start=False, skip_group_check=True)
                    last.then_inc(m_full, 1)
                m_bank(12)
                t_emptied("prompt_cmp", 0, 0)
                for t in range(2):
                    last = mm(ps[:, 7, t * NP:(t + 1) * NP], pvst[0:PBK, :], pcTp[0:PBK, t, :])
                last.then_inc(m_full, 1)
                assert t_at[0] == NTU

            pe.wait_ge(ots_out, 1)
            pe.wait_ge(m_free, B * NMU + 1)
            with pe.Fori(0, 2) as i:
                for n in range(8):
                    u, half = n // 2, n % 2
                    if half == 0:
                        pe.wait_ge(y_free, i * 4 + u + 1)
                    pe.wait_ge(w_full[n], i * 16 + 16 * (U_OUT // WS + 1))
                    for tt, (t0, nt) in enumerate(TOK):
                        for k in range(8):
                            h = half * 8 + k
                            lhsT = qP[:, h, t0:t0 + nt] if tt < 2 else oTs[:, h, :]
                            last = mm(ps[0:nt, 3 * (u % 2) + tt, 0:UNIT], lhsT, slot[n][:, k, :], start=h == 0, stop=False,
                                      skip_group_check=True)
                    last.then_inc(w_used, 1)
                    if half == 1:
                        pe.wait_ge(xst_out, i * 4 + u + 1)
                        for tt, (t0, nt) in enumerate(TOK):
                            for j in range(2):
                                last = mm(ps[0:nt, 3 * (u % 2) + tt, j * P:(j + 1) * P], xst[u % 2][:, j, t0:t0 + nt], ident[:],
                                          start=False, stop=True, skip_group_check=True)
                        last.then_inc(y_full, 1)

        @block.vector
        def _(dve):
            v = nc.vector
            link = Chain(dve, dchain)

            v.memset(cpad[:, :, 0:2], 0.0)
            for kt in range(0, KT, 2):
                dve.wait_ge(tp_full, kt + 1)
                v.tensor_copy(xT[:, kt, :], ps[:, kt % 8, 0:NT]).then_inc(tpd_free, 1)
            dve.wait_ge(consts_in, 16 * 13)
            dve.wait_ge(w2_zero, 1)
            for n, lo in enumerate((0, BLK)):
                v.tensor_copy(w2[lo:lo + BLK, :, :, n].rearrange("p c g -> p (c g)"), csb[lo:lo + BLK, 0, 0:2 * G]).then_inc(w2_done, 1)
            v.tensor_copy(tri[:], trif).then_inc(consts_used, 1)
            dve.wait_ge(vec_full, 1)
            v.tensor_copy(vecT[:], ps[:, 0, 0:100]).then_inc(vec_out, 1)
            dve.wait_ge(vec_full, 2)
            v.tensor_copy(stT.rearrange("p k c -> p (k c)"), ps[:, 1, 0:2 * B * KT]).then_inc(vec_out, 1)

            def scale_rows(gcol):
                for kt in range(KT):
                    v.scalar_tensor_tensor(out=hn[:, kt, :], in0=xT[:, kt, :], scalar=vecT[:, gcol + kt:gcol + kt + 1], in1=rstd,
                                           op0=ALU.mult, op1=ALU.mult).then_inc(hn_out, 1)

            def norm(n, bank, gcol):
                dve.wait_ge(sq_out, n)
                v.tensor_reduce(ssum, xsq.rearrange("p k t -> p t k"), AX.X, ALU.add).then_inc(sum_out, 1)
                dve.wait_ge(sum_full, n)
                v.tensor_scalar(rstd, ps[:, bank, 0:NT], 1.0 / D, EPS, ALU.mult, ALU.add).then_inc(var_out, 1)
                dve.wait_ge(sd_out, n)
                link(v.reciprocal(rstd, rstd))
                scale_rows(gcol)

            norm(1, 2, 0)

            with dve.Fori(0, B) as i:
                link.enter(i, 6)
                done = lambda u: dve.wait_ge(w_used, i * 8 + (WS + 2 * u + 2))
                done(1)
                dve.wait_ge(c_out, i + 1)
                v.tensor_tensor(cpad[:, :, 2:], csb[:, :, 0:NP], ps[:, 2:4, 0:NP], ALU.mult)
                for t in range(2):
                    ins = v.tensor_tensor(spad[:, t, :, 2:], csb[:, t, NP:NT].rearrange("p (b s) -> p b s", b=B),
                                          ps[:, 2 + t, NP:NT].rearrange("p (b s) -> p b s", b=B), ALU.mult)
                ins.then_inc(h_used, 1)
                for t in range(2):
                    ins = v.tensor_copy(spad[:, t, :, 0:2], stT[:, bass.ds(i * 2 + t, 1), :].rearrange("p o (b w) -> p (o b) w", w=2))
                link(ins)
                v.tensor_copy(cso[:, bass.ds(i * 2, 2), 0:2], cpad[:, :, NP:NP + 2])
                for t in range(2):
                    v.tensor_copy(cso[:, bass.ds(i * 2 + t, 1), 2:].rearrange("p o (b w) -> p (o b) w", w=2), spad[:, t, :, T:T + 2])
                for w in range(3):
                    for t in range(2):
                        tap = vecT[:, bass.ds(i * 2 + (48 + w * KT + t), 1)]
                        for o, a in ((bc[:, t, 0:NP], cpad[:, t, w:w + NP]),
                                     (bc[:, t, NP:NT].rearrange("p (b s) -> p b s", b=B), spad[:, t, :, w:w + T])):
                            if w == 0:
                                ins = v.tensor_scalar(o, a, tap, None, ALU.mult)
                            else:
                                ins = v.scalar_tensor_tensor(out=o, in0=a, scalar=tap, in1=o, op0=ALU.mult, op1=ALU.add)
                    link(ins)
                done(2)
                dve.wait_ge(e_out, i + 1)
                link(v.tensor_scalar(ez, ez, 1.0, None, ALU.add))
                link(v.reciprocal(ez, ez))
                ins = v.tensor_tensor(ez, ez, ps[:, 0:2, 0:NT], ALU.mult)
                ins.then_inc(zc_used, 1)
                done(3)
                ins = v.tensor_tensor(bc, bc, ps[:, 2:4, 0:NT], ALU.mult)
                ins.then_inc(b_used, 1)
                dve.wait_ge(b_used, i + 1 + 1)
                dve.wait_ge(zc_used, i + 1 + 1)
                v.tensor_tensor(yT[:, bass.ds(i * 2, 2), :], bc, ez, ALU.mult).then_inc(y_out, 1)
                dve.wait_ge(pg_used, i * NPG + (CS + NPG))
                v.tensor_copy(kcT[:, bass.ds(i, 1)].rearrange("p o g n -> p (o g n)"), ps[:, 6, 0:G * NBK]).then_inc(kc_out, 1)
            link.leave(B)

            with dve.Fori(0, 2) as i:
                for u in range(4):
                    dve.wait_ge(w_used, i * 8 + (WS + U_MIX + 2 * u + 2))
                    x = xT[:, bass.ds(i * 8 + 2 * u, 2), :]
                    v.tensor_tensor(x, x, ps[:, 2 * (u % 2):2 * (u % 2) + 2, 0:NT], ALU.add).then_inc(x1_out, 1)
            norm(2, 4, KT)

            def head_norm(q, gain, outs_, before):
                dve.wait_ge(hs_full, q + 1)
                v.tensor_scalar(rs, ps[:, 4:6, 0:NT], 1.0 / HD, EPS, ALU.mult, ALU.add).then_inc(hv_out, 1)
                dve.wait_ge(hsd_out, q + 1)
                link(v.reciprocal(rs, rs))
                link(v.scalar_tensor_tensor(out=kn, in0=raw, scalar=gain, in1=rs, op0=ALU.mult, op1=ALU.mult))
                two = lambda a: a.unsqueeze(1).to_broadcast([a.shape[0], 2, NT])
                v.tensor_tensor(ra, kn, two(cosT[:]), ALU.mult)
                v.tensor_tensor(sq[0:64], kn[64:128], two(sinT[64:128]), ALU.mult)
                link(v.tensor_tensor(sq[64:128], kn[0:64], two(sinT[0:64]), ALU.mult))
                before()
                for o, sel in outs_[:-1]:
                    v.tensor_tensor(o, sel(ra), sel(sq), ALU.add)
                o, sel = outs_[-1]
                v.tensor_tensor(o, sel(ra), sel(sq), ALU.add).then_inc(rope_out, 1)

            with dve.Fori(0, 3) as i:
                link.enter(i, 6)
                for gp in range(2):
                    def before(gp=gp):
                        if gp == 0:
                            dve.wait_ge(kcp_out, i + 1)
                            dve.wait_ge(kt_full, i * 3 + 1)
                    head_norm(i * 2 + gp, vecT[:, bass.ds(i + 96, 1)], [(kro[:, 2 * gp:2 * gp + 2, :], lambda a: a)], before)
                dve.wait_ge(w_used, i * 8 + (WS + U_KV + 8))
                for tt, (t0, nt) in enumerate(TOK):
                    v.tensor_copy(vto[0:nt, bass.ds(i, 1), tt, :].rearrange("p o c -> p (o c)"), ps[0:nt, tt, :]).then_inc(vt_out, 1)
            link.leave(3)
            scale_rows(2 * KT)
            dve.wait_ge(pc_full, 1)
            v.tensor_copy(pcK.rearrange("p g n -> p (g n)"), ps[:, 6, 0:G * PBK]).then_inc(pc_out, 1)
            v.tensor_copy(pcvT[:].rearrange("p g n -> p (g n)"), ps[:, 7, 0:G * PBK]).then_inc(pc_out, 1)

            with dve.Fori(0, 2) as i:
                link.enter(i, 12)
                for u in range(4):
                    h = i * 8 + 2 * u
                    outs_ = [(qP[:, bass.ds(h, 2), :], lambda a: a[:, :, 0:NP])]
                    for t in range(2):
                        outs_.append((qS[:, :, bass.ds((h + t) * T, T)],
                                      lambda a, t=t: a[:, t, NP:NT].rearrange("p (b s) -> p b s", b=B)))
                    head_norm(i * 4 + 6 + u, vecT[:, 99:100], outs_, lambda: None)
            link.leave(2)
            dve.wait_ge(pv_full, 1)
            v.tensor_copy(pcV.rearrange("p g d -> p (g d)")[0:PBK], ps[0:PBK, 6, :]).then_inc(pv_out, 1)
            dve.wait_ge(ge_out, 1)
            v.tensor_scalar(gd[0:GATES], gd[0:GATES], 1.0, None, ALU.add).then_inc(gd_out, 1)
            dve.wait_ge(gates_out, 16)
            dve.wait_ge(kv_store, 16 * 12)
            dve.wait_ge(x1_store, 16)
            dve.wait_ge(vts_out, 2)

            PER_MAIN = 24
            with dve.Fori(0, B) as i:
                link.enter(i, PER_MAIN)
                st = lambda a, n=1: stat[:, a:a + n]

                def m_copy(n, out, in_):
                    dve.wait_ge(m_full, i * NMU + n + 1)
                    v.tensor_copy(out, in_).then_inc(m_free, 1)
                    dve.wait_ge(m_free, i * NMU + n + 1)

                def negmax(a, src):
                    link(v.tensor_reduce(st(a), src, AX.X, ALU.max, negate=True))
                    return v.tensor_scalar(st(a), st(a), SCALE, None, ALU.mult)

                def normalise(a, probs):
                    link(v.reciprocal(st(a + 2), st(a + 1)))
                    return v.tensor_scalar(probs, probs, st(a + 2), None, ALU.mult)

                def evens(lo, hi):
                    for n in range(lo, hi):
                        if n % 2 == 0:
                            empty_t(dve, v.tensor_copy, n, i)

                def z_unit(u):
                    dve.wait_ge(ze_out, i * 3 + u + 1)
                    dve.wait_ge(gb_full[u % 2], (i * 32 + 16 * (u // 2 + 1)) if u % 2 == 0 else i * 16 + 16)
                    v.scalar_tensor_tensor(out=ezm, in0=ezm, scalar=1.0, in1=gbc[u % 2], op0=ALU.add, op1=ALU.mult).then_inc(gb_used, 1)
                    dve.wait_ge(gb_used, i * 3 + u + 1)
                    link(v.reciprocal(ezm, ezm))
                    bank = 2 * (u % 2)
                    v.tensor_tensor(zgP[:, u], ezm[:, :, 0:NP], ps[:, bank:bank + 2, 0:NP], ALU.mult)
                    v.tensor_tensor(zS[:, u, bass.ds(i * 2, 2), :], ezm[:, :, NP:NT], ps[:, bank:bank + 2, NP:NT], ALU.mult).then_inc(zu_free, 1)

                def s_wait(n):
                    dve.wait_ge(s_full, i * NSU + n + 1)

                def sel_scores(c):
                    s_wait(c)
                    lo = 8 * (c - 1)
                    v.tensor_tensor(S[:, SL + lo * BLK:SL + (lo + 8) * BLK].rearrange("p (n l) -> p n l", l=BLK),
                                    ps[:, 6, :].rearrange("p (n l) -> p n l", l=BLK),
                                    bmask[:, lo:lo + 8].unsqueeze(2).to_broadcast([P, 8, BLK]), ALU.add).then_inc(s_free, 1)

                evens(0, 1)
                m_copy(1, msb, ps[:, 7, 0:192])
                nm = newmask[:, bass.ds(i, 1), :].rearrange("p o s -> p (o s)")
                v.tensor_tensor(S[:, WN:WN + NS], msb[:, 64:128], nm, ALU.add)
                v.tensor_tensor(S[:, SN:SN + NS], msb[:, 128:192], nm, ALU.add)
                negmax(0, msb[:, 0:NBK]).then_inc(cexp_in, 1)
                dve.wait_ge(cexp_out, i + 1)
                normalise(0, pcm).then_inc(p_ready, 1)
                m_copy(2, psc, ps[:, 7, 0:NBK])
                evens(1, 3)
                m_copy(3, vcb[0:NBK], ps[0:NBK, 7, :])
                m_copy(4, pcT[0:NBK], ps[0:NBK, 7, 0:P])
                s_wait(0)
                v.tensor_tensor(S[:, 0:T], ps[:, 6, 0:T], winmask[:], ALU.add)
                v.tensor_copy(S[:, T:WIN], ps[:, 6, T:WIN]).then_inc(s_free, 1)
                dve.wait_ge(s_free, i * NSU + 2)
                m_copy(5, oS[:, 0, bass.ds(i, 1), :].rearrange("p o c -> p (o c)"), ps[:, 7, 0:H * T])
                negmax(3, S[:, 0:WIN + NS]).then_inc(wexp_in, 1)
                evens(3, 5)
                s_i = psc[:, 1:1 + MID].unsqueeze(1).to_broadcast([P, MID, MID])
                s_j = psc[:, 1:1 + MID].unsqueeze(2).to_broadcast([P, MID, MID])
                v.tensor_tensor(gt, s_i, s_j, ALU.is_gt)
                link(v.tensor_tensor(eq, s_i, s_j, ALU.is_equal))
                link(v.tensor_tensor(eq, eq, tri[:], ALU.mult))
                link(v.tensor_tensor(gt, gt, eq, ALU.add))
                v.memset(bmask[:, 0:1], 0.0)
                v.memset(bmask[:, NBK - 1:NBK], 0.0)
                link(v.tensor_reduce(bmask[:, 1:1 + MID], gt, AX.X, ALU.add))
                link(v.tensor_scalar(bmask[:, 1:1 + MID], bmask[:, 1:1 + MID], float(KEEP), NEG, ALU.is_ge, ALU.mult))
                dve.wait_ge(wexp_out, i + 1)
                normalise(3, S[:, 0:WIN + NS]).then_inc(w_ready, 1)
                evens(5, 8)
                sel_scores(1)
                evens(8, 9)
                m_copy(6, PTn[0:NS, 1, :], ps[0:NS, 7, 0:P])
                m_copy(7, oS[:, 2, bass.ds(i, 1), :].rearrange("p o c -> p (o c)"), ps[:, 7, 0:H * T])
                z_unit(0)
                evens(9, 13)
                sel_scores(2)
                evens(13, 17)
                sel_scores(3)
                z_unit(1)
                evens(17, 21)
                sel_scores(4)
                dve.wait_ge(s_free, i * NSU + CHUNKS + 1)
                negmax(6, S[:, SL:]).then_inc(sexp_in, 1)

                def prompt_scores(qt, t):
                    s_wait(CHUNKS + 2 * qt + t)
                    bank = ps[:, 6, :].rearrange("p (a k) -> p a k", a=2)
                    if qt:
                        v.tensor_copy(Sp[:, qt, 2 * t:2 * t + 2, 0:P], bank[:, :, 0:P])
                    v.tensor_tensor(Sp[:, qt, 2 * t:2 * t + 2, qt * P:(qt + 1) * P], bank[:, :, qt * P:(qt + 1) * P],
                                    causal[:].unsqueeze(1).to_broadcast([P, 2, P]), ALU.add).then_inc(s_free, 1)

                def prompt_max(qt):
                    dve.wait_ge(s_free, i * NSU + CHUNKS + 2 * qt + 3)
                    link(v.tensor_reduce(st(16 + 4 * qt, 4), Sp[:, qt, :, 0:(qt + 1) * P], AX.X, ALU.max, negate=True))
                    v.tensor_scalar(st(16 + 4 * qt, 4), st(16 + 4 * qt, 4), SCALE, None, ALU.mult).then_inc(pexp_in, 1)

                def prompt_scale(qt):
                    dve.wait_ge(pexp_out, i * 3 + qt + 1)
                    link(v.reciprocal(st(32 + 4 * qt, 4), st(24 + 4 * qt, 4)))
                    a = Sp[:, qt, :, 0:(qt + 1) * P]
                    v.tensor_tensor(a, a, st(32 + 4 * qt, 4).unsqueeze(2).to_broadcast([P, 4, (qt + 1) * P]), ALU.mult).then_inc(pp_ready, 1)

                prompt_scores(0, 0)
                prompt_scores(0, 1)
                prompt_max(0)
                dve.wait_ge(sexp_out, i + 1)
                normalise(6, S[:, SL:]).then_inc(sel_ready, 1)
                prompt_scores(1, 0)
                prompt_scores(1, 1)
                prompt_max(1)
                prompt_scale(0)
                z_unit(2)
                dve.wait_ge(m_full, i * NMU + 8 + 1)
                four = lambda a: a.unsqueeze(2).to_broadcast([P, 4, PBK])
                mask = lambda a: a[:].unsqueeze(2).to_broadcast([P, 2, 2, PBK])
                pcs4 = pcs.rearrange("p (q t) n -> p q t n", t=2)
                v.tensor_tensor(pcs4, ps[:, 7, 0:4 * PBK].rearrange("p (q t n) -> p q t n", q=2, t=2), mask(pcmask), ALU.add).then_inc(m_free, 1)
                dve.wait_ge(m_free, i * NMU + 9)
                link(v.tensor_reduce(st(40, 4), pcs, AX.X, ALU.max))
                v.tensor_tensor(pcs, pcs, four(st(40, 4)), ALU.subtract).then_inc(pexp_in, 1)
                prompt_scale(1)
                dve.wait_ge(pexp_out, i * 3 + 3)
                link(v.tensor_reduce(st(44, 4), pcs, AX.X, ALU.add))
                link(v.reciprocal(st(48, 4), st(44, 4)))
                link(v.tensor_tensor(pcs, pcs, four(st(48, 4)), ALU.mult))
                v.tensor_tensor(pcs4, pcs4, mask(pckeep), ALU.mult).then_inc(pp_ready, 1)
                evens(21, 26)
                m_copy(9, oS[:, 1, bass.ds(i, 1), :].rearrange("p o c -> p (o c)"), ps[:, 7, 0:H * T])
                evens(26, NTU)
                o = qP[:, bass.ds(i * 2, 2), :]
                for n, br in ((10, 1), (11, 2), (12, 0)):
                    dve.wait_ge(m_full, i * NMU + n + 1)
                    pso = ps[:, 7, :].rearrange("p (t q) -> p t q", t=2)
                    v.tensor_tensor(o if n == 10 else otmp, zgP[:, br], pso, ALU.mult).then_inc(m_free, 1)
                    dve.wait_ge(m_free, i * NMU + n + 1)
                    if n > 10:
                        link(v.tensor_tensor(o, o, otmp, ALU.add))
            link.leave(B)

            bht = lambda a: a.rearrange("p b (h s) -> p b h s", s=T)
            hbt = lambda a: a.rearrange("p h (b s) -> p b h s", s=T)
            dve.wait_ge(m_full, B * NMU + 1)
            for br in range(3):
                ins = None
                for b in range(B):
                    o3 = hbt(oTs if br == 0 else oadd)[:, b]
                    ins = v.tensor_tensor(o3, bht(oS[:, br])[:, b], hbt(zS[:, br])[:, b], ALU.mult)
                link(ins)
                if br == 1:
                    link(v.tensor_tensor(oTs, oTs, oadd, ALU.add))
            v.tensor_tensor(oTs, oTs, oadd, ALU.add).then_inc(ots_out, 1)

        @block.scalar
        def _(act):
            s = nc.scalar
            link = Chain(act, achain)

            for kt in range(1, KT, 2):
                act.wait_ge(tp_full, kt + 1)
                s.copy(xT[:, kt, :], ps[:, kt % 8, 0:NT]).then_inc(tpa_free, 1)

            def norm(n):
                s.activation(xsq, xT, ACT.Square).then_inc(sq_out, 1)
                act.wait_ge(var_out, n)
                s.activation(rstd, rstd, ACT.Sqrt).then_inc(sd_out, 1)

            act.wait_ge(tpd_free, 8)
            act.wait_ge(tpa_free, 8)
            act.wait_ge(vec_out, 2)
            act.wait_ge(consts_used, 1)
            norm(1)
            act.wait_ge(w2_done, 2)

            with act.Fori(0, B) as i:
                act.wait_ge(w_used, i * 8 + (WS + 2))
                act.wait_ge(h_used, i + 1)
                s.copy(csb, ps[:, 0:2, 0:NT]).then_inc(c_out, 1)
                act.wait_ge(w_used, i * 8 + (WS + 6))
                act.wait_ge(y_out, i + 1)
                s.activation(ez, ps[:, 0:2, 0:NT], ACT.Exp, scale=-1.0).then_inc(e_out, 1)
                act.wait_ge(pg_used, i * NPG + (CS + NPG))
                s.copy(vcT[:, bass.ds(i, 1)].rearrange("p o g n -> p (o g n)"), ps[:, 7, 0:G * NBK]).then_inc(vc_out, 1)
            for n in range(4):
                act.wait_ge(cs_full, n + 1)
                s.copy(crow[0:18, n * 512:(n + 1) * 512], ps[0:18, 4 + n % 2, :]).then_inc(cs_out, 1)
            act.wait_ge(cs_out, 4)
            act.dma_start(conv_p.rearrange("l b w d -> (l b w) d"), crow[0:2, :]).then_inc(cs_store, 16)
            act.dma_start(conv_s.rearrange("l b w d -> (l b w) d"), crow[2:18, :]).then_inc(cs_store, 16)

            act.wait_ge(cs_store, 32)
            act.wait_ge(x1_out, 2 + 8)
            norm(2)
            act.dma_start(x1_dram.rearrange("p (k t) -> p k t", k=KT), xT).then_inc(x1_store, 16)

            def head(q, use, bank):
                act.wait_ge(w_used, use)
                act.wait_ge(rope_out, q + 1)
                s.copy(raw, ps[:, bank:bank + 2, 0:NT])
                s.activation(sq, ps[:, bank:bank + 2, 0:NT], ACT.Square).then_inc(sqr_out, 1)
                act.wait_ge(hv_out, q + 1)
                s.activation(rs, rs, ACT.Sqrt).then_inc(hsd_out, 1)

            with act.Fori(0, 3) as i:
                for gp in range(2):
                    head(i * 2 + gp, i * 8 + (WS + U_KV + 2 * gp + 2), 2 * gp)
                for tt, (t0, nt) in enumerate(TOK):
                    act.wait_ge(kt_full, i * 3 + tt + 1 + 1)
                    s.copy(kto[0:nt, bass.ds(i, 1), tt, :].rearrange("p o c -> p (o c)"), ps[0:nt, (6, 7, 3)[tt], :]).then_inc(kt_out, 1)
            act.wait_ge(kt_out, 3 + 9)
            act.wait_ge(vt_out, 10)
            for br in range(3):
                for c, src in ((0, kto), (1, vto)):
                    if br < 2:
                        dp = rows_p[0, :, 2 * br + c].rearrange("(t p) g d -> p t (g d)", p=P)
                        ds_ = rows_s[:, :, 2 * br + c].rearrange("b t g d -> (b t) (g d)")
                        act.dma_start(dp, src[:, br, 0:2, :]).then_inc(kv_store, 16)
                        act.dma_start(ds_, src[0:NS, br, 2, :]).then_inc(kv_store, 16)
                    else:
                        dp = win_p[0, :, c].rearrange("(t p) g d -> p t (g d)", p=P)
                        act.dma_start(dp, src[:, br, 0:2, :]).then_inc(kv_store, 16)
                        act.dma_start(win_s[:, WIN - T:WIN, c].rearrange("b t g d -> b t (g d)"), src[0:NS, br, 2, :]).then_inc(kv_store, 16)
            act.wait_ge(kv_store, 16 * 12)
            act.wait_ge(pc_full, 1)
            act.dma_start(wgt, w_qz[0, :, 4 * HDALL:4 * HDALL + GATES].rearrange("(k p) c -> p k c", p=P)).then_inc(wg_in, 16)

            with act.Fori(0, 2) as i:
                for u in range(4):
                    head(i * 4 + 6 + u, i * 8 + (WS + U_QUERY + 2 * u + 2), 2 * (u % 2))
            act.wait_ge(g_full, 1)
            act.wait_ge(rope_out, 15)
            s.activation(gd[0:GATES], ps[0:GATES, 0, 0:NT], ACT.Exp, scale=-1.0).then_inc(ge_out, 1)
            act.wait_ge(gd_out, 1)
            act.dma_start(gates_dram, gd[0:GATES]).then_inc(gates_out, 16)
            act.wait_ge(gates_out, 16)
            act.wait_ge(x1_store, 16)
            act.wait_ge(vts_out, 2)

            with act.Fori(0, B) as i:
                st = lambda a, n=1: stat[:, a:a + n]

                def odds(lo, hi):
                    for n in range(lo, hi):
                        if n % 2 == 1:
                            empty_t(act, s.copy, n, i)

                def exp_z(u):
                    act.wait_ge(z_used, i * 12 + (ZS + 4 * u + 4))
                    act.wait_ge(zu_free, i * 3 + u + 1)
                    s.activation(ezm, ps[:, 2 * (u % 2):2 * (u % 2) + 2, 0:NT], ACT.Exp, scale=-1.0).then_inc(ze_out, 1)

                act.wait_ge(cexp_in, i + 1)
                s.activation(pcm, msb[:, 0:NBK], ACT.Exp, bias=st(0), scale=SCALE, accum_out=st(1)).then_inc(cexp_out, 1)
                odds(0, 4)
                act.wait_ge(wexp_in, i + 1)
                s.activation(S[:, 0:WIN + NS], S[:, 0:WIN + NS], ACT.Exp, bias=st(3), scale=SCALE, accum_out=st(4)).then_inc(wexp_out, 1)
                odds(4, 8)
                exp_z(0)
                odds(8, 16)
                exp_z(1)
                odds(16, 21)
                act.wait_ge(sexp_in, i + 1)
                s.activation(S[:, SL:], S[:, SL:], ACT.Exp, bias=st(6), scale=SCALE, accum_out=st(7)).then_inc(sexp_out, 1)
                for qt in range(2):
                    act.wait_ge(pexp_in, i * 3 + qt + 1)
                    for a in range(4):
                        x = Sp[:, qt, a, 0:(qt + 1) * P]
                        ins = s.activation(x, x, ACT.Exp, bias=st(16 + 4 * qt + a), scale=SCALE, accum_out=st(24 + 4 * qt + a))
                    ins.then_inc(pexp_out, 1)
                exp_z(2)
                act.wait_ge(pexp_in, i * 3 + 3)
                s.activation(pcs, pcs, ACT.Exp, scale=SCALE).then_inc(pexp_out, 1)
                odds(21, NTU)

            for n in range(8):
                act.wait_ge(y_full, n + 1)
                if n >= 2:
                    act.wait_ge(y_stored[n % 2], 32 * (n // 2))
                for tt, (t0, nt) in enumerate(TOK):
                    ins = s.copy(ysb[n % 2][0:nt, tt, :], ps[0:nt, 3 * (n % 2) + tt, 0:UNIT])
                ins.then_inc(y_free, 1)
                act.wait_ge(y_free, 2 + n + 1)
                cols = slice(n * UNIT, (n + 1) * UNIT)
                act.dma_start(y_p[0, :, cols].rearrange("(t p) c -> p t c", p=P), ysb[n % 2][:, 0:2, :]).then_inc(y_stored[n % 2], 16)
                act.dma_start(y_s[:, :, cols].rearrange("b t c -> (b t) c"), ysb[n % 2][0:NS, 2, :]).then_inc(y_stored[n % 2], 16)


_INS = ['x_prompt', 'x_sample', 'state_conv', 'cache_kv', 'state_win', 'page_table', 'g_a', 'w_in_a', 'conv_w', 'w_out_a',
        'g_kv', 'w_kv', 'g_k', 'w_cmp', 'g_b', 'w_qz', 'g_q', 'w_out_b']
_OUTS = [(1, NP, D), (B, T, D), (1, 1, 2, D), (1, B, 2, D), (1, NP, 4, G, HD), (B, T, 4, G, HD), (1, NP, 2, G, HD),
         (B, WIN, 2, G, HD)]


def tables():
    f = np.float32
    half = HD // 2
    inv = (10000.0 ** (-np.arange(half) / half)).astype(f)
    pos = np.concatenate([np.arange(NP), np.tile(PAST + np.arange(T), B)]).astype(f)
    ang = (pos[None, :] * inv[:, None]).astype(np.float64)
    row, t = np.arange(P), np.arange(P) % T
    new_b, new_t = np.arange(NS) // T, np.arange(NS) % T
    ok_new = (new_b[None, None] == np.arange(B)[None, :, None]) & (new_t[None, None] <= t[:, None, None])
    blk_end = np.arange(PBK) * BLK + BLK - 1
    ok_cmp = blk_end[None, None] <= row[:, None, None] + P * np.arange(2)[None, :, None]
    hide = lambda ok: np.where(ok, 0.0, NEG).astype(f)
    j = np.arange(MID)
    return {
        "ident": np.eye(P, dtype=f),
        "ones": np.ones((P, P), f),
        "group": ((row[:, None] // 32 == row[None] // 32) & (t[:, None] == t[None])).astype(f),
        "causal": hide(row[None] <= row[:, None]),
        "cosT": np.tile(np.cos(ang), (2, 1)).astype(f),
        "sinT": np.concatenate([np.sin(ang), -np.sin(ang)]).astype(f),
        "newmask": hide(ok_new),
        "winmask": hide(np.arange(T)[None] > t[:, None]),
        "tri": np.tile((j[None] < j[:, None]).astype(f)[None], (P, 1, 1)),
        "pcmask": hide(ok_cmp),
        "pckeep": ok_cmp.astype(f),
    }


def kernel(**inputs):
    import concourse.bacc as bacc
    from concourse.bass_utils import run_bass_kernel_spmd

    nc = bacc.Bacc("TRN2", target_bir_lowering=False, num_devices=1, dynamic_dma_scratch_size=1024)
    arrays, ins = {}, []
    for name in _INS:
        a = np.ascontiguousarray(inputs[name])
        arrays[f"in_{name}"] = a
        ins.append(nc.dram_tensor(f"in_{name}", a.shape, mybir.dt.from_np(a.dtype), kind="ExternalInput").ap())
    consts = {}
    for name, a in tables().items():
        arrays[f"table_{name}"] = a
        consts[name] = nc.dram_tensor(f"table_{name}", a.shape, F32, kind="ExternalInput").ap()
    outs = [nc.dram_tensor(f"out_{n}", shape, F32, kind="ExternalOutput").ap() for n, shape in enumerate(_OUTS)]
    scratch = [nc.dram_tensor("gates", (GATES, NT), F32, kind="Internal").ap(),
               nc.dram_tensor("x1", (P, KT * NT), F32, kind="Internal").ap()]
    build(nc, ins, consts, outs, scratch)
    r = run_bass_kernel_spmd(nc, [arrays], core_ids=[0])
    return tuple(r.results[0][f"out_{n}"] for n in range(len(_OUTS)))
```

```python
from contextlib import ExitStack

import numpy as np

import concourse.bass as bass
import concourse.mybir as mybir

F32 = mybir.dt.float32
FR = mybir.dt.float32r
BF16 = mybir.dt.bfloat16
I32 = mybir.dt.int32
ACT = mybir.ActivationFunctionType
ALU = mybir.AluOpType
AX = mybir.AxisListType

P = 128
D = 2048
KT = D // P
NP = 256
B, T = 8, 8
NS = B * T
NT = NP + NS
H, G = 16, 4
R = H // G
HD = 128
PAST, PAGE, BLK, WIN = 2048, 128, 64, 512
N_SEL = 16
NPG = PAST // PAGE
NBK = PAST // BLK
PBK = NP // BLK
MID = NBK - 2
KEEP = N_SEL - 3
EPS = 1e-6
NEG = -1e30
SCALE = HD ** -0.5
UNIT = 256
GATES = 3 * H

WS = 4
WSZ = KT // 4 * UNIT
GK = 2
GSZ = GK * UNIT
GPS = WSZ // GSZ
HS = 4
HALF = KT // 2 // GK
ZS = 2
CS = 2
CPG = 4
TPP = CPG * PAGE // P
GPSQ = NPG // CPG
VS = 4
VSZ = 2 * G * HD

TOK = ((0, P), (P, P), (NP, NS))


class Chain:

    def __init__(self, eng, sem):
        self.eng, self.sem, self.base, self.n = eng, sem, 0, 0

    def __call__(self, ins):
        self.n += 1
        ins.then_inc(self.sem, 1)
        self.eng.wait_ge(self.sem, self.base + self.n)

    def enter(self, i, per):
        self.start, self.per = self.base + self.n, per
        self.base, self.n = i * per + self.start, 0

    def leave(self, trips):
        assert self.n == self.per, (self.n, self.per)
        self.base, self.n = self.start + trips * self.per, 0


T_USES = ([("keys", c, g) for c in range(2) for g in range(G)] + [("probs_win", 0, 0)]
          + [("keys", c, g) for c in range(2, 5) for g in range(G)]
          + [("probs_sel", c, 0) for c in range(4)] + [("probs_new", 0, 0)]
          + [("prompt", c, 0) for c in range(3)] + [("prompt_cmp", 0, 0)])
NTU = len(T_USES)
assert NTU % 2 == 0
CHUNKS = 1 + PAST // 512
NSU = CHUNKS + 4
NMU = 12
KEY_USE = (0, 2, 6, 8, 10)
VWIN_USE, VSEL_USE, V_USES = 4, 12, 20


def build(nc, ins, consts, outs, scratch):
    (x_prompt, x_sample, state_conv, cache_kv, state_win, page_table, g_a, w_in_a, conv_w, w_out_a,
     g_kv, w_kv, g_k, w_cmp, g_b, w_qz, g_q, w_out_b) = ins
    y_p, y_s, conv_p, conv_s, rows_p, rows_s, win_p, win_s = outs
    gates_dram, x1_dram = scratch

    with ExitStack() as ctx:
        def sem(name):
            return ctx.enter_context(nc.semaphore(name))

        ps = ctx.enter_context(nc.psum_tensor("ps", [P, 8, 512], F32))

        def sb(name, *shape, dt=F32):
            return ctx.enter_context(nc.sbuf_tensor(name, [P, *shape], dt))

        ident, ones, group, causal = (sb(n, P) for n in ("ident", "ones", "group", "causal"))
        cosT, sinT = sb("cosT", NT), sb("sinT", NT)
        newmask = sb("newmask", B, NS)
        winmask = sb("winmask", T)
        tri = sb("tri", MID, MID, dt=BF16)
        pcmask, pckeep = sb("pcmask", 2, PBK), sb("pckeep", 2, PBK)
        vecT = sb("vecT", 100)
        w2 = sb("w2", 2, G, 2)
        wc = sb("wc", TPP, 2 * G)
        inblk = sb("inblk", P // (BLK // TPP))
        ptab = sb("ptab", B * NPG, dt=I32)
        pcvT = sb("pcvT", G, PBK)
        kcT, vcT = sb("kcT", B, G, NBK), sb("vcT", B, G, NBK)
        WRING = 7168
        wring = sb("wring", WRING)
        w_hi, w_lo = sb("w_hi", HS, GK, UNIT, dt=FR), sb("w_lo", HS, GK, UNIT, dt=FR)
        hn_hi, hn_lo = sb("hn_hi", KT, NT, dt=FR), sb("hn_lo", KT, NT, dt=FR)
        as_f32 = lambda a: a.bitcast(F32)
        BIG = 30720
        big = sb("big", BIG)

        class Region:
            def __init__(self, lo, hi):
                self.at, self.hi = lo, hi

            def take(self, *shape):
                n = int(np.prod(shape))
                v = big[:, self.at:self.at + n]
                self.at += n
                assert self.at <= self.hi, ("region", self.at, self.hi)
                if len(shape) > 1:
                    names = "abcd"[:len(shape)]
                    v = v.rearrange(f"p ({' '.join(names)}) -> p {' '.join(names)}", **dict(zip(names, shape)))
                return v

        kc = lambda a: a.rearrange("p (k c) -> p k c", c=UNIT)
        slot = [kc(wring[:, s * WSZ:(s + 1) * WSZ]) for s in range(WS)]
        zslot = [kc(wring[:, s * GSZ:(s + 1) * GSZ]) for s in range(ZS)]
        Sp = wring[:, WSZ:WSZ + 2048].rearrange("p (q a k) -> p q a k", q=2, a=4)
        VLO = WSZ + 2048
        assert ZS * GSZ <= WSZ and VLO + VS * VSZ <= WRING and VLO + VSZ >= WS * WSZ
        vslot = [wring[:, VLO + s * VSZ:VLO + (s + 1) * VSZ].rearrange("p (k c) -> p k c", k=2) for s in range(VS)]

        XLO = BIG - KT * NT
        xT = big[:, XLO:BIG].rearrange("p (k t) -> p k t", k=KT)
        rstd = big[:, XLO - NT:XLO]
        keep = Region(0, BIG)
        qS = keep.take(B, H * T)
        qP = keep.take(H, NP)
        kTs = keep.take(2, G, NT)
        vts = keep.take(2, 3, G * HD)
        pcK = keep.take(G, PBK)
        pcV = keep.take(G, HD)
        tmp = Region(keep.at, XLO - NT)
        kro = tmp.take(G, NT)
        vto, kto = tmp.take(3, 3, G * HD), tmp.take(3, 3, G * HD)
        HEADS = tmp.at
        raw, sq, rs, kn, ra = (tmp.take(2, NT) for _ in range(5))
        wgt = kto.rearrange("p a b c -> p (a b c)")[:, 0:KT * GATES].rearrange("p (k c) -> p k c", c=GATES)
        wg_hi, wg_lo = (w[:].rearrange("p h k c -> p (h k c)")[:, 0:KT * GATES].rearrange("p (k c) -> p k c", c=GATES)
                        for w in (w_hi, w_lo))
        hnf_b = [big[:, a:a + 4 * NT].rearrange("p (k t) -> p k t", t=NT) for a in (HEADS, HEADS + 4 * NT)]
        gd = rs[:, 0, :]
        early = Region(0, XLO - NT)
        yT = early.take(KT, NT)
        pgs = early.take(CS, TPP, 2 * G * HD)
        pg = [pgs[:, s] for s in range(CS)]
        xin = big[:, KT * NT:KT * NT + 3 * D].rearrange("p (t d) -> p t d", t=3)
        cpad = early.take(2, NP + 2)
        spad = early.take(2, B, T + 2)
        csb, ez, bc = (early.take(2, NT) for _ in range(3))
        stT = early.take(KT, 2 * B)
        cso = early.take(KT, 2 + 2 * B)
        ssum = early.take(NT)
        xsq = early.take(KT, NT)
        xsqf = xsq.rearrange("p k t -> p (k t)")
        vecs, stin = xsqf[:, 0:P], xsqf[:, P:P + D]
        crow = pgs[:, 0].rearrange("p t c -> p (t c)")[:, 0:D]
        hnf = [early.take(4, NT) for _ in range(2)]
        trif = xsqf[:, P + D:P + D + MID * MID].rearrange("p (j i) -> p j i", i=MID)
        main = Region(keep.at, BIG)
        zS = main.take(3, H, NS)
        oS = main.take(3, B, H * T)
        LATE = main.at
        KTb = main.take(G, 512)
        Pp = KTb.rearrange("p g k -> p (g k)")[:, 0:4 * 384].rearrange("p (a q) -> p a q", a=4)
        S = main.take(WIN + NS + PAST + NS)
        PT = [main.take(4, P) for _ in range(2)]
        gt, eq = (PT[n].rearrange("p a b -> p (a b)")[:, 0:MID * MID // 2].bitcast(BF16)
                  .rearrange("p (j i) -> p j i", i=MID) for n in range(2))
        PTn = main.take(2, P)
        gbc = [main.take(2, NT) for _ in range(2)]
        ezm = main.take(2, NT)
        zgP = main.take(3, 2, NP)
        vst = main.take(2, 2, HD)
        pvst = main.take(HD)
        qst = main.take(2, NP)
        qSb = main.take(H * T)
        vcst, kcst = main.take(G, NBK), main.take(G, NBK)
        vcb = main.take(G * HD)
        msb = main.take(192)
        pcm, psc, bmask = main.take(NBK), main.take(NBK), main.take(NBK)
        pcT = main.take(H * T)
        pcTp = main.take(2, NP)
        pcs = main.take(4, PBK)
        stat = main.take(64)
        otmp = main.take(2, NP)
        late = Region(LATE, XLO)
        oTs = late.take(H, NS)
        oadd = late.take(H, NS)
        xst = [late.take(2, NT) for _ in range(2)]
        ysb = [late.take(3, UNIT) for _ in range(2)]

        WN, SL, SN = WIN, WIN + NS, WIN + NS + PAST

        KT_BANKS, VT_BANKS = (7, 3, 2), (0, 1, 6)

        x_in, misc_in, consts_in = sem("x_in"), sem("misc_in"), sem("consts_in")
        w2_zero, w2_done, consts_used = sem("w2_zero"), sem("w2_done"), sem("consts_used")
        tp_full, tpd_free, tpa_free = sem("tp_full"), sem("tpd_free"), sem("tpa_free")
        vec_full, vec_out = sem("vec_full"), sem("vec_out")
        sq_out, sum_out, sum_full, var_out, sd_out, hn_out = (sem(n) for n in (
            "sq_out", "sum_out", "sum_full", "var_out", "sd_out", "hn_out"))
        w_full, w_used = [sem(f"w_full{s}") for s in range(WS)], sem("w_used")
        w_asked = sem("w_asked")
        hi_out, split_out, hn_raw, hn_hid = sem("hi_out"), sem("split_out"), sem("hn_raw"), sem("hn_hid")
        z_full = [sem(f"z_full{s}") for s in range(ZS)]
        v_full, v_used = [sem(f"v_full{s}") for s in range(VS)], sem("v_used")
        pg_full, pg_used, pg_summed = [sem(f"pg_full{s}") for s in range(CS)], sem("pg_used"), sem("pg_summed")
        c_out, h_used, e_out, zc_used, b_used, y_out = (sem(n) for n in (
            "c_out", "h_used", "e_out", "zc_used", "b_used", "y_out"))
        kc_out, vc_out = sem("kc_out"), sem("vc_out")
        cs_full, cs_out = sem("cs_full"), sem("cs_out")
        x1_out = sem("x1_out")
        dchain, achain = sem("dchain"), sem("achain")
        cs_store, x1_store, kv_store, wcopy = (sem(n) for n in ("cs_store", "x1_store", "kv_store", "wcopy"))
        sqr_out, hs_full, hv_out, hsd_out, rope_out, kcp_out = (sem(n) for n in (
            "sqr_out", "hs_full", "hv_out", "hsd_out", "rope_out", "kcp_out"))
        kt_full, kt_out, vt_out = sem("kt_full"), sem("kt_out"), sem("vt_out")
        pc_full, pc_out, pv_full, pv_out, vts_out = (sem(n) for n in ("pc_full", "pc_out", "pv_full", "pv_out", "vts_out"))
        wg_in, wg_out, g_full, ge_out, gd_out, gates_out = (sem(n) for n in ("wg_in", "wg_out", "g_full", "ge_out", "gd_out", "gates_out"))
        gb_full, gb_used = [sem("gb_full0"), sem("gb_full1")], sem("gb_used")
        st_sample, st_prompt = sem("st_sample"), sem("st_prompt")
        t_full, td_free, ta_free = sem("t_full"), sem("td_free"), sem("ta_free")
        s_full, s_free, m_full, m_free = sem("s_full"), sem("s_free"), sem("m_full"), sem("m_free")
        ze_out, zu_free = sem("ze_out"), sem("zu_free")
        cexp_in, cexp_out, wexp_in, wexp_out, sexp_in, sexp_out, pexp_in, pexp_out = (sem(n) for n in (
            "cexp_in", "cexp_out", "wexp_in", "wexp_out", "sexp_in", "sexp_out", "pexp_in", "pexp_out"))
        p_ready, w_ready, sel_ready, pp_ready = sem("p_ready"), sem("w_ready"), sem("sel_ready"), sem("pp_ready")
        x1_back = sem("x1_back")
        ots_out, xst_out, y_full, y_free = sem("ots_out"), sem("xst_out"), sem("y_full"), sem("y_free")
        y_stored = [sem("y_stored0"), sem("y_stored1")]

        U_MIX, U_KV, U_QUERY, U_OUT = 64, 80, 104, 120
        G_Z = U_OUT * HALF
        ZG = 3 * KT // GK
        G_OUT = G_Z + B * ZG
        HDALL = H * HD

        def wload(sp, w, half, col, use, n):
            col = sp.snap(col)
            for q in range(2):
                s, row = (2 * n + q) % WS, (2 * half + q) * D // 4
                sp.wait_ge(split_out, use * HALF + GPS * (q + 1))
                sp.sem_inc(w_asked, 1)
                sp.dma_start(slot[s], w[row:row + D // 4, bass.ds(col, UNIT)]
                             .rearrange("(k p) c -> p k c", p=P)).then_inc(w_full[s], 16)

        def empty_t(eng, copy, n, i):
            kind, c, g = T_USES[n]
            bank, free = 4 + n % 2, (td_free, ta_free)[n % 2]
            if kind == "keys":
                eng.wait_ge(*((s_full, i * NSU + c) if c else (m_full, i * NMU + 1)))
            eng.wait_ge(t_full, i * NTU + n + 1)
            four = ps[:, bank, :].rearrange("p (a q) -> p a q", a=4)
            if kind == "keys":
                ins = copy(KTb[:, g, :], ps[:, bank, :])
            elif kind in ("probs_win", "probs_sel"):
                ins = copy(PT[c % 2], four)
            elif kind == "probs_new":
                ins = copy(PTn[0:NS, 0, :], ps[0:NS, bank, 0:P])
            elif kind == "prompt":
                ins = copy(Pp[:, :, c * P:(c + 1) * P], four)
            else:
                ins = copy(pcTp[0:PBK], ps[0:PBK, bank, :].rearrange("p (t q) -> p t q", t=2))
            ins.then_inc(free, 1)

        NORM_A, MIXED, NORM_KV, NORM_B, GATED = range(1, 6)
        RAWS = (NORM_A, NORM_KV, NORM_B)
        quarter = lambda q: slice(4 * q, 4 * q + 4)

        def normed(buf):
            return lambda q: [((slice(None), quarter(q)), buf[q % len(buf)])]

        def mixed(q):
            return [((slice(None), quarter(q)), yT[:, quarter(q)])]

        def gated(q):
            return [((slice(None), quarter(q), slice(0, NP)), qP[:, quarter(q)]),
                    ((slice(None), quarter(q), slice(NP, NT)), oTs[:, quarter(q)])]

        N_CONSTS = 14 + P // (BLK // TPP)

        block = ctx.enter_context(nc.Block())

        @block.sync
        def _(sp):
            for tt, (t0, n) in enumerate(TOK[:2]):
                sp.dma_start(xin[:, tt, :], x_prompt[0, t0:t0 + n, :]).then_inc(x_in, 16)
            sp.dma_start(xin[0:NS, 2, :], x_sample.rearrange("b t d -> (b t) d")).then_inc(x_in, 16)
            sp.dma_start(ident[:], consts["ident"]).then_inc(x_in, 16)
            sp.dma_start(vecs[0:16, :], g_a.rearrange("l (k p) -> (l k) p", p=P)).then_inc(misc_in, 16)
            sp.dma_start(vecs[16:32, :], g_kv.rearrange("(k p) -> k p", p=P)).then_inc(misc_in, 16)
            sp.dma_start(vecs[32:48, :], g_b.rearrange("l (k p) -> (l k) p", p=P)).then_inc(misc_in, 16)
            sp.dma_start(vecs[48:96, :], conv_w.rearrange("l w (k p) -> (l w k) p", p=P)).then_inc(misc_in, 16)
            sp.dma_start(vecs[96:99, :], g_k).then_inc(misc_in, 16)
            sp.dma_start(vecs[99:100, :], g_q).then_inc(misc_in, 16)
            sp.dma_start(stin[0:2 * B, :], state_conv.rearrange("l b w d -> (l b w) d")).then_inc(misc_in, 16)
            for t, name in ((ones, "ones"), (group, "group"), (causal, "causal"), (cosT, "cosT"), (sinT, "sinT"),
                            (newmask, "newmask"), (winmask, "winmask"), (trif, "tri"), (pcmask, "pcmask"), (pckeep, "pckeep"),
                            (inblk, "inblk")):
                sp.dma_start(t[:] if t is not trif else t, consts[name]).then_inc(consts_in, 16)
            sp.dma_start(ptab[0:1, :], page_table.rearrange("(o b) n -> o (b n)", o=1)).then_inc(consts_in, 16)
            for lo in (0, BLK):
                sp.dma_start(csb[lo:lo + BLK, 0, 0:2 * G], w_cmp.rearrange("l c g -> l (c g)")).then_inc(consts_in, 16)
            for lo in range(0, P, BLK // TPP):
                sp.dma_start(wc[lo:lo + BLK // TPP].rearrange("p t c -> p (t c)"), w_cmp.rearrange("(p t) c g -> p (t c g)", t=TPP)).then_inc(consts_in, 16)
            sp.wait_ge(consts_in, 16 * N_CONSTS)

            def conv_step(i, first):
                for n in range(8):
                    quarter, half = (1, 2, 3, 0)[n // 2], n % 2
                    wload(sp, w_in_a[0], half, i * UNIT + quarter * D, i * 8 + n, n)
                    if first and n == 0:
                        sp.wait_ge(tp_full, KT)
                    if n % 2 == 0:
                        q, rows = n // 2, P // CPG
                        for k in range(CPG):
                            page = sp.value_load(ptab[0:1, bass.ds(i * NPG + q * CPG + k, 1)], min_val=0, max_val=cache_kv.shape[0] - 1)
                            if k == 0:
                                sp.wait_ge(pg_used, i * GPSQ + q + 1)
                            sp.dma_start(pg[q % CS][k * rows:(k + 1) * rows], cache_kv[bass.ds(page, 1), :, 0:2].rearrange(
                                "o (l t) c g d -> (o l) t (c g d)", t=TPP)).then_inc(pg_full[q % CS], 16)

            conv_step(0, True)
            with sp.Fori(1, B) as i:
                conv_step(i, False)
            with sp.Fori(0, 2) as i:
                for n in range(8):
                    wload(sp, w_out_a[0], n % 2, i * (4 * UNIT) + n // 2 * UNIT, i * 8 + U_MIX + n, n)

            def window_copy(b):
                sp.dma_start(win_s[bass.ds(b, 1), 0:WIN - T].rearrange("o l c g d -> o (l c g d)"),
                             state_win[bass.ds(b, 1), T:WIN].rearrange("o l c g d -> o (l c g d)")).then_inc(wcopy, 16)

            with sp.Fori(0, 3) as i:
                for n in range(8):
                    wload(sp, w_kv, n % 2, i * (8 * HD) + n // 2 * UNIT, i * 8 + U_KV + n, n)
                    if n % 4 == 3:
                        window_copy(i * 2 + n // 4)
            with sp.Fori(0, 2) as i:
                for n in range(8):
                    wload(sp, w_qz[0], n % 2, i * (4 * UNIT) + n // 2 * UNIT, i * 8 + U_QUERY + n, n)
                window_copy(i + 6)

            def zload(i, use):
                u, kk, s = use // 8, use % 8, use % ZS
                col = sp.snap(i * UNIT + (1 + u) * HDALL)
                sp.wait_ge(split_out, i * ZG + (G_Z + WS * GPS - ZS + use + 1))
                sp.dma_start(zslot[s], w_qz[0, kk * GK * P:(kk + 1) * GK * P, bass.ds(col, UNIT)]
                             .rearrange("(k p) c -> p k c", p=P)).then_inc(z_full[s], 16)

            def vload(i, use, first, window, chunk, part, which):
                s = use % VS
                if first and s == 0:
                    sp.wait_ge(split_out, WS * GPS + G_Z)
                srcs = []
                for k in range(2):
                    j = 4 * chunk + 2 * part + k
                    if window:
                        src = state_win[bass.ds(i, 1), j * P:(j + 1) * P, which].rearrange("o l g d -> (o l) (g d)")
                    else:
                        page = sp.value_load(ptab[0:1, bass.ds(i * NPG + j, 1)], min_val=0, max_val=cache_kv.shape[0] - 1)
                        src = cache_kv[bass.ds(page, 1), :, 2 + which].rearrange("o l g d -> (o l) (g d)")
                    srcs.append(src)
                sp.wait_ge(v_used, i * V_USES + use + 1)
                for k in range(2):
                    sp.dma_start(vslot[s][:, k, :], srcs[k]).then_inc(v_full[s], 16)

            def gload(i, u):
                row = sp.snap(i * 2 + u * H)
                sp.wait_ge(gb_used, i * 3 + (1 if u == 2 else 0))
                sp.dma_start(gbc[u % 2], gates_dram[bass.ds(row, 2), :].rearrange("(o h) t -> o h t", o=1)
                             .to_broadcast([P, 2, NT])).then_inc(gb_full[u % 2], 16)

            def main_step(i, first):
                for c in range(CHUNKS):
                    for part in range(2):
                        vload(i, KEY_USE[c] + part, first, c == 0, max(c - 1, 0), part, 0)
                        zload(i, 4 * c + 2 * part)
                        zload(i, 4 * c + 2 * part + 1)
                    if c == 1:
                        for part in range(2):
                            vload(i, VWIN_USE + part, first, True, 0, part, 1)
                    if c == 2:
                        if first:
                            sp.wait_ge(gates_out, 16)
                        gload(i, 0)
                    if c == 3:
                        gload(i, 1)
                for n in range(8):
                    if n < 4:
                        zload(i, 20 + n)
                    if n == 4:
                        gload(i, 2)
                    vload(i, VSEL_USE + n, False, False, n // 2, n % 2, 1)

            main_step(0, True)
            with sp.Fori(1, B) as i:
                main_step(i, False)

            def out_load(i, n, first):
                if first and n == 0:
                    sp.wait_ge(m_full, B * NMU + 1)
                if first and n == 1:
                    sp.wait_ge(ots_out, 1)
                    sp.dma_start(xT, x1_dram.rearrange("p (k t) -> p k t", k=KT)).then_inc(x1_back, 16)
                for q in range(2):
                    s, row, col = (2 * n + q) % WS, (2 * (n % 2) + q) * D // 4, i * 4 * UNIT + n // 2 * UNIT
                    sp.wait_ge(split_out, G_OUT + (i * 8 + n) * HALF + GPS * (q + 1))
                    sp.dma_start(slot[s], w_out_b[0, row:row + D // 4, col:col + UNIT]
                                 .rearrange("(k p) c -> p k c", p=P)).then_inc(w_full[s], 16)

            for i in range(2):
                for n in range(8):
                    out_load(i, n, i == 0)
            sp.wait_ge(wcopy, 16 * B)
            sp.wait_ge(cs_store, 32)
            sp.wait_ge(x1_store, 16)
            sp.wait_ge(kv_store, 16 * 12)
            for q in y_stored:
                sp.wait_ge(q, 32 * 4)

        @block.gpsimd
        def _(pool):
            pool.sem_inc(split_out, WS * GPS)
            pool.sem_inc(w_used, HS)
            pool.sem_inc(pg_used, CS)
            pool.sem_inc(x1_out, 2)
            pool.sem_inc(sqr_out, 2)
            pool.sem_inc(kt_out, 3)
            pool.sem_inc(v_used, VS)
            pool.sem_inc(td_free, 1)
            pool.sem_inc(ta_free, 1)
            pool.sem_inc(s_free, 1)
            pool.sem_inc(m_free, 1)
            pool.sem_inc(y_free, 2)
            for count in (zc_used, b_used, kc_out, vc_out, vt_out, zu_free, m_full, kcp_out, kt_full, h_used, y_out, rope_out):
                pool.sem_inc(count, 1)
            nc.gpsimd.memset(w2[:], 0.0).then_inc(w2_zero, 1)

            def rest_of(g, raw, h):
                pool.wait_ge(hi_out, g + 1)
                nc.gpsimd.tensor_tensor(w_lo[:, h], raw, as_f32(w_hi[:, h]), ALU.subtract).then_inc(split_out, 1)

            def split(g, raw, h):
                pool.wait_ge(w_used, g + 1)
                pool.sem_inc(w_asked, 1)
                nc.gpsimd.tensor_scalar(w_hi[:, h], raw, 1.0, 0.0, ALU.mult, ALU.add).then_inc(hi_out, 1)
                rest_of(g, raw, h)

            with pool.Fori(0, G_Z // (WS * GPS)) as j:
                for g in range(WS * GPS):
                    rest_of(j * (WS * GPS) + g, slot[g // GPS][:, g % GPS * GK:(g % GPS + 1) * GK, :], g % HS)

            def zsplit(i, n):
                pool.wait_ge(z_full[n % ZS], i * (16 * ZG // ZS) + 16 * (n // ZS + 1))
                split(i * ZG + (G_Z + n), zslot[n % ZS], n % HS)

            def stage_sample(i):
                nc.gpsimd.tensor_copy(qSb, qS[:, bass.ds(i, 1), :].rearrange("p o c -> p (o c)")).then_inc(st_sample, 1)
                nc.gpsimd.tensor_copy(vcst, vcT[:, bass.ds(i, 1)].rearrange("p o g n -> p (o g) n")).then_inc(st_sample, 1)
                nc.gpsimd.tensor_copy(kcst, kcT[:, bass.ds(i, 1)].rearrange("p o g n -> p (o g) n")).then_inc(st_sample, 1)

            def step(i, more):
                pool.wait_ge(m_full, i * NMU + 1)
                nc.gpsimd.tensor_copy(qst, qP[:, bass.ds(i * 2, 2), :]).then_inc(st_prompt, 1)
                for br in range(2):
                    nc.gpsimd.tensor_copy(vst[:, br], vts[:, br, 0:2, bass.ds(i // 2 * HD, HD)]).then_inc(st_prompt, 1)
                nc.gpsimd.tensor_copy(pvst[0:PBK, :], pcV[0:PBK, bass.ds(i // 2, 1), :].rearrange("p o d -> p (o d)")).then_inc(st_prompt, 1)
                for n in range(HS, 20):
                    zsplit(i, n)
                if more:
                    pool.wait_ge(s_full, i * NSU + CHUNKS)
                    stage_sample(i + 1)
                for n in range(20, ZG + (HS if more else 0)):
                    zsplit(i, n)

            pool.wait_ge(g_full, 1)
            for n in range(HS):
                zsplit(0, n)
            pool.wait_ge(rope_out, 15)
            pool.wait_ge(vts_out, 2)
            pool.wait_ge(pv_out, 1)
            pool.wait_ge(gd_out, 1)
            pool.wait_ge(gates_out, 16)
            pool.wait_ge(x1_store, 16)
            stage_sample(0)
            with pool.Fori(0, B - 1) as i:
                step(i, True)
            step(B - 1, False)
            for n in range(8):
                for g in range(2 * HALF * n, 2 * HALF * (n + 1)):
                    m = g // GPS % WS
                    if g % GPS == 0:
                        pool.wait_ge(w_full[m], 16 * ((G_Z + g) // (WS * GPS) + 1))
                    split(G_OUT + g, slot[m][:, g % GPS * GK:(g % GPS + 1) * GK, :], g % HS)
                if n == 0:
                    pool.wait_ge(x1_back, 16)
                pool.wait_ge(y_free, n + 1)
                nc.gpsimd.tensor_copy(xst[n % 2], xT[:, 2 * n:2 * n + 2, :]).then_inc(xst_out, 1)

        @block.tensor
        def _(pe):
            def mm(out, lhsT, rhs, start=True, stop=True, **kw):
                return nc.tensor.matmul(out, lhsT, rhs, start=start, stop=stop, **kw)

            def tr(out, in_):
                n = in_.shape[0]
                return nc.tensor.transpose(out, in_, ident[0:n, 0:n])

            pe.wait_ge(x_in, 64)
            for kt in range(KT):
                if kt >= 8:
                    pe.wait_ge((tpd_free, tpa_free)[kt % 2], (kt - 8) // 2 + 1)
                for tt, (t0, n) in enumerate(TOK):
                    last = tr(ps[:, kt % 8, t0:t0 + n], xin[0:n, tt, kt * P:(kt + 1) * P])
                last.then_inc(tp_full, 1)
            pe.wait_ge(misc_in, 16 * 7)
            pe.wait_ge(tpd_free, 8)
            pe.wait_ge(tpa_free, 8)
            tr(ps[:, 0, 0:100], vecs[0:100, :]).then_inc(vec_full, 1)
            for kt in range(KT):
                last = tr(ps[:, 1, kt * 2 * B:(kt + 1) * 2 * B], stin[0:2 * B, kt * P:(kt + 1) * P])
            last.then_inc(vec_full, 1)
            pe.wait_ge(consts_in, 16 * N_CONSTS)
            pe.wait_ge(sum_out, 1)
            mm(ps[:, 2, 0:NT], ones[:], ssum).then_inc(sum_full, 1)
            pe.wait_ge(var_out, 1)
            pe.wait_ge(vec_out, 2)

            def products(out, w, x, start, stop):
                (wh, wl), (xh, xl) = w, x
                mm(out, wh, xh, start=start, stop=False, skip_group_check=True)
                mm(out, wh, xl, start=False, stop=False, skip_group_check=True)
                return mm(out, wl, xh, start=False, stop=stop, skip_group_check=True)

            def granule(g, k, c):
                return w_hi[:, g % HS, k, c], w_lo[:, g % HS, k, c]

            def split_wait(g):
                pe.wait_ge(split_out, g + (WS * GPS + 1))

            def half_unit(g0, bank, half, filled=0):
                for g in range(HALF):
                    split_wait(g0 + g)
                    if filled and g % 2 == 0:
                        pe.wait_ge(hn_out, 4 * (filled - 1) + 2 * half + g // 2 + 1)
                    for t in range(2):
                        for k in range(GK):
                            kt = half * 8 + g * GK + k
                            last = products(ps[:, bank + t, 0:NT], granule(g, k, slice(t * P, (t + 1) * P)),
                                            (hn_hi[:, kt, :], hn_lo[:, kt, :]), kt == 0, kt == KT - 1)
                    last.then_inc(w_used, 1)

            pe.wait_ge(w2_done, 2)
            with pe.Fori(0, B) as i:
                for n in range(8):
                    u, half = n // 2, n % 2
                    if half == 0:
                        if u == 0:
                            pe.wait_ge(zc_used, i + 1)
                        if u == 1:
                            pe.wait_ge(b_used, i + 1)
                        if u == 2:
                            pe.wait_ge(c_out, i + 1)
                        if u == 3:
                            pe.wait_ge(h_used, i + 1 + 1)
                    half_unit(i * 32 + n * HALF, 2 * (u % 2), half, NORM_A if u == 0 else 0)
                    if half == 1:
                        q, nb = u, CPG * PAGE // BLK
                        if q == 0:
                            pe.wait_ge(kc_out, i + 1)
                            pe.wait_ge(vc_out, i + 1)
                        pe.wait_ge(pg_summed, i * GPSQ + q + 1)
                        for c in range(2):
                            for g in range(G):
                                last = mm(ps[:, 6 + c, g * NBK + nb * q:g * NBK + nb * (q + 1)],
                                          pg[q % CS][:, 0, (c * G + g) * HD:(c * G + g + 1) * HD], inblk[:])
                        last.then_inc(pg_used, 1)

            pe.wait_ge(y_out, B + 1)
            for n in range(4):
                if n >= 2:
                    pe.wait_ge(cs_out, n - 1)
                for k in range(4):
                    last = tr(ps[0:18, 4 + n % 2, k * P:(k + 1) * P], cso[:, 4 * n + k, :])
                last.then_inc(cs_full, 1)

            with pe.Fori(0, 2) as i:
                for n in range(8):
                    u, half = n // 2, n % 2
                    if half == 0:
                        pe.wait_ge(x1_out, i * 4 + u + 1)
                    half_unit(i * 32 + (U_MIX + n) * HALF, 2 * (u % 2), half, MIXED if u == 0 else 0)
            pe.wait_ge(sum_out, 2)
            mm(ps[:, 4, 0:NT], ones[:], ssum).then_inc(sum_full, 1)
            pe.wait_ge(x1_out, 2 + 8)

            def head_sums(q):
                pe.wait_ge(sqr_out, 2 + q + 1)
                mm(ps[:, 4, 0:NT], ones[:], sq[:, 0, :])
                mm(ps[:, 5, 0:NT], ones[:], sq[:, 1, :]).then_inc(hs_full, 1)

            with pe.Fori(0, 3) as i:
                for n in range(8):
                    half = n % 2
                    if n < 4:
                        if n == 0:
                            pe.wait_ge(vt_out, i * 3 + 1)
                        if n == 2:
                            pe.wait_ge(kt_out, i * 3 + 3)
                        half_unit(i * 32 + (U_KV + n) * HALF, 2 * (n // 2), half, NORM_KV if n < 2 else 0)
                    else:
                        if n == 4:
                            pe.wait_ge(sqr_out, i * 2 + 3)
                        hf = (n - 4) // 2
                        for g in range(HALF):
                            split_wait(i * 32 + ((U_KV + n) * HALF + g))
                            for tt, (t0, nt) in enumerate(TOK):
                                for k in range(GK):
                                    kt = half * 8 + g * GK + k
                                    last = products(ps[0:nt, VT_BANKS[tt], hf * UNIT:(hf + 1) * UNIT],
                                                    (hn_hi[:, kt, t0:t0 + nt], hn_lo[:, kt, t0:t0 + nt]),
                                                    granule(g, k, slice(0, UNIT)), kt == 0, kt == KT - 1)
                            last.then_inc(w_used, 1)
                    if n in (3, 5):
                        head_sums(i * 2 + n // 5)
                    if n == 7:
                        pe.wait_ge(rope_out, i * 2 + 2 + 1)
                        for tt, (t0, nt) in enumerate(TOK):
                            for g in range(G):
                                last = tr(ps[0:nt, KT_BANKS[tt], g * HD:(g + 1) * HD], kro[:, g, t0:t0 + nt])
                            last.then_inc(kt_full, 1)
            pe.wait_ge(kt_out, 3 + 9)
            pe.wait_ge(vt_out, 10)
            for c, src in ((0, kto), (1, vto)):
                for tt in range(2):
                    for g in range(G):
                        last = mm(ps[:, 6 + c, g * PBK + 2 * tt:g * PBK + 2 * tt + 2], src[:, 0, tt, g * HD:(g + 1) * HD], w2[:, c, g, :])
            last.then_inc(pc_full, 1)

            with pe.Fori(0, 2) as i:
                for n in range(8):
                    u, half = n // 2, n % 2
                    if half == 0:
                        pe.wait_ge(sqr_out, i * 4 + 6 + u + 1)
                    half_unit(i * 32 + (U_QUERY + n) * HALF, 2 * (u % 2), half, NORM_B if u == 0 else 0)
                    if half == 0 and u >= 1:
                        head_sums(i * 4 + 6 + u - 1)
                head_sums(i * 4 + 6 + 3)
            pe.wait_ge(pc_out, 2)
            for g in range(G):
                last = tr(ps[0:PBK, 6, g * HD:(g + 1) * HD], pcvT[:, g, :])
            last.then_inc(pv_full, 1)
            pe.wait_ge(wg_out, 2)
            for kt in range(KT):
                last = products(ps[0:GATES, 0, 0:NT], (wg_hi[:, kt, :], wg_lo[:, kt, :]), (hn_hi[:, kt, :], hn_lo[:, kt, :]),
                                kt == 0, kt == KT - 1)
            last.then_inc(g_full, 1)
            pe.wait_ge(ge_out, 1)
            pe.wait_ge(pv_out, 1)
            pe.wait_ge(hv_out, 14)

            with pe.Fori(0, B) as i:
                t_at = [0]

                def t_bank(known_free=False):
                    n = t_at[0]
                    t_at[0] += 1
                    if not known_free:
                        pe.wait_ge((td_free, ta_free)[n % 2], i * (NTU // 2) + n // 2 + 1)
                    return 4 + n % 2

                def t_emptied(kind, c, g):
                    n = T_USES.index((kind, c, g))
                    pe.wait_ge((td_free, ta_free)[n % 2], i * (NTU // 2) + n // 2 + 2)

                def m_bank(n):
                    pe.wait_ge(m_free, i * NMU + n)

                def z_part(part):
                    u, kk = part // 8, part % 8
                    if kk == 0:
                        pe.wait_ge(zu_free, i * 3 + (1 if u == 2 else 0) + 1)
                    split_wait(i * ZG + (G_Z + part))
                    for t in range(2):
                        for k in range(GK):
                            kt = kk * GK + k
                            last = products(ps[:, 2 * (u % 2) + t, 0:NT], granule(part, k, slice(t * P, (t + 1) * P)),
                                            (hn_hi[:, kt, :], hn_lo[:, kt, :]), kt == 0, kt == KT - 1)
                    last.then_inc(w_used, 1)

                def keys(c, g):
                    for h in range(2):
                        use = KEY_USE[c] + h
                        if g == 0:
                            pe.wait_ge(v_full[use % VS], i * (32 * V_USES // VS) + 32 * (use // VS + 1))
                    bank = t_bank()
                    for p in range(4):
                        last = tr(ps[:, bank, p * P:(p + 1) * P], vslot[(KEY_USE[c] + p // 2) % VS][:, p % 2, g * HD:(g + 1) * HD])
                        if g == G - 1 and p == 1:
                            last.then_inc(v_used, 1)
                    last.then_inc(t_full, 1)

                def scores(c):
                    pe.wait_ge(s_free, i * NSU + c + 1)
                    for g in range(G):
                        t_emptied("keys", c, g)
                        last = mm(ps[32 * g:32 * g + 32, 6, :], qSb[:, 32 * g:32 * g + 32], KTb[:, g, :])
                        if g == 0:
                            last.then_inc(v_used, 1)
                    last.then_inc(s_full, 1)

                def pv(use, probs, start):
                    for p in range(4):
                        s = (use + p // 2) % VS
                        if p % 2 == 0:
                            pe.wait_ge(v_full[s], i * (32 * V_USES // VS) + 32 * ((use + p // 2) // VS + 1))
                        for g in range(G):
                            last = mm(ps[:, 7, 32 * g:32 * g + 32], vslot[s][:, p % 2, g * HD:(g + 1) * HD],
                                      probs[:, p, 32 * g:32 * g + 32], start=start and p == 0 and g == 0, stop=False, skip_group_check=True)
                        if p % 2 == 1:
                            last.then_inc(v_used, 1)

                def pv_new(br):
                    for g in range(G):
                        last = mm(ps[:, 7, 32 * g:32 * g + 32], vts[0:NS, br, 2, g * HD:(g + 1) * HD],
                                  PTn[0:NS, br, 32 * g:32 * g + 32], start=False, stop=True, skip_group_check=True)
                    last.then_inc(m_full, 1)

                def prompt_scores(qt, t):
                    pe.wait_ge(s_free, i * NSU + CHUNKS + qt * 2 + t + 1)
                    nk = (qt + 1) * P
                    for br in range(2):
                        last = mm(ps[:, 6, br * 256:br * 256 + nk], qst[:, t, qt * P:(qt + 1) * P],
                                  kTs[:, br, bass.ds(i // 2, 1), 0:nk].rearrange("p o k -> p (o k)"))
                    last.then_inc(s_full, 1)

                pe.wait_ge(st_sample, i * 3 + 3)
                for g in range(G):
                    keys(0, g)
                    z_part(g)
                    if g == 0:
                        m_bank(1)
                        for gg in range(G):
                            q = qSb[:, 32 * gg:32 * gg + 32]
                            mm(ps[32 * gg:32 * gg + 32, 7, 0:NBK], q, kcst[:, gg, :])
                            mm(ps[32 * gg:32 * gg + 32, 7, 64:128], q, kTs[:, 1, gg, NP:NT])
                            last = mm(ps[32 * gg:32 * gg + 32, 7, 128:192], q, kTs[:, 0, gg, NP:NT])
                        last.then_inc(m_full, 1)
                    if g == 1:
                        m_bank(2)
                        pe.wait_ge(p_ready, i + 1)
                        mm(ps[:, 7, 0:NBK], group[:], pcm).then_inc(m_full, 1)
                    if g == 2:
                        m_bank(3)
                        for gg in range(G):
                            last = tr(ps[0:NBK, 7, gg * HD:(gg + 1) * HD], vcst[:, gg, :])
                        last.then_inc(m_full, 1)
                    if g == 3:
                        m_bank(4)
                        tr(ps[0:NBK, 7, 0:P], pcm).then_inc(m_full, 1)
                scores(0)
                m_bank(5)
                for g in range(G):
                    last = mm(ps[:, 7, 32 * g:32 * g + 32], vcb[0:NBK, g * HD:(g + 1) * HD], pcT[0:NBK, 32 * g:32 * g + 32])
                last.then_inc(m_full, 1)
                for g in range(G):
                    keys(1, g)
                    z_part(4 + g)
                scores(1)
                pe.wait_ge(w_ready, i + 1)
                m_bank(6)
                bank = t_bank()
                for p in range(4):
                    last = tr(ps[:, bank, p * P:(p + 1) * P], S[:, p * P:(p + 1) * P])
                last.then_inc(t_full, 1)
                tr(ps[0:NS, 7, 0:P], S[:, WN:WN + NS]).then_inc(m_full, 1)
                for c in range(2, CHUNKS):
                    for g in range(G):
                        keys(c, g)
                        z_part(4 * c + g)
                        if c == 2 and g == 0:
                            m_bank(7)
                            t_emptied("probs_win", 0, 0)
                            pv(VWIN_USE, PT[0], True)
                            pv_new(1)
                    scores(c)
                pe.wait_ge(st_prompt, i * 4 + 4)
                for n in range(4):
                    z_part(20 + n)
                    prompt_scores(n // 2, n % 2)
                m_bank(8)
                for qt in range(2):
                    for t in range(2):
                        last = mm(ps[:, 7, (qt * 2 + t) * PBK:(qt * 2 + t + 1) * PBK], qst[:, t, qt * P:(qt + 1) * P],
                                  pcK[:, bass.ds(i // 2, 1), :].rearrange("p o n -> p (o n)"))
                last.then_inc(m_full, 1)
                pe.wait_ge(sel_ready, i + 1)
                for c in range(5):
                    bank = t_bank(c == 4)
                    if c < 4:
                        for p in range(4):
                            last = tr(ps[:, bank, p * P:(p + 1) * P], S[:, SL + (4 * c + p) * P:SL + (4 * c + p + 1) * P])
                    else:
                        last = tr(ps[0:NS, bank, 0:P], S[:, SN:SN + NS])
                    last.then_inc(t_full, 1)
                    if c == 0:
                        m_bank(9)
                    if c >= 1:
                        t_emptied("probs_sel", c - 1, 0)
                        pv(VSEL_USE + 2 * (c - 1), PT[(c - 1) % 2], c == 1)
                t_emptied("probs_new", 0, 0)
                pv_new(0)
                for c, (kt, qt) in enumerate(((0, 0), (0, 1), (1, 1))):
                    pe.wait_ge(pp_ready, i * 3 + qt + 1)
                    bank = t_bank()
                    for a in range(4):
                        last = tr(ps[:, bank, a * P:(a + 1) * P], Sp[:, qt, a, kt * P:(kt + 1) * P])
                    last.then_inc(t_full, 1)
                pe.wait_ge(pp_ready, i * 3 + 3)
                bank = t_bank()
                for t in range(2):
                    for qt in range(2):
                        last = tr(ps[0:PBK, bank, (t * 2 + qt) * P:(t * 2 + qt + 1) * P], pcs[:, qt * 2 + t, :])
                last.then_inc(t_full, 1)
                for br in range(2):
                    m_bank(10 + br)
                    if br == 0:
                        for c in range(3):
                            t_emptied("prompt", c, 0)
                    for t in range(2):
                        a = 2 * t + br
                        mm(ps[:, 7, t * NP:(t + 1) * NP], vst[:, br, 0, :], Pp[:, a, 0:NP], stop=False, skip_group_check=True)
                        last = mm(ps[:, 7, t * NP + P:(t + 1) * NP], vst[:, br, 1, :], Pp[:, a, NP:NP + P], start=False, skip_group_check=True)
                    last.then_inc(m_full, 1)
                m_bank(12)
                t_emptied("prompt_cmp", 0, 0)
                for t in range(2):
                    last = mm(ps[:, 7, t * NP:(t + 1) * NP], pvst[0:PBK, :], pcTp[0:PBK, t, :])
                last.then_inc(m_full, 1)
                assert t_at[0] == NTU

            pe.wait_ge(m_free, B * NMU + 1)
            with pe.Fori(0, 2) as i:
                for n in range(8):
                    u, half = n // 2, n % 2
                    if half == 0:
                        pe.wait_ge(y_free, i * 4 + u + 1)
                    for g in range(HALF):
                        split_wait(i * 32 + (G_OUT + n * HALF + g))
                        if u == 0 and g % 2 == 0:
                            pe.wait_ge(hn_out, 4 * (GATED - 1) + 2 * half + g // 2 + 1)
                        for tt, (t0, nt) in enumerate(TOK):
                            for k in range(GK):
                                h = half * 8 + g * GK + k
                                last = products(ps[0:nt, 3 * (u % 2) + tt, 0:UNIT],
                                                (hn_hi[:, h, t0:t0 + nt], hn_lo[:, h, t0:t0 + nt]),
                                                granule(g, k, slice(0, UNIT)), h == 0, False)
                        last.then_inc(w_used, 1)
                    if half == 1:
                        pe.wait_ge(xst_out, i * 4 + u + 1)
                        for tt, (t0, nt) in enumerate(TOK):
                            for j in range(2):
                                last = mm(ps[0:nt, 3 * (u % 2) + tt, j * P:(j + 1) * P], xst[u % 2][:, j, t0:t0 + nt], ident[:],
                                          start=False, stop=True, skip_group_check=True)
                        last.then_inc(y_full, 1)

        @block.vector
        def _(dve):
            v = nc.vector
            link = Chain(dve, dchain)

            v.memset(cpad[:, :, 0:2], 0.0)
            for kt in range(0, KT, 2):
                dve.wait_ge(tp_full, kt + 1)
                v.tensor_copy(xT[:, kt, :], ps[:, kt % 8, 0:NT]).then_inc(tpd_free, 1)
            dve.wait_ge(consts_in, 16 * N_CONSTS)
            dve.wait_ge(w2_zero, 1)
            for n, lo in enumerate((0, BLK)):
                v.tensor_copy(w2[lo:lo + BLK, :, :, n].rearrange("p c g -> p (c g)"), csb[lo:lo + BLK, 0, 0:2 * G]).then_inc(w2_done, 1)
            v.tensor_copy(tri[:], trif).then_inc(consts_used, 1)
            dve.wait_ge(vec_full, 1)
            v.tensor_copy(vecT[:], ps[:, 0, 0:100]).then_inc(vec_out, 1)
            dve.wait_ge(vec_full, 2)
            v.tensor_copy(stT.rearrange("p k c -> p (k c)"), ps[:, 1, 0:2 * B * KT]).then_inc(vec_out, 1)

            def rest(q, n, src):
                dve.wait_ge(hn_hid, 4 * (n - 1) + q + 1)
                for d, x in src(q):
                    ins = v.tensor_tensor(hn_lo[d], x, as_f32(hn_hi[d]), ALU.subtract)
                ins.then_inc(hn_out, 1)

            def scale_rows(n, gcol, buf):
                for q in range(4):
                    nq = len(buf)
                    if q >= nq:
                        rest(q - nq, n, normed(buf))
                        dve.wait_ge(hn_out, 4 * (n - 1) + q - nq + 1)
                    for kt in range(4 * q, 4 * q + 4):
                        ins = v.scalar_tensor_tensor(out=buf[q % nq][:, kt % 4, :], in0=xT[:, kt, :],
                                                     scalar=vecT[:, gcol + kt:gcol + kt + 1], in1=rstd, op0=ALU.mult, op1=ALU.mult)
                    ins.then_inc(hn_raw, 1)
                for q in range(4 - nq, 4):
                    rest(q, n, normed(buf))

            def norm(n, bank, gcol, filling):
                dve.wait_ge(sq_out, n)
                v.tensor_reduce(ssum, xsq.rearrange("p k t -> p t k"), AX.X, ALU.add).then_inc(sum_out, 1)
                dve.wait_ge(sum_full, n)
                v.tensor_scalar(rstd, ps[:, bank, 0:NT], 1.0 / D, EPS, ALU.mult, ALU.add).then_inc(var_out, 1)
                dve.wait_ge(sd_out, n)
                link(v.reciprocal(rstd, rstd))
                scale_rows(filling, gcol, hnf)

            norm(1, 2, 0, NORM_A)

            with dve.Fori(0, B) as i:
                link.enter(i, 14)

                def group(q):
                    pages = pg[q % CS]
                    dve.wait_ge(pg_full[q % CS], i * (16 * CPG * GPSQ // CS) + 16 * CPG * (q // CS + 1))
                    x = pages.rearrange("p t (c d) -> p (t c) d", d=HD)
                    link(v.tensor_tensor(x, x, wc[:].rearrange("p t c -> p (t c)").unsqueeze(2).to_broadcast([P, TPP * 2 * G, HD]), ALU.mult))
                    link(v.tensor_tensor(pages[:, 0:2], pages[:, 0:2], pages[:, 2:4], ALU.add))
                    v.tensor_tensor(pages[:, 0], pages[:, 0], pages[:, 1], ALU.add).then_inc(pg_summed, 1)

                group(0)
                group(1)
                done = lambda u: dve.wait_ge(w_used, (i * 8 + (1 + 2 * u + 2)) * HALF)
                done(1)
                dve.wait_ge(c_out, i + 1)
                v.tensor_tensor(cpad[:, :, 2:], csb[:, :, 0:NP], ps[:, 2:4, 0:NP], ALU.mult)
                for t in range(2):
                    ins = v.tensor_tensor(spad[:, t, :, 2:], csb[:, t, NP:NT].rearrange("p (b s) -> p b s", b=B),
                                          ps[:, 2 + t, NP:NT].rearrange("p (b s) -> p b s", b=B), ALU.mult)
                ins.then_inc(h_used, 1)
                for t in range(2):
                    ins = v.tensor_copy(spad[:, t, :, 0:2], stT[:, bass.ds(i * 2 + t, 1), :].rearrange("p o (b w) -> p (o b) w", w=2))
                link(ins)
                v.tensor_copy(cso[:, bass.ds(i * 2, 2), 0:2], cpad[:, :, NP:NP + 2])
                for t in range(2):
                    v.tensor_copy(cso[:, bass.ds(i * 2 + t, 1), 2:].rearrange("p o (b w) -> p (o b) w", w=2), spad[:, t, :, T:T + 2])
                for w in range(3):
                    for t in range(2):
                        tap = vecT[:, bass.ds(i * 2 + (48 + w * KT + t), 1)]
                        for o, a in ((bc[:, t, 0:NP], cpad[:, t, w:w + NP]),
                                     (bc[:, t, NP:NT].rearrange("p (b s) -> p b s", b=B), spad[:, t, :, w:w + T])):
                            if w == 0:
                                ins = v.tensor_scalar(o, a, tap, None, ALU.mult)
                            else:
                                ins = v.scalar_tensor_tensor(out=o, in0=a, scalar=tap, in1=o, op0=ALU.mult, op1=ALU.add)
                    link(ins)
                group(2)
                done(2)
                dve.wait_ge(e_out, i + 1)
                link(v.tensor_scalar(ez, ez, 1.0, None, ALU.add))
                link(v.reciprocal(ez, ez))
                ins = v.tensor_tensor(ez, ez, ps[:, 0:2, 0:NT], ALU.mult)
                ins.then_inc(zc_used, 1)
                group(3)
                done(3)
                ins = v.tensor_tensor(bc, bc, ps[:, 2:4, 0:NT], ALU.mult)
                ins.then_inc(b_used, 1)
                dve.wait_ge(b_used, i + 1 + 1)
                dve.wait_ge(zc_used, i + 1 + 1)
                v.tensor_tensor(yT[:, bass.ds(i * 2, 2), :], bc, ez, ALU.mult).then_inc(y_out, 1)
                dve.wait_ge(pg_used, i * GPSQ + (CS + GPSQ))
                v.tensor_copy(kcT[:, bass.ds(i, 1)].rearrange("p o g n -> p (o g n)"), ps[:, 6, 0:G * NBK]).then_inc(kc_out, 1)
            link.leave(B)

            for q in range(4):
                rest(q, MIXED, mixed)
            with dve.Fori(0, 2) as i:
                for u in range(4):
                    dve.wait_ge(w_used, (i * 8 + (1 + U_MIX + 2 * u + 2)) * HALF)
                    x = xT[:, bass.ds(i * 8 + 2 * u, 2), :]
                    v.tensor_tensor(x, x, ps[:, 2 * (u % 2):2 * (u % 2) + 2, 0:NT], ALU.add).then_inc(x1_out, 1)
            norm(2, 4, KT, NORM_KV)

            def head_norm(q, gain, outs_, before):
                dve.wait_ge(hs_full, q + 1)
                v.tensor_scalar(rs, ps[:, 4:6, 0:NT], 1.0 / HD, EPS, ALU.mult, ALU.add).then_inc(hv_out, 1)
                dve.wait_ge(hsd_out, q + 1)
                link(v.reciprocal(rs, rs))
                link(v.scalar_tensor_tensor(out=kn, in0=raw, scalar=gain, in1=rs, op0=ALU.mult, op1=ALU.mult))
                two = lambda a: a.unsqueeze(1).to_broadcast([a.shape[0], 2, NT])
                v.tensor_tensor(ra, kn, two(cosT[:]), ALU.mult)
                v.tensor_tensor(sq[0:64], kn[64:128], two(sinT[64:128]), ALU.mult)
                link(v.tensor_tensor(sq[64:128], kn[0:64], two(sinT[0:64]), ALU.mult))
                before()
                for o, sel in outs_[:-1]:
                    v.tensor_tensor(o, sel(ra), sel(sq), ALU.add)
                o, sel = outs_[-1]
                v.tensor_tensor(o, sel(ra), sel(sq), ALU.add).then_inc(rope_out, 1)

            with dve.Fori(0, 3) as i:
                link.enter(i, 6)
                for gp in range(2):
                    def before(gp=gp):
                        if gp == 0:
                            dve.wait_ge(kcp_out, i + 1)
                            dve.wait_ge(kt_full, i * 3 + 1)
                    head_norm(i * 2 + gp, vecT[:, bass.ds(i + 96, 1)], [(kro[:, 2 * gp:2 * gp + 2, :], lambda a: a)], before)
                dve.wait_ge(w_used, (i * 8 + (1 + U_KV + 8)) * HALF)
                for tt, (t0, nt) in enumerate(TOK):
                    v.tensor_copy(vto[0:nt, bass.ds(i, 1), tt, :].rearrange("p o c -> p (o c)"), ps[0:nt, VT_BANKS[tt], :]).then_inc(vt_out, 1)
            link.leave(3)
            dve.wait_ge(rope_out, 7)
            scale_rows(NORM_B, 2 * KT, hnf_b)
            dve.wait_ge(pc_full, 1)
            v.tensor_copy(pcK.rearrange("p g n -> p (g n)"), ps[:, 6, 0:G * PBK]).then_inc(pc_out, 1)
            v.tensor_copy(pcvT[:].rearrange("p g n -> p (g n)"), ps[:, 7, 0:G * PBK]).then_inc(pc_out, 1)

            with dve.Fori(0, 2) as i:
                link.enter(i, 12)
                for u in range(4):
                    h = i * 8 + 2 * u
                    outs_ = [(qP[:, bass.ds(h, 2), :], lambda a: a[:, :, 0:NP])]
                    for t in range(2):
                        outs_.append((qS[:, :, bass.ds((h + t) * T, T)],
                                      lambda a, t=t: a[:, t, NP:NT].rearrange("p (b s) -> p b s", b=B)))
                    head_norm(i * 4 + 6 + u, vecT[:, 99:100], outs_, lambda: None)
            link.leave(2)
            dve.wait_ge(wg_out, 1)
            v.tensor_tensor(wg_lo, wgt, as_f32(wg_hi), ALU.subtract).then_inc(wg_out, 1)
            dve.wait_ge(pv_full, 1)
            v.tensor_copy(pcV.rearrange("p g d -> p (g d)")[0:PBK], ps[0:PBK, 6, :]).then_inc(pv_out, 1)
            dve.wait_ge(ge_out, 1)
            v.tensor_scalar(gd[0:GATES], gd[0:GATES], 1.0, None, ALU.add).then_inc(gd_out, 1)
            dve.wait_ge(gates_out, 16)
            dve.wait_ge(kv_store, 16 * 12)
            dve.wait_ge(x1_store, 16)
            dve.wait_ge(vts_out, 2)

            PER_MAIN = 24
            with dve.Fori(0, B) as i:
                link.enter(i, PER_MAIN)
                st = lambda a, n=1: stat[:, a:a + n]

                def m_copy(n, out, in_):
                    dve.wait_ge(m_full, i * NMU + n + 1)
                    v.tensor_copy(out, in_).then_inc(m_free, 1)
                    dve.wait_ge(m_free, i * NMU + n + 1)

                def negmax(a, src):
                    link(v.tensor_reduce(st(a), src, AX.X, ALU.max, negate=True))
                    return v.tensor_scalar(st(a), st(a), SCALE, None, ALU.mult)

                def normalise(a, probs):
                    link(v.reciprocal(st(a + 2), st(a + 1)))
                    return v.tensor_scalar(probs, probs, st(a + 2), None, ALU.mult)

                def evens(lo, hi):
                    for n in range(lo, hi):
                        if n % 2 == 0:
                            empty_t(dve, v.tensor_copy, n, i)

                def z_unit(u):
                    dve.wait_ge(ze_out, i * 3 + u + 1)
                    dve.wait_ge(gb_full[u % 2], (i * 32 + 16 * (u // 2 + 1)) if u % 2 == 0 else i * 16 + 16)
                    v.scalar_tensor_tensor(out=ezm, in0=ezm, scalar=1.0, in1=gbc[u % 2], op0=ALU.add, op1=ALU.mult).then_inc(gb_used, 1)
                    dve.wait_ge(gb_used, i * 3 + u + 1)
                    link(v.reciprocal(ezm, ezm))
                    bank = 2 * (u % 2)
                    v.tensor_tensor(zgP[:, u], ezm[:, :, 0:NP], ps[:, bank:bank + 2, 0:NP], ALU.mult)
                    v.tensor_tensor(zS[:, u, bass.ds(i * 2, 2), :], ezm[:, :, NP:NT], ps[:, bank:bank + 2, NP:NT], ALU.mult).then_inc(zu_free, 1)

                def s_wait(n):
                    dve.wait_ge(s_full, i * NSU + n + 1)

                def sel_scores(c):
                    s_wait(c)
                    lo = 8 * (c - 1)
                    v.tensor_tensor(S[:, SL + lo * BLK:SL + (lo + 8) * BLK].rearrange("p (n l) -> p n l", l=BLK),
                                    ps[:, 6, :].rearrange("p (n l) -> p n l", l=BLK),
                                    bmask[:, lo:lo + 8].unsqueeze(2).to_broadcast([P, 8, BLK]), ALU.add).then_inc(s_free, 1)

                evens(0, 1)
                m_copy(1, msb, ps[:, 7, 0:192])
                nm = newmask[:, bass.ds(i, 1), :].rearrange("p o s -> p (o s)")
                v.tensor_tensor(S[:, WN:WN + NS], msb[:, 64:128], nm, ALU.add)
                v.tensor_tensor(S[:, SN:SN + NS], msb[:, 128:192], nm, ALU.add)
                negmax(0, msb[:, 0:NBK]).then_inc(cexp_in, 1)
                dve.wait_ge(cexp_out, i + 1)
                normalise(0, pcm).then_inc(p_ready, 1)
                m_copy(2, psc, ps[:, 7, 0:NBK])
                evens(1, 3)
                m_copy(3, vcb[0:NBK], ps[0:NBK, 7, :])
                m_copy(4, pcT[0:NBK], ps[0:NBK, 7, 0:P])
                s_wait(0)
                v.tensor_tensor(S[:, 0:T], ps[:, 6, 0:T], winmask[:], ALU.add)
                v.tensor_copy(S[:, T:WIN], ps[:, 6, T:WIN]).then_inc(s_free, 1)
                dve.wait_ge(s_free, i * NSU + 2)
                m_copy(5, oS[:, 0, bass.ds(i, 1), :].rearrange("p o c -> p (o c)"), ps[:, 7, 0:H * T])
                negmax(3, S[:, 0:WIN + NS]).then_inc(wexp_in, 1)
                evens(3, 5)
                s_i = psc[:, 1:1 + MID].unsqueeze(1).to_broadcast([P, MID, MID])
                s_j = psc[:, 1:1 + MID].unsqueeze(2).to_broadcast([P, MID, MID])
                v.tensor_tensor(gt, s_i, s_j, ALU.is_gt)
                link(v.tensor_tensor(eq, s_i, s_j, ALU.is_equal))
                link(v.tensor_tensor(eq, eq, tri[:], ALU.mult))
                link(v.tensor_tensor(gt, gt, eq, ALU.add))
                v.memset(bmask[:, 0:1], 0.0)
                v.memset(bmask[:, NBK - 1:NBK], 0.0)
                link(v.tensor_reduce(bmask[:, 1:1 + MID], gt, AX.X, ALU.add))
                link(v.tensor_scalar(bmask[:, 1:1 + MID], bmask[:, 1:1 + MID], float(KEEP), NEG, ALU.is_ge, ALU.mult))
                dve.wait_ge(wexp_out, i + 1)
                normalise(3, S[:, 0:WIN + NS]).then_inc(w_ready, 1)
                evens(5, 8)
                sel_scores(1)
                evens(8, 9)
                m_copy(6, PTn[0:NS, 1, :], ps[0:NS, 7, 0:P])
                m_copy(7, oS[:, 2, bass.ds(i, 1), :].rearrange("p o c -> p (o c)"), ps[:, 7, 0:H * T])
                z_unit(0)
                evens(9, 13)
                sel_scores(2)
                evens(13, 17)
                sel_scores(3)
                z_unit(1)
                evens(17, 21)
                sel_scores(4)
                dve.wait_ge(s_free, i * NSU + CHUNKS + 1)
                negmax(6, S[:, SL:]).then_inc(sexp_in, 1)

                def prompt_scores(qt, t):
                    s_wait(CHUNKS + 2 * qt + t)
                    bank = ps[:, 6, :].rearrange("p (a k) -> p a k", a=2)
                    if qt:
                        v.tensor_copy(Sp[:, qt, 2 * t:2 * t + 2, 0:P], bank[:, :, 0:P])
                    v.tensor_tensor(Sp[:, qt, 2 * t:2 * t + 2, qt * P:(qt + 1) * P], bank[:, :, qt * P:(qt + 1) * P],
                                    causal[:].unsqueeze(1).to_broadcast([P, 2, P]), ALU.add).then_inc(s_free, 1)

                def prompt_max(qt):
                    dve.wait_ge(s_free, i * NSU + CHUNKS + 2 * qt + 3)
                    link(v.tensor_reduce(st(16 + 4 * qt, 4), Sp[:, qt, :, 0:(qt + 1) * P], AX.X, ALU.max, negate=True))
                    v.tensor_scalar(st(16 + 4 * qt, 4), st(16 + 4 * qt, 4), SCALE, None, ALU.mult).then_inc(pexp_in, 1)

                def prompt_scale(qt):
                    dve.wait_ge(pexp_out, i * 3 + qt + 1)
                    link(v.reciprocal(st(32 + 4 * qt, 4), st(24 + 4 * qt, 4)))
                    a = Sp[:, qt, :, 0:(qt + 1) * P]
                    v.tensor_tensor(a, a, st(32 + 4 * qt, 4).unsqueeze(2).to_broadcast([P, 4, (qt + 1) * P]), ALU.mult).then_inc(pp_ready, 1)

                prompt_scores(0, 0)
                prompt_scores(0, 1)
                prompt_max(0)
                dve.wait_ge(sexp_out, i + 1)
                normalise(6, S[:, SL:]).then_inc(sel_ready, 1)
                prompt_scores(1, 0)
                prompt_scores(1, 1)
                prompt_max(1)
                prompt_scale(0)
                z_unit(2)
                dve.wait_ge(m_full, i * NMU + 8 + 1)
                four = lambda a: a.unsqueeze(2).to_broadcast([P, 4, PBK])
                mask = lambda a: a[:].unsqueeze(2).to_broadcast([P, 2, 2, PBK])
                pcs4 = pcs.rearrange("p (q t) n -> p q t n", t=2)
                v.tensor_tensor(pcs4, ps[:, 7, 0:4 * PBK].rearrange("p (q t n) -> p q t n", q=2, t=2), mask(pcmask), ALU.add).then_inc(m_free, 1)
                dve.wait_ge(m_free, i * NMU + 9)
                link(v.tensor_reduce(st(40, 4), pcs, AX.X, ALU.max))
                v.tensor_tensor(pcs, pcs, four(st(40, 4)), ALU.subtract).then_inc(pexp_in, 1)
                prompt_scale(1)
                dve.wait_ge(pexp_out, i * 3 + 3)
                link(v.tensor_reduce(st(44, 4), pcs, AX.X, ALU.add))
                link(v.reciprocal(st(48, 4), st(44, 4)))
                link(v.tensor_tensor(pcs, pcs, four(st(48, 4)), ALU.mult))
                v.tensor_tensor(pcs4, pcs4, mask(pckeep), ALU.mult).then_inc(pp_ready, 1)
                evens(21, 26)
                m_copy(9, oS[:, 1, bass.ds(i, 1), :].rearrange("p o c -> p (o c)"), ps[:, 7, 0:H * T])
                evens(26, NTU)
                o = qP[:, bass.ds(i * 2, 2), :]
                for n, br in ((10, 1), (11, 2), (12, 0)):
                    dve.wait_ge(m_full, i * NMU + n + 1)
                    pso = ps[:, 7, :].rearrange("p (t q) -> p t q", t=2)
                    v.tensor_tensor(o if n == 10 else otmp, zgP[:, br], pso, ALU.mult).then_inc(m_free, 1)
                    dve.wait_ge(m_free, i * NMU + n + 1)
                    if n > 10:
                        link(v.tensor_tensor(o, o, otmp, ALU.add))
            link.leave(B)

            bht = lambda a: a.rearrange("p b (h s) -> p b h s", s=T)
            hbt = lambda a: a.rearrange("p h (b s) -> p b h s", s=T)
            dve.wait_ge(m_full, B * NMU + 1)
            for br in range(3):
                ins = None
                for b in range(B):
                    o3 = hbt(oTs if br == 0 else oadd)[:, b]
                    ins = v.tensor_tensor(o3, bht(oS[:, br])[:, b], hbt(zS[:, br])[:, b], ALU.mult)
                link(ins)
                if br == 1:
                    link(v.tensor_tensor(oTs, oTs, oadd, ALU.add))
            v.tensor_tensor(oTs, oTs, oadd, ALU.add).then_inc(ots_out, 1)
            dve.wait_ge(ots_out, 1)
            for q in range(4):
                rest(q, GATED, gated)

        @block.scalar
        def _(act):
            s = nc.scalar
            link = Chain(act, achain)

            for kt in range(1, KT, 2):
                act.wait_ge(tp_full, kt + 1)
                s.copy(xT[:, kt, :], ps[:, kt % 8, 0:NT]).then_inc(tpa_free, 1)

            def lead_w(i, before, lo, hi):
                for g in range(lo, hi):
                    if g % GPS == 0:
                        act.wait_ge(w_full[g // GPS % WS], i * (16 * 32 // (WS * GPS)) + 16 * ((before + g) // (WS * GPS) + 1))
                    act.wait_ge(w_used, i * 32 + (before + g + 1))
                    s.copy(w_hi[:, g % HS], slot[g // GPS % WS][:, g % GPS * GK:(g % GPS + 1) * GK, :]).then_inc(hi_out, 1)

            def lead(n, src, ready=True):
                for q in range(4):
                    if not ready:
                        act.wait_ge(hn_raw, 4 * RAWS.index(n) + q + 1)
                    for d, x in src(q):
                        ins = s.copy(hn_hi[d], x)
                    ins.then_inc(hn_hid, 1)

            def norm(n):
                s.activation(xsq, xT, ACT.Square).then_inc(sq_out, 1)
                if n == 1:
                    lead_w(0, 0, 0, HS)
                act.wait_ge(var_out, n)
                s.activation(rstd, rstd, ACT.Sqrt).then_inc(sd_out, 1)

            act.wait_ge(tpd_free, 8)
            act.wait_ge(tpa_free, 8)
            act.wait_ge(vec_out, 2)
            act.wait_ge(consts_used, 1)
            norm(1)
            lead(NORM_A, normed(hnf), False)
            act.wait_ge(w2_done, 2)

            with act.Fori(0, B) as i:
                lead_w(i, 0, HS, 12)
                act.wait_ge(w_used, (i * 8 + (1 + 2)) * HALF)
                act.wait_ge(h_used, i + 1)
                s.copy(csb, ps[:, 0:2, 0:NT]).then_inc(c_out, 1)
                lead_w(i, 0, 12, 28)
                act.wait_ge(w_used, (i * 8 + (1 + 6)) * HALF)
                act.wait_ge(y_out, i + 1)
                s.activation(ez, ps[:, 0:2, 0:NT], ACT.Exp, scale=-1.0).then_inc(e_out, 1)
                lead_w(i, 0, 28, 32 + HS)
                act.wait_ge(pg_used, i * GPSQ + (CS + GPSQ))
                s.copy(vcT[:, bass.ds(i, 1)].rearrange("p o g n -> p (o g n)"), ps[:, 7, 0:G * NBK]).then_inc(vc_out, 1)
            for n in range(4):
                act.wait_ge(cs_full, n + 1)
                s.copy(crow[0:18, n * 512:(n + 1) * 512], ps[0:18, 4 + n % 2, :]).then_inc(cs_out, 1)
            act.wait_ge(cs_out, 4)
            act.dma_start(conv_p.rearrange("l b w d -> (l b w) d"), crow[0:2, :]).then_inc(cs_store, 16)
            act.dma_start(conv_s.rearrange("l b w d -> (l b w) d"), crow[2:18, :]).then_inc(cs_store, 16)

            act.wait_ge(y_out, B + 1)
            act.wait_ge(w_used, HS + U_MIX * HALF)
            lead(MIXED, mixed)
            with act.Fori(0, 2) as i:
                lead_w(i, U_MIX * HALF, HS, 32 + HS)
            act.wait_ge(cs_store, 32)
            act.wait_ge(x1_out, 2 + 8)
            norm(2)
            lead(NORM_KV, normed(hnf), False)
            act.dma_start(x1_dram.rearrange("p (k t) -> p k t", k=KT), xT).then_inc(x1_store, 16)

            def squares(q, use, bank):
                act.wait_ge(w_used, use * HALF)
                act.wait_ge(rope_out, q + 1)
                s.copy(raw, ps[:, bank:bank + 2, 0:NT])
                s.activation(sq, ps[:, bank:bank + 2, 0:NT], ACT.Square).then_inc(sqr_out, 1)

            def root(q):
                act.wait_ge(hv_out, q + 1)
                s.activation(rs, rs, ACT.Sqrt).then_inc(hsd_out, 1)

            with act.Fori(0, 3) as i:
                at = U_KV * HALF
                lead_w(i, at, HS, 12)
                squares(i * 2, i * 8 + (1 + U_KV + 2), 0)
                lead_w(i, at, 12, 20)
                root(i * 2)
                lead_w(i, at, 20, 24)
                squares(i * 2 + 1, i * 8 + (1 + U_KV + 4), 2)
                lead_w(i, at, 24, 28)
                root(i * 2 + 1)
                lead_w(i, at, 28, 32 + HS)
                for tt, (t0, nt) in enumerate(TOK):
                    act.wait_ge(kt_full, i * 3 + tt + 1 + 1)
                    s.copy(kto[0:nt, bass.ds(i, 1), tt, :].rearrange("p o c -> p (o c)"), ps[0:nt, KT_BANKS[tt], :]).then_inc(kt_out, 1)
                s.copy(kTs[:, bass.ds(i // 2, 1)].rearrange("p o g t -> p (o g) t"), kro).then_inc(kcp_out, 1)
            lead(NORM_B, normed(hnf_b), False)
            act.wait_ge(kt_out, 3 + 9)
            act.wait_ge(vt_out, 10)
            s.copy(vts[:, :, 0:2, :], vto[:, 1:3, 0:2, :]).then_inc(vts_out, 1)
            s.copy(vts[0:NS, :, 2, :], vto[0:NS, 1:3, 2, :]).then_inc(vts_out, 1)
            for br in range(3):
                for c, src in ((0, kto), (1, vto)):
                    if br < 2:
                        dp = rows_p[0, :, 2 * br + c].rearrange("(t p) g d -> p t (g d)", p=P)
                        ds_ = rows_s[:, :, 2 * br + c].rearrange("b t g d -> (b t) (g d)")
                        act.dma_start(dp, src[:, br, 0:2, :]).then_inc(kv_store, 16)
                        act.dma_start(ds_, src[0:NS, br, 2, :]).then_inc(kv_store, 16)
                    else:
                        dp = win_p[0, :, c].rearrange("(t p) g d -> p t (g d)", p=P)
                        act.dma_start(dp, src[:, br, 0:2, :]).then_inc(kv_store, 16)
                        act.dma_start(win_s[:, WIN - T:WIN, c].rearrange("b t g d -> b t (g d)"), src[0:NS, br, 2, :]).then_inc(kv_store, 16)
            act.wait_ge(kv_store, 16 * 12)
            act.wait_ge(pc_full, 1)
            act.dma_start(wgt, w_qz[0, :, 4 * HDALL:4 * HDALL + GATES].rearrange("(k p) c -> p k c", p=P)).then_inc(wg_in, 16)

            for i in range(2):
                at, last = U_QUERY * HALF, i == 1
                lead_w(i, at, HS, 12)
                for u in range(4):
                    squares(i * 4 + 6 + u, i * 8 + (1 + U_QUERY + 2 * u + 2), 2 * (u % 2))
                    lead_w(i, at, 8 * u + 12, min(8 * u + 16, 32 if last else 32 + HS))
                    root(i * 4 + 6 + u)
                    lead_w(i, at, 8 * u + 16, min(8 * u + 20, 32 if last else 32 + HS))
            act.wait_ge(wg_in, 16)
            act.wait_ge(w_used, HS + G_Z)
            s.copy(wg_hi, wgt).then_inc(wg_out, 1)
            act.wait_ge(g_full, 1)
            act.wait_ge(rope_out, 15)
            s.activation(gd[0:GATES], ps[0:GATES, 0, 0:NT], ACT.Exp, scale=-1.0).then_inc(ge_out, 1)
            act.wait_ge(gd_out, 1)
            act.dma_start(gates_dram, gd[0:GATES]).then_inc(gates_out, 16)
            act.wait_ge(gates_out, 16)
            act.wait_ge(x1_store, 16)
            act.wait_ge(vts_out, 2)

            with act.Fori(0, B) as i:
                st = lambda a, n=1: stat[:, a:a + n]

                def odds(lo, hi):
                    for n in range(lo, hi):
                        if n % 2 == 1:
                            empty_t(act, s.copy, n, i)

                def exp_z(u):
                    act.wait_ge(w_used, i * ZG + (HS + G_Z + 8 * u + 8))
                    act.wait_ge(zu_free, i * 3 + u + 1)
                    s.activation(ezm, ps[:, 2 * (u % 2):2 * (u % 2) + 2, 0:NT], ACT.Exp, scale=-1.0).then_inc(ze_out, 1)

                act.wait_ge(cexp_in, i + 1)
                s.activation(pcm, msb[:, 0:NBK], ACT.Exp, bias=st(0), scale=SCALE, accum_out=st(1)).then_inc(cexp_out, 1)
                odds(0, 4)
                act.wait_ge(wexp_in, i + 1)
                s.activation(S[:, 0:WIN + NS], S[:, 0:WIN + NS], ACT.Exp, bias=st(3), scale=SCALE, accum_out=st(4)).then_inc(wexp_out, 1)
                odds(4, 8)
                exp_z(0)
                odds(8, 16)
                exp_z(1)
                odds(16, 21)
                act.wait_ge(sexp_in, i + 1)
                s.activation(S[:, SL:], S[:, SL:], ACT.Exp, bias=st(6), scale=SCALE, accum_out=st(7)).then_inc(sexp_out, 1)
                for qt in range(2):
                    act.wait_ge(pexp_in, i * 3 + qt + 1)
                    for a in range(4):
                        x = Sp[:, qt, a, 0:(qt + 1) * P]
                        ins = s.activation(x, x, ACT.Exp, bias=st(16 + 4 * qt + a), scale=SCALE, accum_out=st(24 + 4 * qt + a))
                    ins.then_inc(pexp_out, 1)
                exp_z(2)
                act.wait_ge(pexp_in, i * 3 + 3)
                s.activation(pcs, pcs, ACT.Exp, scale=SCALE).then_inc(pexp_out, 1)
                odds(21, NTU)

            act.wait_ge(m_free, B * NMU + 1)
            act.wait_ge(w_used, HS + G_OUT)
            act.wait_ge(ots_out, 1)
            lead(GATED, gated)
            for n in range(8):
                act.wait_ge(y_full, n + 1)
                if n >= 2:
                    act.wait_ge(y_stored[n % 2], 32 * (n // 2))
                for tt, (t0, nt) in enumerate(TOK):
                    ins = s.copy(ysb[n % 2][0:nt, tt, :], ps[0:nt, 3 * (n % 2) + tt, 0:UNIT])
                ins.then_inc(y_free, 1)
                act.wait_ge(y_free, 2 + n + 1)
                cols = slice(n * UNIT, (n + 1) * UNIT)
                act.dma_start(y_p[0, :, cols].rearrange("(t p) c -> p t c", p=P), ysb[n % 2][:, 0:2, :]).then_inc(y_stored[n % 2], 16)
                act.dma_start(y_s[:, :, cols].rearrange("b t c -> (b t) c"), ysb[n % 2][0:NS, 2, :]).then_inc(y_stored[n % 2], 16)


_INS = ['x_prompt', 'x_sample', 'state_conv', 'cache_kv', 'state_win', 'page_table', 'g_a', 'w_in_a', 'conv_w', 'w_out_a',
        'g_kv', 'w_kv', 'g_k', 'w_cmp', 'g_b', 'w_qz', 'g_q', 'w_out_b']
_OUTS = [(1, NP, D), (B, T, D), (1, 1, 2, D), (1, B, 2, D), (1, NP, 4, G, HD), (B, T, 4, G, HD), (1, NP, 2, G, HD),
         (B, WIN, 2, G, HD)]


def tables():
    f = np.float32
    half = HD // 2
    inv = (10000.0 ** (-np.arange(half) / half)).astype(f)
    pos = np.concatenate([np.arange(NP), np.tile(PAST + np.arange(T), B)]).astype(f)
    ang = (pos[None, :] * inv[:, None]).astype(np.float64)
    row, t = np.arange(P), np.arange(P) % T
    new_b, new_t = np.arange(NS) // T, np.arange(NS) % T
    ok_new = (new_b[None, None] == np.arange(B)[None, :, None]) & (new_t[None, None] <= t[:, None, None])
    blk_end = np.arange(PBK) * BLK + BLK - 1
    ok_cmp = blk_end[None, None] <= row[:, None, None] + P * np.arange(2)[None, :, None]
    hide = lambda ok: np.where(ok, 0.0, NEG).astype(f)
    j = np.arange(MID)
    return {
        "ident": np.eye(P, dtype=f),
        "ones": np.ones((P, P), f),
        "inblk": (row[:, None] // (BLK // TPP) == np.arange(P // (BLK // TPP))[None]).astype(f),
        "group": ((row[:, None] // 32 == row[None] // 32) & (t[:, None] == t[None])).astype(f),
        "causal": hide(row[None] <= row[:, None]),
        "cosT": np.tile(np.cos(ang), (2, 1)).astype(f),
        "sinT": np.concatenate([np.sin(ang), -np.sin(ang)]).astype(f),
        "newmask": hide(ok_new),
        "winmask": hide(np.arange(T)[None] > t[:, None]),
        "tri": np.tile((j[None] < j[:, None]).astype(f)[None], (P, 1, 1)),
        "pcmask": hide(ok_cmp),
        "pckeep": ok_cmp.astype(f),
    }


def kernel(**inputs):
    import concourse.bacc as bacc
    from concourse.bass_utils import run_bass_kernel_spmd

    nc = bacc.Bacc("TRN2", target_bir_lowering=False, num_devices=1, dynamic_dma_scratch_size=1024)
    arrays, ins = {}, []
    for name in _INS:
        a = np.ascontiguousarray(inputs[name])
        arrays[f"in_{name}"] = a
        ins.append(nc.dram_tensor(f"in_{name}", a.shape, mybir.dt.from_np(a.dtype), kind="ExternalInput").ap())
    consts = {}
    for name, a in tables().items():
        arrays[f"table_{name}"] = a
        consts[name] = nc.dram_tensor(f"table_{name}", a.shape, F32, kind="ExternalInput").ap()
    outs = [nc.dram_tensor(f"out_{n}", shape, F32, kind="ExternalOutput").ap() for n, shape in enumerate(_OUTS)]
    scratch = [nc.dram_tensor("gates", (GATES, NT), F32, kind="Internal").ap(),
               nc.dram_tensor("x1", (P, KT * NT), F32, kind="Internal").ap()]
    build(nc, ins, consts, outs, scratch)
    r = run_bass_kernel_spmd(nc, [arrays], core_ids=[0])
    return tuple(r.results[0][f"out_{n}"] for n in range(len(_OUTS)))
```

```python
from contextlib import ExitStack

import numpy as np

import concourse.bass as bass
import concourse.mybir as mybir

F32 = mybir.dt.float32
FR = mybir.dt.float32r
BF16 = mybir.dt.bfloat16
I32 = mybir.dt.int32
ACT = mybir.ActivationFunctionType
ALU = mybir.AluOpType
AX = mybir.AxisListType

P = 128
D = 2048
KT = D // P
NP = 256
B, T = 8, 8
NS = B * T
NT = NP + NS
H, G = 16, 4
R = H // G
HD = 128
PAST, PAGE, BLK, WIN = 2048, 128, 64, 512
N_SEL = 16
NPG = PAST // PAGE
NBK = PAST // BLK
PBK = NP // BLK
MID = NBK - 2
KEEP = N_SEL - 3
EPS = 1e-6
NEG = -1e30
SCALE = HD ** -0.5
UNIT = 256
GATES = 3 * H

WS = 4
WSZ = KT // 4 * UNIT
GK = 2
GSZ = GK * UNIT
GPS = WSZ // GSZ
HS = 4
HALF = KT // 2 // GK
ZS = 2
CS = 2
CPG = 4
TPP = CPG * PAGE // P
GPSQ = NPG // CPG
VS = 5
VSZ = 2 * G * HD

TOK = ((0, P), (P, P), (NP, NS))


class Chain:

    def __init__(self, eng, sem):
        self.eng, self.sem, self.base, self.n = eng, sem, 0, 0

    def __call__(self, ins):
        self.n += 1
        ins.then_inc(self.sem, 1)
        self.eng.wait_ge(self.sem, self.base + self.n)

    def enter(self, i, per):
        self.start, self.per = self.base + self.n, per
        self.base, self.n = i * per + self.start, 0

    def leave(self, trips):
        assert self.n == self.per, (self.n, self.per)
        self.base, self.n = self.start + trips * self.per, 0


T_USES = ([("keys", c, g) for c in range(2) for g in range(G)] + [("probs_win", 0, 0)]
          + [("keys", c, g) for c in range(2, 5) for g in range(G)]
          + [("probs_sel", c, 0) for c in range(4)] + [("probs_new", 0, 0)]
          + [("prompt", c, 0) for c in range(3)] + [("prompt_cmp", 0, 0)])
NTU = len(T_USES)
assert NTU % 2 == 0
CHUNKS = 1 + PAST // 512
NSU = CHUNKS + 4
NMU = 12
KEY_USE = (0, 2, 4, 8, 10)
VWIN_USE, VSEL_USE, V_USES = 6, 12, 20


def build(nc, ins, consts, outs, scratch):
    (x_prompt, x_sample, state_conv, cache_kv, state_win, page_table, g_a, w_in_a, conv_w, w_out_a,
     g_kv, w_kv, g_k, w_cmp, g_b, w_qz, g_q, w_out_b) = ins
    y_p, y_s, conv_p, conv_s, rows_p, rows_s, win_p, win_s = outs
    gates_dram, x1_dram = scratch

    with ExitStack() as ctx:
        def sem(name):
            return ctx.enter_context(nc.semaphore(name))

        ps = ctx.enter_context(nc.psum_tensor("ps", [P, 8, 512], F32))

        def sb(name, *shape, dt=F32):
            return ctx.enter_context(nc.sbuf_tensor(name, [P, *shape], dt))

        ident, ones, group, causal = (sb(n, P) for n in ("ident", "ones", "group", "causal"))
        cosT, sinT = sb("cosT", NT), sb("sinT", NT)
        newmask = sb("newmask", B, NS)
        winmask = sb("winmask", T)
        tri = sb("tri", MID, MID, dt=BF16)
        pcmask, pckeep = sb("pcmask", 2, PBK), sb("pckeep", 2, PBK)
        vecT = sb("vecT", 100)
        w2 = sb("w2", 2, G, 2)
        wc = sb("wc", TPP, 2 * G)
        inblk = sb("inblk", P // (BLK // TPP))
        ptab = sb("ptab", B * NPG, dt=I32)
        pcvT = sb("pcvT", G, PBK)
        kcT, vcT = sb("kcT", B, G, NBK), sb("vcT", B, G, NBK)
        WRING = 7168
        wring = sb("wring", WRING)
        w_hi, w_lo = sb("w_hi", HS, GK, UNIT, dt=FR), sb("w_lo", HS, GK, UNIT, dt=FR)
        hn_hi, hn_lo = sb("hn_hi", KT, NT, dt=FR), sb("hn_lo", KT, NT, dt=FR)
        as_f32 = lambda a: a.bitcast(F32)
        BIG = 30720
        big = sb("big", BIG)

        class Region:
            def __init__(self, lo, hi):
                self.at, self.hi = lo, hi

            def take(self, *shape):
                n = int(np.prod(shape))
                v = big[:, self.at:self.at + n]
                self.at += n
                assert self.at <= self.hi, ("region", self.at, self.hi)
                if len(shape) > 1:
                    names = "abcd"[:len(shape)]
                    v = v.rearrange(f"p ({' '.join(names)}) -> p {' '.join(names)}", **dict(zip(names, shape)))
                return v

        kc = lambda a: a.rearrange("p (k c) -> p k c", c=UNIT)
        slot = [kc(wring[:, s * WSZ:(s + 1) * WSZ]) for s in range(WS)]
        zslot = [kc(wring[:, s * GSZ:(s + 1) * GSZ]) for s in range(ZS)]
        Sp = wring[:, WSZ:WSZ + 2048].rearrange("p (q a k) -> p q a k", q=2, a=4)
        VLO = WSZ + 2048
        assert ZS * GSZ <= WSZ and VLO + (VS - 1) * VSZ <= WRING and VLO + VSZ >= WS * WSZ
        vslot = [wring[:, VLO + s * VSZ:VLO + (s + 1) * VSZ].rearrange("p (k c) -> p k c", k=2) for s in range(VS - 1)]

        XLO = BIG - KT * NT
        xT = big[:, XLO:BIG].rearrange("p (k t) -> p k t", k=KT)
        rstd = big[:, XLO - NT:XLO]
        keep = Region(0, BIG)
        qS = keep.take(B, H * T)
        qP = keep.take(H, NP)
        kTs = keep.take(2, G, NT)
        vts = keep.take(2, 3, G * HD)
        pcK = keep.take(G, PBK)
        pcV = keep.take(G, HD)
        tmp = Region(keep.at, XLO - NT)
        kro = tmp.take(G, NT)
        vto, kto = tmp.take(3, 3, G * HD), tmp.take(3, 3, G * HD)
        HEADS = tmp.at
        raw, sq, rs, kn, ra = (tmp.take(2, NT) for _ in range(5))
        wgt = wring[:, WS * WSZ:WS * WSZ + KT * GATES].rearrange("p (k c) -> p k c", c=GATES)
        wg_hi, wg_lo = (w[:].rearrange("p h k c -> p (h k c)")[:, 0:KT * GATES].rearrange("p (k c) -> p k c", c=GATES)
                        for w in (w_hi, w_lo))
        hnf_b = [big[:, a:a + 2 * NT].rearrange("p (k t) -> p k t", t=NT) for a in range(HEADS, HEADS + 8 * NT, 2 * NT)]
        gd = kro[:, 0, :]
        early = Region(0, XLO - NT)
        yT = early.take(KT, NT)
        pgs = early.take(CS, TPP, 2 * G * HD)
        pg = [pgs[:, s] for s in range(CS)]
        xin = big[:, KT * NT:KT * NT + 3 * D].rearrange("p (t d) -> p t d", t=3)
        cpad = early.take(2, NP + 2)
        spad = early.take(2, B, T + 2)
        csb = early.take(2, NT)
        ssum = big[:, early.at:early.at + 4 * NT].rearrange("p (q t) -> p q t", q=4)
        ez, bc = (early.take(2, NT) for _ in range(2))
        stT = early.take(KT, 2 * B)
        cso = early.take(KT, 2 + 2 * B)
        xsq = early.take(KT, NT)
        small = yT.rearrange("p k t -> p (k t)")
        vecs, stin = small[:, 0:P], small[:, P:P + D]
        trif = small[:, P + D:P + D + MID * MID].rearrange("p (j i) -> p j i", i=MID)
        crow = pgs[:, 0].rearrange("p t c -> p (t c)")[:, 0:D]
        hnf = [early.take(GK, NT) for _ in range(4)]
        main = Region(keep.at, BIG)
        zS = main.take(3, H, NS)
        oS = main.take(3, B, H * T)
        LATE = main.at
        KTb = main.take(G, 512)
        Pp = KTb.rearrange("p g k -> p (g k)")[:, 0:4 * 384].rearrange("p (a q) -> p a q", a=4)
        S = main.take(WIN + NS + PAST + NS)
        PT = [main.take(4, P) for _ in range(2)]
        gt, eq = (PT[n].rearrange("p a b -> p (a b)")[:, 0:MID * MID // 2].bitcast(BF16)
                  .rearrange("p (j i) -> p j i", i=MID) for n in range(2))
        PTn = main.take(2, P)
        gbc = main.take(2, NT)
        ezm = main.take(2, NT)
        zgP = main.take(3, 2, NP)
        vst = main.take(2, 2, HD)
        pvst = main.take(HD)
        qst = main.take(2, NP)
        qSb = sb("qSb", H * T)[:]
        vcst, kcst = main.take(G, NBK), main.take(G, NBK)
        vcb = main.take(G * HD)
        msb = main.take(192)
        pcm, psc, bmask = main.take(NBK), main.take(NBK), main.take(NBK)
        pcT = main.take(H * T)
        pcTp = main.take(2, NP)
        pcs = main.take(4, PBK)
        stat = main.take(64)
        otmp = main.take(2, NP)
        vslot.append(main.take(2, VSZ // 2))
        late = Region(LATE, XLO)
        oTs = late.take(H, NS)
        oadd = late.take(H, NS)
        xst = [late.take(2, NT) for _ in range(2)]
        ysb = [late.take(3, UNIT) for _ in range(2)]

        WN, SL, SN = WIN, WIN + NS, WIN + NS + PAST

        CS_BANKS = (5, 6, 7, 3)
        KT_BANKS, VT_BANKS = (7, 3, 2), (0, 1, 6)

        x_in, misc_in, consts_in = sem("x_in"), sem("misc_in"), sem("consts_in")
        w2_zero, w2_done, consts_used = sem("w2_zero"), sem("w2_done"), sem("consts_used")
        tp_full, tpd_free, tpa_free = sem("tp_full"), sem("tpd_free"), sem("tpa_free")
        vec_full, vec_out = sem("vec_full"), sem("vec_out")
        sq_out, sum_out, sum_full, var_out, sd_out, hn_out = (sem(n) for n in (
            "sq_out", "sum_out", "sum_full", "var_out", "sd_out", "hn_out"))
        w_full, w_used = [sem(f"w_full{s}") for s in range(WS)], sem("w_used")
        w_asked = sem("w_asked")
        hi_out, split_out, hn_raw, hn_hid = sem("hi_out"), sem("split_out"), sem("hn_raw"), sem("hn_hid")
        z_full = [sem(f"z_full{s}") for s in range(ZS)]
        v_full, v_used = [sem(f"v_full{s}") for s in range(VS)], sem("v_used")
        pg_full, pg_used, pg_summed = [sem(f"pg_full{s}") for s in range(CS)], sem("pg_used"), sem("pg_summed")
        c_out, h_used, e_out, zc_used, b_used, y_out = (sem(n) for n in (
            "c_out", "h_used", "e_out", "zc_used", "b_used", "y_out"))
        kc_out, vc_out = sem("kc_out"), sem("vc_out")
        cs_full, cs_out = sem("cs_full"), sem("cs_out")
        x1_out = sem("x1_out")
        dchain, achain = sem("dchain"), sem("achain")
        cs_store, x1_store, kv_store, wcopy = (sem(n) for n in ("cs_store", "x1_store", "kv_store", "wcopy"))
        sqr_out, hs_full, hv_out, hsd_out, rope_out, kcp_out = (sem(n) for n in (
            "sqr_out", "hs_full", "hv_out", "hsd_out", "rope_out", "kcp_out"))
        kt_full, kt_out, vt_out = sem("kt_full"), sem("kt_out"), sem("vt_out")
        pc_full, pc_out, pv_full, pv_out, vts_out = (sem(n) for n in ("pc_full", "pc_out", "pv_full", "pv_out", "vts_out"))
        wg_in, wg_out, g_full, ge_out, gd_out, gates_out = (sem(n) for n in ("wg_in", "wg_out", "g_full", "ge_out", "gd_out", "gates_out"))
        gb_full, gb_used = sem("gb_full"), sem("gb_used")
        st_sample, st_prompt = sem("st_sample"), sem("st_prompt")
        t_full, t_free = sem("t_full"), sem("t_free")
        s_full, s_free, m_full, m_free = sem("s_full"), sem("s_free"), sem("m_full"), sem("m_free")
        ze_out, zu_free = sem("ze_out"), sem("zu_free")
        cexp_in, cexp_out, wexp_in, wexp_out, sexp_in, sexp_out, pexp_in, pexp_out = (sem(n) for n in (
            "cexp_in", "cexp_out", "wexp_in", "wexp_out", "sexp_in", "sexp_out", "pexp_in", "pexp_out"))
        p_ready, rank_out, pp_ready, os_full = sem("p_ready"), sem("rank_out"), sem("pp_ready"), sem("os_full")
        x1_back = sem("x1_back")
        ots_out, xst_out, y_full, y_free = sem("ots_out"), sem("xst_out"), sem("y_full"), sem("y_free")
        y_stored = [sem("y_stored0"), sem("y_stored1")]

        U_MIX, U_KV, U_QUERY, U_OUT = 64, 80, 104, 120
        G_Z = U_OUT * HALF
        ZG = 3 * KT // GK
        G_OUT = G_Z + B * ZG
        HDALL = H * HD

        def wload(sp, w, half, col, use, n):
            col = sp.snap(col)
            for q in range(2):
                s, row = (2 * n + q) % WS, (2 * half + q) * D // 4
                sp.wait_ge(split_out, use * HALF + GPS * (q + 1))
                sp.sem_inc(w_asked, 1)
                sp.dma_start(slot[s], w[row:row + D // 4, bass.ds(col, UNIT)]
                             .rearrange("(k p) c -> p k c", p=P)).then_inc(w_full[s], 16)

        def empty_t(eng, copy, n, i):
            kind, c, g = T_USES[n]
            bank = 4 + n % 2
            if kind == "keys":
                eng.wait_ge(*((s_full, i * NSU + c) if c else (m_full, i * NMU + 1)))
            eng.wait_ge(t_full, i * NTU + n + 1)
            four = ps[:, bank, :].rearrange("p (a q) -> p a q", a=4)
            if kind == "keys":
                ins = copy(KTb[:, g, :], ps[:, bank, :])
            elif kind in ("probs_win", "probs_sel"):
                ins = copy(PT[c % 2], four)
            elif kind == "probs_new":
                ins = copy(PTn[0:NS, 0, :], ps[0:NS, bank, 0:P])
            elif kind == "prompt":
                ins = copy(Pp[:, :, c * P:(c + 1) * P], four)
            else:
                ins = copy(pcTp[0:PBK], ps[0:PBK, bank, :].rearrange("p (t q) -> p t q", t=2))
            ins.then_inc(t_free, 1)

        NORM_A, MIXED, NORM_KV, NORM_B, GATED = range(1, 6)
        RAWS = (NORM_A, NORM_KV, NORM_B)
        PIECES = KT // GK
        piece = lambda q: slice(GK * q, GK * q + GK)

        def normed(buf):
            return lambda q: [((slice(None), piece(q)), buf[q % len(buf)])]

        def mixed(q):
            return [((slice(None), piece(q)), yT[:, piece(q)])]

        def gated(q):
            return [((slice(None), piece(q), slice(0, NP)), qP[:, piece(q)]),
                    ((slice(None), piece(q), slice(NP, NT)), oTs[:, piece(q)])]

        SMAX, SSUM = 52, 56
        N_CONSTS = 13 + P // (BLK // TPP)

        block = ctx.enter_context(nc.Block())

        @block.sync
        def _(sp):
            for tt, (t0, n) in enumerate(TOK[:2]):
                sp.dma_start(xin[:, tt, :], x_prompt[0, t0:t0 + n, :]).then_inc(x_in, 16)
            sp.dma_start(xin[0:NS, 2, :], x_sample.rearrange("b t d -> (b t) d")).then_inc(x_in, 16)
            sp.dma_start(ident[:], consts["ident"]).then_inc(x_in, 16)
            sp.dma_start(ones[:], consts["ones"]).then_inc(x_in, 16)
            sp.dma_start(vecs[0:16, :], g_a.rearrange("l (k p) -> (l k) p", p=P)).then_inc(misc_in, 16)
            sp.dma_start(vecs[16:32, :], g_kv.rearrange("(k p) -> k p", p=P)).then_inc(misc_in, 16)
            sp.dma_start(vecs[32:48, :], g_b.rearrange("l (k p) -> (l k) p", p=P)).then_inc(misc_in, 16)
            sp.dma_start(vecs[48:96, :], conv_w.rearrange("l w (k p) -> (l w k) p", p=P)).then_inc(misc_in, 16)
            sp.dma_start(vecs[96:99, :], g_k).then_inc(misc_in, 16)
            sp.dma_start(vecs[99:100, :], g_q).then_inc(misc_in, 16)
            sp.dma_start(stin[0:2 * B, :], state_conv.rearrange("l b w d -> (l b w) d")).then_inc(misc_in, 16)
            for half in range(2):
                wload(sp, w_in_a[0], half, D, half, half)
            for t, name in ((group, "group"), (causal, "causal"), (cosT, "cosT"), (sinT, "sinT"),
                            (newmask, "newmask"), (winmask, "winmask"), (trif, "tri"), (pcmask, "pcmask"), (pckeep, "pckeep"),
                            (inblk, "inblk")):
                sp.dma_start(t[:] if t is not trif else t, consts[name]).then_inc(consts_in, 16)
            sp.dma_start(ptab[0:1, :], page_table.rearrange("(o b) n -> o (b n)", o=1)).then_inc(consts_in, 16)
            for lo in (0, BLK):
                sp.dma_start(csb[lo:lo + BLK, 0, 0:2 * G], w_cmp.rearrange("l c g -> l (c g)")).then_inc(consts_in, 16)
            for lo in range(0, P, BLK // TPP):
                sp.dma_start(wc[lo:lo + BLK // TPP].rearrange("p t c -> p (t c)"), w_cmp.rearrange("(p t) c g -> p (t c g)", t=TPP)).then_inc(consts_in, 16)
            sp.wait_ge(consts_in, 16 * N_CONSTS)

            def conv_step(i, first):
                for n in range(8):
                    quarter, half = (1, 2, 3, 0)[n // 2], n % 2
                    if not (first and n < 2):
                        wload(sp, w_in_a[0], half, i * UNIT + quarter * D, i * 8 + n, n)
                    if first and n == 0:
                        sp.wait_ge(tp_full, KT)
                    if n % 2 == 0:
                        q, rows = n // 2, P // CPG
                        for k in range(CPG):
                            page = sp.value_load(ptab[0:1, bass.ds(i * NPG + q * CPG + k, 1)], min_val=0, max_val=cache_kv.shape[0] - 1)
                            if k == 0:
                                sp.wait_ge(pg_used, i * GPSQ + q + 1)
                            sp.dma_start(pg[q % CS][k * rows:(k + 1) * rows], cache_kv[bass.ds(page, 1), :, 0:2].rearrange(
                                "o (l t) c g d -> (o l) t (c g d)", t=TPP)).then_inc(pg_full[q % CS], 16)

            conv_step(0, True)
            with sp.Fori(1, B) as i:
                conv_step(i, False)
            with sp.Fori(0, 2) as i:
                for n in range(8):
                    wload(sp, w_out_a[0], n % 2, i * (4 * UNIT) + n // 2 * UNIT, i * 8 + U_MIX + n, n)

            def window_copy(b):
                sp.dma_start(win_s[bass.ds(b, 1), 0:WIN - T].rearrange("o l c g d -> o (l c g d)"),
                             state_win[bass.ds(b, 1), T:WIN].rearrange("o l c g d -> o (l c g d)")).then_inc(wcopy, 16)

            sp.dma_start(wgt, w_qz[0, :, 4 * HDALL:4 * HDALL + GATES].rearrange("(k p) c -> p k c", p=P)).then_inc(wg_in, 16)
            with sp.Fori(0, 3) as i:
                for n in range(8):
                    wload(sp, w_kv, n % 2, i * (8 * HD) + n // 2 * UNIT, i * 8 + U_KV + n, n)
                    if n % 4 == 3:
                        window_copy(i * 2 + n // 4)
            with sp.Fori(0, 2) as i:
                for n in range(8):
                    wload(sp, w_qz[0], n % 2, i * (4 * UNIT) + n // 2 * UNIT, i * 8 + U_QUERY + n, n)
                window_copy(i + 6)

            def zload(i, use):
                u, kk, s = use // 8, use % 8, use % ZS
                col = sp.snap(i * UNIT + (1 + u) * HDALL)
                sp.wait_ge(split_out, i * ZG + (G_Z + WS * GPS - ZS + use + 1))
                sp.dma_start(zslot[s], w_qz[0, kk * GK * P:(kk + 1) * GK * P, bass.ds(col, UNIT)]
                             .rearrange("(k p) c -> p k c", p=P)).then_inc(z_full[s], 16)

            def vload(i, use, first, window, chunk, part, which):
                s = use % VS
                if first and s == 0:
                    sp.wait_ge(split_out, WS * GPS + G_Z)
                if first and s == 1:
                    sp.wait_ge(wg_out, 2)
                if first and s == VS - 1:
                    sp.wait_ge(x1_store, 16)
                    sp.wait_ge(hn_out, PIECES * NORM_B)
                srcs = []
                for k in range(2):
                    j = 4 * chunk + 2 * part + k
                    if window:
                        src = state_win[bass.ds(i, 1), j * P:(j + 1) * P, which].rearrange("o l g d -> (o l) (g d)")
                    else:
                        page = sp.value_load(ptab[0:1, bass.ds(i * NPG + j, 1)], min_val=0, max_val=cache_kv.shape[0] - 1)
                        src = cache_kv[bass.ds(page, 1), :, 2 + which].rearrange("o l g d -> (o l) (g d)")
                    srcs.append(src)
                sp.wait_ge(v_used, i * V_USES + use + 1)
                for k in range(2):
                    sp.dma_start(vslot[s][:, k, :], srcs[k]).then_inc(v_full[s], 16)

            def gload(i, u):
                row = sp.snap(i * 2 + u * H)
                if u or not isinstance(i, int):
                    sp.wait_ge(gb_used, i * 3 + u)
                sp.dma_start(gbc, gates_dram[bass.ds(row, 2), :].rearrange("(o h) t -> o h t", o=1)
                             .to_broadcast([P, 2, NT])).then_inc(gb_full, 16)

            def main_step(i, first):
                for c in range(CHUNKS):
                    for part in range(2):
                        vload(i, KEY_USE[c] + part, first, c == 0, max(c - 1, 0), part, 0)
                        zload(i, 4 * c + 2 * part)
                        zload(i, 4 * c + 2 * part + 1)
                    if c == 2:
                        for part in range(2):
                            vload(i, VWIN_USE + part, first, True, 0, part, 1)
                    if c == 2:
                        if first:
                            sp.wait_ge(gates_out, 16)
                        gload(i, 0)
                    if c == 3:
                        gload(i, 1)
                for n in range(8):
                    if n < 4:
                        zload(i, 20 + n)
                    if n == 4:
                        gload(i, 2)
                    vload(i, VSEL_USE + n, False, False, n // 2, n % 2, 1)

            main_step(0, True)
            with sp.Fori(1, B) as i:
                main_step(i, False)

            def out_load(i, n, first):
                if first and n == 0:
                    sp.wait_ge(m_full, B * NMU + 1)
                if first and n == 1:
                    sp.wait_ge(ots_out, 1)
                    sp.dma_start(xT, x1_dram.rearrange("p (k t) -> p k t", k=KT)).then_inc(x1_back, 16)
                for q in range(2):
                    s, row, col = (2 * n + q) % WS, (2 * (n % 2) + q) * D // 4, i * 4 * UNIT + n // 2 * UNIT
                    sp.wait_ge(split_out, G_OUT + (i * 8 + n) * HALF + GPS * (q + 1))
                    sp.dma_start(slot[s], w_out_b[0, row:row + D // 4, col:col + UNIT]
                                 .rearrange("(k p) c -> p k c", p=P)).then_inc(w_full[s], 16)

            for i in range(2):
                for n in range(8):
                    out_load(i, n, i == 0)
            sp.wait_ge(wcopy, 16 * B)
            sp.wait_ge(cs_store, 32)
            sp.wait_ge(x1_store, 16)
            sp.wait_ge(kv_store, 16 * 12)
            for q in y_stored:
                sp.wait_ge(q, 32 * 4)

        @block.gpsimd
        def _(pool):
            pool.sem_inc(split_out, WS * GPS)
            pool.sem_inc(w_used, HS)
            pool.sem_inc(pg_used, CS)
            pool.sem_inc(x1_out, 2)
            pool.sem_inc(sqr_out, 2)
            pool.sem_inc(kt_out, 3)
            pool.sem_inc(v_used, VS)
            pool.sem_inc(t_free, 2)
            pool.sem_inc(s_free, 1)
            pool.sem_inc(m_free, 1)
            pool.sem_inc(y_free, 2)
            for count in (zc_used, b_used, kc_out, vc_out, vt_out, zu_free, m_full, kcp_out, kt_full, h_used, y_out, rope_out):
                pool.sem_inc(count, 1)
            nc.gpsimd.memset(w2[:], 0.0).then_inc(w2_zero, 1)

            def rest_of(g, raw, h):
                pool.wait_ge(hi_out, g + 1)
                nc.gpsimd.tensor_tensor(w_lo[:, h], raw, as_f32(w_hi[:, h]), ALU.subtract).then_inc(split_out, 1)

            def split(g, raw, h):
                pool.wait_ge(w_used, g + 1)
                pool.sem_inc(w_asked, 1)
                nc.gpsimd.tensor_scalar(w_hi[:, h], raw, 1.0, 0.0, ALU.mult, ALU.add).then_inc(hi_out, 1)
                rest_of(g, raw, h)

            def rests(lo, hi):
                with pool.Fori(lo * HALF // (WS * GPS), hi * HALF // (WS * GPS)) as j:
                    for g in range(WS * GPS):
                        rest_of(j * (WS * GPS) + g, slot[g // GPS][:, g % GPS * GK:(g % GPS + 1) * GK, :], g % HS)

            rests(0, U_QUERY)
            pool.wait_ge(wg_out, 1)
            nc.gpsimd.tensor_tensor(wg_lo, wgt, as_f32(wg_hi), ALU.subtract).then_inc(wg_out, 1)
            rests(U_QUERY, U_OUT)

            def zsplit(i, n):
                pool.wait_ge(z_full[n % ZS], i * (16 * ZG // ZS) + 16 * (n // ZS + 1))
                split(i * ZG + (G_Z + n), zslot[n % ZS], n % HS)

            def stage_sample(i):
                nc.gpsimd.tensor_copy(vcst, vcT[:, bass.ds(i, 1)].rearrange("p o g n -> p (o g) n")).then_inc(st_sample, 1)
                nc.gpsimd.tensor_copy(kcst, kcT[:, bass.ds(i, 1)].rearrange("p o g n -> p (o g) n")).then_inc(st_sample, 1)
                nc.gpsimd.tensor_copy(qSb, qS[:, bass.ds(i, 1), :].rearrange("p o c -> p (o c)")).then_inc(st_sample, 1)

            def step(i, more):
                pool.wait_ge(m_full, i * NMU + 1)
                nc.gpsimd.tensor_copy(qst, qP[:, bass.ds(i * 2, 2), :]).then_inc(st_prompt, 1)
                for br in range(2):
                    nc.gpsimd.tensor_copy(vst[:, br], vts[:, br, 0:2, bass.ds(i // 2 * HD, HD)]).then_inc(st_prompt, 1)
                nc.gpsimd.tensor_copy(pvst[0:PBK, :], pcV[0:PBK, bass.ds(i // 2, 1), :].rearrange("p o d -> p (o d)")).then_inc(st_prompt, 1)
                for n in range(HS, 20):
                    zsplit(i, n)
                for n in range(20, ZG):
                    zsplit(i, n)
                if more:
                    pool.wait_ge(s_full, i * NSU + CHUNKS)
                    stage_sample(i + 1)
                    for n in range(ZG, ZG + HS):
                        zsplit(i, n)

            for n in range(HS):
                zsplit(0, n)
            pool.wait_ge(rope_out, 15)
            pool.wait_ge(vts_out, 2)
            pool.wait_ge(pv_out, 1)
            pool.wait_ge(gd_out, 1)
            pool.wait_ge(gates_out, 16)
            pool.wait_ge(x1_store, 16)
            stage_sample(0)
            with pool.Fori(0, B - 1) as i:
                step(i, True)
            step(B - 1, False)
            for n in range(8):
                for g in range(2 * HALF * n, 2 * HALF * (n + 1)):
                    m = g // GPS % WS
                    if g % GPS == 0:
                        pool.wait_ge(w_full[m], 16 * ((G_Z + g) // (WS * GPS) + 1))
                    split(G_OUT + g, slot[m][:, g % GPS * GK:(g % GPS + 1) * GK, :], g % HS)
                if n == 0:
                    pool.wait_ge(x1_back, 16)
                pool.wait_ge(y_free, n + 1)
                nc.gpsimd.tensor_copy(xst[n % 2], xT[:, 2 * n:2 * n + 2, :]).then_inc(xst_out, 1)

        @block.tensor
        def _(pe):
            def mm(out, lhsT, rhs, start=True, stop=True, **kw):
                return nc.tensor.matmul(out, lhsT, rhs, start=start, stop=stop, **kw)

            def tr(out, in_):
                n = in_.shape[0]
                return nc.tensor.transpose(out, in_, ident[0:n, 0:n])

            pe.wait_ge(x_in, 80)
            for kt in range(KT):
                if kt >= 8:
                    pe.wait_ge((tpd_free, tpa_free)[kt % 2], (kt - 8) // 2 + 1)
                for tt, (t0, n) in enumerate(TOK):
                    last = tr(ps[:, kt % 8, t0:t0 + n], xin[0:n, tt, kt * P:(kt + 1) * P])
                last.then_inc(tp_full, 1)
            pe.wait_ge(misc_in, 16 * 7)
            pe.wait_ge(tpd_free, 8)
            pe.wait_ge(tpa_free, 8)
            tr(ps[:, 0, 0:100], vecs[0:100, :]).then_inc(vec_full, 1)
            for kt in range(KT):
                last = tr(ps[:, 1, kt * 2 * B:(kt + 1) * 2 * B], stin[0:2 * B, kt * P:(kt + 1) * P])
            last.then_inc(vec_full, 1)

            def sum_partitions(n, bank):
                for q in range(4):
                    pe.wait_ge(sum_out, 4 * (n - 1) + q + 1)
                    last = mm(ps[:, bank, 0:NT], ones[:], ssum[:, q, :], start=q == 0, stop=q == 3)
                last.then_inc(sum_full, 1)

            sum_partitions(1, 4)

            def products(out, w, x, start, stop):
                (wh, wl), (xh, xl) = w, x
                mm(out, wh, xh, start=start, stop=False, skip_group_check=True)
                mm(out, wh, xl, start=False, stop=False, skip_group_check=True)
                return mm(out, wl, xh, start=False, stop=stop, skip_group_check=True)

            def granule(g, k, c):
                return w_hi[:, g % HS, k, c], w_lo[:, g % HS, k, c]

            def split_wait(g):
                pe.wait_ge(split_out, g + (WS * GPS + 1))

            def half_unit(g0, bank, half, filled=0, aside=None):
                for g in range(HALF):
                    split_wait(g0 + g)
                    if filled:
                        pe.wait_ge(hn_out, PIECES * (filled - 1) + HALF * half + g + 1)
                    for t in range(2):
                        for k in range(GK):
                            kt = half * 8 + g * GK + k
                            last = products(ps[:, bank + t, 0:NT], granule(g, k, slice(t * P, (t + 1) * P)),
                                            (hn_hi[:, kt, :], hn_lo[:, kt, :]), kt == 0, kt == KT - 1)
                    last.then_inc(w_used, 1)
                    if g == 1 and aside:
                        aside()

            with pe.Fori(0, B) as i:
                for n in range(8):
                    u, half = n // 2, n % 2
                    if half == 0:
                        if u == 0:
                            pe.wait_ge(zc_used, i + 1)
                        if u == 1:
                            pe.wait_ge(b_used, i + 1)
                        if u == 2:
                            pe.wait_ge(c_out, i + 1)
                        if u == 3:
                            pe.wait_ge(h_used, i + 1 + 1)
                    half_unit(i * 32 + n * HALF, 2 * (u % 2), half, NORM_A if u == 0 else 0)
                    if half == 1:
                        q, nb = u, CPG * PAGE // BLK
                        if q == 0:
                            pe.wait_ge(kc_out, i + 1)
                            pe.wait_ge(vc_out, i + 1)
                        if q == 0:
                            pe.wait_ge(consts_in, 16 * N_CONSTS)
                        pe.wait_ge(pg_summed, i * GPSQ + q + 1)
                        for c in range(2):
                            for g in range(G):
                                last = mm(ps[:, 6 + c, g * NBK + nb * q:g * NBK + nb * (q + 1)],
                                          pg[q % CS][:, 0, (c * G + g) * HD:(c * G + g + 1) * HD], inblk[:])
                        last.then_inc(pg_used, 1)

            with pe.Fori(0, 2) as i:
                for n in range(8):
                    u, half = n // 2, n % 2
                    if half == 0:
                        pe.wait_ge(x1_out, i * 4 + u + 1)
                    half_unit(i * 32 + (U_MIX + n) * HALF, 2 * (u % 2), half, MIXED if u == 0 else 0)
            sum_partitions(2, 4)

            pe.wait_ge(y_out, B + 1)
            for n in range(4):
                if n == 3:
                    pe.wait_ge(x1_out, 2 + 8)
                for k in range(4):
                    last = tr(ps[0:18, CS_BANKS[n], k * P:(k + 1) * P], cso[:, 4 * n + k, :])
                last.then_inc(cs_full, 1)

            def head_sums(q):
                pe.wait_ge(sqr_out, 2 + q + 1)
                mm(ps[:, 4, 0:NT], ones[:], sq[:, 0, :])
                mm(ps[:, 5, 0:NT], ones[:], sq[:, 1, :]).then_inc(hs_full, 1)

            with pe.Fori(0, 3) as i:
                for n in range(8):
                    half = n % 2
                    if n < 4:
                        if n == 0:
                            pe.wait_ge(vt_out, i * 3 + 1)
                        if n == 2:
                            pe.wait_ge(kt_out, i * 3 + 3)
                            pe.wait_ge(cs_out, 4)
                        half_unit(i * 32 + (U_KV + n) * HALF, 2 * (n // 2), half, NORM_KV if n < 2 else 0)
                    else:
                        if n == 4:
                            pe.wait_ge(sqr_out, i * 2 + 3)
                        hf = (n - 4) // 2
                        for g in range(HALF):
                            split_wait(i * 32 + ((U_KV + n) * HALF + g))
                            for tt, (t0, nt) in enumerate(TOK):
                                for k in range(GK):
                                    kt = half * 8 + g * GK + k
                                    last = products(ps[0:nt, VT_BANKS[tt], hf * UNIT:(hf + 1) * UNIT],
                                                    (hn_hi[:, kt, t0:t0 + nt], hn_lo[:, kt, t0:t0 + nt]),
                                                    granule(g, k, slice(0, UNIT)), kt == 0, kt == KT - 1)
                            last.then_inc(w_used, 1)
                    if n in (2, 4):
                        head_sums(i * 2 + n // 4)
                    if n == 6:
                        pe.wait_ge(rope_out, i * 2 + 2 + 1)
                        for tt, (t0, nt) in enumerate(TOK):
                            for g in range(G):
                                last = tr(ps[0:nt, KT_BANKS[tt], g * HD:(g + 1) * HD], kro[:, g, t0:t0 + nt])
                            last.then_inc(kt_full, 1)
            pe.wait_ge(hv_out, 6)
            pe.wait_ge(wg_out, 2)
            for kt in range(KT):
                if kt % GK == 0:
                    pe.wait_ge(hn_out, PIECES * (NORM_B - 1) + kt // GK + 1)
                last = products(ps[0:GATES, 5, 0:NT], (wg_hi[:, kt, :], wg_lo[:, kt, :]), (hn_hi[:, kt, :], hn_lo[:, kt, :]),
                                kt == 0, kt == KT - 1)
            last.then_inc(g_full, 1)
            pe.wait_ge(w2_done, 2)
            pe.wait_ge(kt_out, 3 + 9)
            pe.wait_ge(vt_out, 10)
            for c, src in ((0, kto), (1, vto)):
                for tt in range(2):
                    for g in range(G):
                        last = mm(ps[:, 6 + c, g * PBK + 2 * tt:g * PBK + 2 * tt + 2], src[:, 0, tt, g * HD:(g + 1) * HD], w2[:, c, g, :])
            last.then_inc(pc_full, 1)
            pe.wait_ge(ge_out, 1)

            with pe.Fori(0, 2) as i:
                for n in range(8):
                    u, half = n // 2, n % 2
                    if half == 0:
                        pe.wait_ge(sqr_out, i * 4 + 6 + u + 1)
                    half_unit(i * 32 + (U_QUERY + n) * HALF, 2 * (u % 2), half, NORM_B if u == 0 else 0,
                              (lambda: head_sums(i * 4 + 6 + u - 1)) if half == 0 and u >= 1 else None)
                head_sums(i * 4 + 6 + 3)
            pe.wait_ge(pc_out, 2)
            for g in range(G):
                last = tr(ps[0:PBK, 6, g * HD:(g + 1) * HD], pcvT[:, g, :])
            last.then_inc(pv_full, 1)
            pe.wait_ge(hv_out, 14)

            with pe.Fori(0, B) as i:
                t_at = [0]

                def t_bank(known_free=False):
                    n = t_at[0]
                    t_at[0] += 1
                    if not known_free:
                        pe.wait_ge(t_free, i * NTU + n + 1)
                    return 4 + n % 2

                def t_emptied(kind, c, g):
                    pe.wait_ge(t_free, i * NTU + T_USES.index((kind, c, g)) + 3)

                def m_bank(n):
                    pe.wait_ge(m_free, i * NMU + n)

                def z_part(part):
                    u, kk = part // 8, part % 8
                    if kk == 0:
                        pe.wait_ge(zu_free, i * 3 + (1 if u == 2 else 0) + 1)
                    split_wait(i * ZG + (G_Z + part))
                    for t in range(2):
                        for k in range(GK):
                            kt = kk * GK + k
                            last = products(ps[:, 2 * (u % 2) + t, 0:NT], granule(part, k, slice(t * P, (t + 1) * P)),
                                            (hn_hi[:, kt, :], hn_lo[:, kt, :]), kt == 0, kt == KT - 1)
                    last.then_inc(w_used, 1)

                def keys(c, g):
                    for h in range(2):
                        use = KEY_USE[c] + h
                        if g == 0:
                            pe.wait_ge(v_full[use % VS], i * (32 * V_USES // VS) + 32 * (use // VS + 1))
                    bank = t_bank()
                    for p in range(4):
                        last = tr(ps[:, bank, p * P:(p + 1) * P], vslot[(KEY_USE[c] + p // 2) % VS][:, p % 2, g * HD:(g + 1) * HD])
                        if g == G - 1 and p == 1:
                            last.then_inc(v_used, 1)
                    last.then_inc(t_full, 1)

                def scores(c):
                    pe.wait_ge(s_free, i * NSU + c + 1)
                    for g in range(G):
                        t_emptied("keys", c, g)
                        last = mm(ps[32 * g:32 * g + 32, 6, :], qSb[:, 32 * g:32 * g + 32], KTb[:, g, :])
                        if g == 0:
                            last.then_inc(v_used, 1)
                    last.then_inc(s_full, 1)

                def pv(use, probs, start, last_chunk=False):
                    for p in range(4):
                        s = (use + p // 2) % VS
                        if p == 3 and last_chunk:
                            t_emptied("probs_new", 0, 0)
                        if p % 2 == 0:
                            pe.wait_ge(v_full[s], i * (32 * V_USES // VS) + 32 * ((use + p // 2) // VS + 1))
                        for g in range(G):
                            last = mm(ps[32 * g:32 * g + 32, 7, 0:HD], probs[:, p, 32 * g:32 * g + 32],
                                      vslot[s][:, p % 2, g * HD:(g + 1) * HD], start=start and p == 0, stop=False, skip_group_check=True)
                        if p % 2 == 1:
                            last.then_inc(v_used, 1)

                def pv_new(br):
                    for g in range(G):
                        last = mm(ps[32 * g:32 * g + 32, 7, 0:HD], PTn[0:NS, br, 32 * g:32 * g + 32],
                                  vts[0:NS, br, 2, g * HD:(g + 1) * HD], start=False, stop=True, skip_group_check=True)
                    last.then_inc(m_full, 1)

                def prompt_scores(qt, t):
                    pe.wait_ge(s_free, i * NSU + CHUNKS + qt * 2 + t + 1)
                    nk = (qt + 1) * P
                    for br in range(2):
                        last = mm(ps[:, 6, br * 256:br * 256 + nk], qst[:, t, qt * P:(qt + 1) * P],
                                  kTs[:, br, bass.ds(i // 2, 1), 0:nk].rearrange("p o k -> p (o k)"))
                    last.then_inc(s_full, 1)

                for g in range(G):
                    keys(0, g)
                    z_part(g)
                    if g == 0:
                        m_bank(1)
                        pe.wait_ge(st_sample, i * 3 + 3)
                        for gg in range(G):
                            q = qSb[:, 32 * gg:32 * gg + 32]
                            mm(ps[32 * gg:32 * gg + 32, 7, 0:NBK], q, kcst[:, gg, :])
                            mm(ps[32 * gg:32 * gg + 32, 7, 64:128], q, kTs[:, 1, gg, NP:NT])
                            last = mm(ps[32 * gg:32 * gg + 32, 7, 128:192], q, kTs[:, 0, gg, NP:NT])
                        last.then_inc(m_full, 1)
                    if g == 1:
                        m_bank(2)
                        pe.wait_ge(p_ready, i + 1)
                        mm(ps[:, 7, 0:NBK], group[:], pcm).then_inc(m_full, 1)
                    if g == 2:
                        m_bank(3)
                        for gg in range(G):
                            last = tr(ps[0:NBK, 7, gg * HD:(gg + 1) * HD], vcst[:, gg, :])
                        last.then_inc(m_full, 1)
                    if g == 3:
                        m_bank(4)
                        tr(ps[0:NBK, 7, 0:P], pcm).then_inc(m_full, 1)
                pe.wait_ge(pv_out, 1)
                scores(0)
                m_bank(5)
                for g in range(G):
                    last = mm(ps[:, 7, 32 * g:32 * g + 32], vcb[0:NBK, g * HD:(g + 1) * HD], pcT[0:NBK, 32 * g:32 * g + 32])
                last.then_inc(m_full, 1)
                for g in range(G):
                    keys(1, g)
                    z_part(4 + g)
                scores(1)
                pe.wait_ge(wexp_out, i + 1)
                m_bank(6)
                bank = t_bank()
                for p in range(4):
                    last = tr(ps[:, bank, p * P:(p + 1) * P], S[:, p * P:(p + 1) * P])
                last.then_inc(t_full, 1)
                tr(ps[0:NS, 7, 0:P], S[:, WN:WN + NS]).then_inc(m_full, 1)
                for c in range(2, CHUNKS):
                    for g in range(G):
                        keys(c, g)
                        z_part(4 * c + g)
                    scores(c)
                    if c == 2:
                        m_bank(7)
                        t_emptied("probs_win", 0, 0)
                        pv(VWIN_USE, PT[0], True)
                        pv_new(1)
                pe.wait_ge(st_prompt, i * 4 + 4)
                for n in range(4):
                    z_part(20 + n)
                    prompt_scores(n // 2, n % 2)
                m_bank(8)
                for qt in range(2):
                    for t in range(2):
                        last = mm(ps[:, 7, (qt * 2 + t) * PBK:(qt * 2 + t + 1) * PBK], qst[:, t, qt * P:(qt + 1) * P],
                                  pcK[:, bass.ds(i // 2, 1), :].rearrange("p o n -> p (o n)"))
                last.then_inc(m_full, 1)
                for c in range(5):
                    if c < 4:
                        pe.wait_ge(sexp_out, i * 5 + (c + 1 if c < 3 else 5))
                    bank = t_bank(c == 4)
                    if c < 4:
                        for p in range(4):
                            last = tr(ps[:, bank, p * P:(p + 1) * P], S[:, SL + (4 * c + p) * P:SL + (4 * c + p + 1) * P])
                    else:
                        last = tr(ps[0:NS, bank, 0:P], S[:, SN:SN + NS])
                    last.then_inc(t_full, 1)
                    if c == 0:
                        m_bank(9)
                    if c >= 1:
                        t_emptied("probs_sel", c - 1, 0)
                        pv(VSEL_USE + 2 * (c - 1), PT[(c - 1) % 2], c == 1, c == 4)
                pv_new(0)
                for c, (kt, qt) in enumerate(((0, 0), (0, 1), (1, 1))):
                    pe.wait_ge(pp_ready, i * 3 + qt + 1)
                    bank = t_bank()
                    for a in range(4):
                        last = tr(ps[:, bank, a * P:(a + 1) * P], Sp[:, qt, a, kt * P:(kt + 1) * P])
                    last.then_inc(t_full, 1)
                pe.wait_ge(pp_ready, i * 3 + 3)
                bank = t_bank()
                for t in range(2):
                    for qt in range(2):
                        last = tr(ps[0:PBK, bank, (t * 2 + qt) * P:(t * 2 + qt + 1) * P], pcs[:, qt * 2 + t, :])
                last.then_inc(t_full, 1)
                for br in range(2):
                    m_bank(10 + br)
                    if br == 0:
                        t_emptied("prompt", 2, 0)
                    for t in range(2):
                        a = 2 * t + br
                        mm(ps[:, 7, t * NP:(t + 1) * NP], vst[:, br, 0, :], Pp[:, a, 0:NP], stop=False, skip_group_check=True)
                        last = mm(ps[:, 7, t * NP + P:(t + 1) * NP], vst[:, br, 1, :], Pp[:, a, NP:NP + P], start=False, skip_group_check=True)
                    last.then_inc(m_full, 1)
                m_bank(12)
                t_emptied("prompt_cmp", 0, 0)
                for t in range(2):
                    last = mm(ps[:, 7, t * NP:(t + 1) * NP], pvst[0:PBK, :], pcTp[0:PBK, t, :])
                last.then_inc(m_full, 1)
                assert t_at[0] == NTU

            pe.wait_ge(m_free, B * NMU + 1)
            pe.wait_ge(zu_free, B * 3 + 1)
            for br in (1, 2):
                for b in range(B):
                    last = tr(ps[:, 2 * (br - 1) + b // 4, b % 4 * P:(b % 4 + 1) * P], oS[:, br, b, :])
            last.then_inc(os_full, 1)
            with pe.Fori(0, 2) as i:
                for n in range(8):
                    u, half = n // 2, n % 2
                    if half == 0:
                        pe.wait_ge(y_free, i * 4 + u + 1)
                    for g in range(HALF):
                        split_wait(i * 32 + (G_OUT + n * HALF + g))
                        if u == 0:
                            pe.wait_ge(hn_out, PIECES * (GATED - 1) + HALF * half + g + 1)
                        for tt, (t0, nt) in enumerate(TOK):
                            for k in range(GK):
                                h = half * 8 + g * GK + k
                                last = products(ps[0:nt, 3 * (u % 2) + tt, 0:UNIT],
                                                (hn_hi[:, h, t0:t0 + nt], hn_lo[:, h, t0:t0 + nt]),
                                                granule(g, k, slice(0, UNIT)), h == 0, False)
                        last.then_inc(w_used, 1)
                    if half == 1:
                        pe.wait_ge(xst_out, i * 4 + u + 1)
                        for tt, (t0, nt) in enumerate(TOK):
                            for j in range(2):
                                last = mm(ps[0:nt, 3 * (u % 2) + tt, j * P:(j + 1) * P], xst[u % 2][:, j, t0:t0 + nt], ident[:],
                                          start=False, stop=True, skip_group_check=True)
                        last.then_inc(y_full, 1)

        @block.vector
        def _(dve):
            v = nc.vector
            link = Chain(dve, dchain)

            v.memset(cpad[:, :, 0:2], 0.0)
            for kt in range(0, KT, 2):
                dve.wait_ge(tp_full, kt + 1)
                v.tensor_copy(xT[:, kt, :], ps[:, kt % 8, 0:NT]).then_inc(tpd_free, 1)
            dve.wait_ge(vec_full, 1)
            v.tensor_copy(vecT[:], ps[:, 0, 0:100]).then_inc(vec_out, 1)
            dve.wait_ge(vec_full, 2)
            v.tensor_copy(stT.rearrange("p k c -> p (k c)"), ps[:, 1, 0:2 * B * KT]).then_inc(vec_out, 1)

            def rest(q, n, src):
                dve.wait_ge(hn_hid, PIECES * (n - 1) + q + 1)
                for d, x in src(q):
                    ins = v.tensor_tensor(hn_lo[d], x, as_f32(hn_hi[d]), ALU.subtract)
                ins.then_inc(hn_out, 1)

            def scale_rows(n, gcol, buf):
                for q in range(PIECES + 2):
                    if q >= 2:
                        rest(q - 2, n, normed(buf))
                    if q >= PIECES:
                        continue
                    if q >= len(buf):
                        dve.wait_ge(hn_out, PIECES * (n - 1) + q - len(buf) + 1)
                    for kt in range(GK * q, GK * q + GK):
                        ins = v.scalar_tensor_tensor(out=buf[q % len(buf)][:, kt % GK, :], in0=xT[:, kt, :],
                                                     scalar=vecT[:, gcol + kt:gcol + kt + 1], in1=rstd, op0=ALU.mult, op1=ALU.mult)
                    ins.then_inc(hn_raw, 1)

            def sum_squares(n, q):
                dve.wait_ge(sq_out, 4 * (n - 1) + q + 1)
                v.tensor_reduce(ssum[:, bass.ds(q, 1), :].rearrange("p o t -> p (o t)"),
                                xsq[:, bass.ds(q * 4, 4), :].rearrange("p k t -> p t k"), AX.X, ALU.add).then_inc(sum_out, 1)

            def norm(n, bank, gcol, filling):
                dve.wait_ge(sum_full, n)
                v.tensor_scalar(rstd, ps[:, bank, 0:NT], 1.0 / D, EPS, ALU.mult, ALU.add).then_inc(var_out, 1)
                dve.wait_ge(sd_out, n)
                link(v.reciprocal(rstd, rstd))
                scale_rows(filling, gcol, hnf)

            for q in range(4):
                sum_squares(1, q)
            dve.wait_ge(vec_out, 2)
            norm(1, 4, 0, NORM_A)
            dve.wait_ge(consts_in, 16 * N_CONSTS)
            dve.wait_ge(w2_zero, 1)
            for n, lo in enumerate((0, BLK)):
                v.tensor_copy(w2[lo:lo + BLK, :, :, n].rearrange("p c g -> p (c g)"), csb[lo:lo + BLK, 0, 0:2 * G]).then_inc(w2_done, 1)
            v.tensor_copy(tri[:], trif).then_inc(consts_used, 1)

            with dve.Fori(0, B) as i:
                link.enter(i, 14)

                def group(q):
                    pages = pg[q % CS]
                    dve.wait_ge(pg_full[q % CS], i * (16 * CPG * GPSQ // CS) + 16 * CPG * (q // CS + 1))
                    x = pages.rearrange("p t (c d) -> p (t c) d", d=HD)
                    link(v.tensor_tensor(x, x, wc[:].rearrange("p t c -> p (t c)").unsqueeze(2).to_broadcast([P, TPP * 2 * G, HD]), ALU.mult))
                    link(v.tensor_tensor(pages[:, 0:2], pages[:, 0:2], pages[:, 2:4], ALU.add))
                    v.tensor_tensor(pages[:, 0], pages[:, 0], pages[:, 1], ALU.add).then_inc(pg_summed, 1)

                group(0)
                group(1)
                done = lambda u: dve.wait_ge(w_used, (i * 8 + (1 + 2 * u + 2)) * HALF)
                done(1)
                dve.wait_ge(c_out, i + 1)
                v.tensor_tensor(cpad[:, :, 2:], csb[:, :, 0:NP], ps[:, 2:4, 0:NP], ALU.mult)
                for t in range(2):
                    ins = v.tensor_tensor(spad[:, t, :, 2:], csb[:, t, NP:NT].rearrange("p (b s) -> p b s", b=B),
                                          ps[:, 2 + t, NP:NT].rearrange("p (b s) -> p b s", b=B), ALU.mult)
                ins.then_inc(h_used, 1)
                for t in range(2):
                    ins = v.tensor_copy(spad[:, t, :, 0:2], stT[:, bass.ds(i * 2 + t, 1), :].rearrange("p o (b w) -> p (o b) w", w=2))
                link(ins)
                v.tensor_copy(cso[:, bass.ds(i * 2, 2), 0:2], cpad[:, :, NP:NP + 2])
                for t in range(2):
                    v.tensor_copy(cso[:, bass.ds(i * 2 + t, 1), 2:].rearrange("p o (b w) -> p (o b) w", w=2), spad[:, t, :, T:T + 2])
                for w in range(3):
                    for t in range(2):
                        tap = vecT[:, bass.ds(i * 2 + (48 + w * KT + t), 1)]
                        for o, a in ((bc[:, t, 0:NP], cpad[:, t, w:w + NP]),
                                     (bc[:, t, NP:NT].rearrange("p (b s) -> p b s", b=B), spad[:, t, :, w:w + T])):
                            if w == 0:
                                ins = v.tensor_scalar(o, a, tap, None, ALU.mult)
                            else:
                                ins = v.scalar_tensor_tensor(out=o, in0=a, scalar=tap, in1=o, op0=ALU.mult, op1=ALU.add)
                    link(ins)
                group(2)
                done(2)
                dve.wait_ge(e_out, i + 1)
                link(v.tensor_scalar(ez, ez, 1.0, None, ALU.add))
                link(v.reciprocal(ez, ez))
                ins = v.tensor_tensor(ez, ez, ps[:, 0:2, 0:NT], ALU.mult)
                ins.then_inc(zc_used, 1)
                group(3)
                done(3)
                ins = v.tensor_tensor(bc, bc, ps[:, 2:4, 0:NT], ALU.mult)
                ins.then_inc(b_used, 1)
                dve.wait_ge(b_used, i + 1 + 1)
                dve.wait_ge(zc_used, i + 1 + 1)
                v.tensor_tensor(yT[:, bass.ds(i * 2, 2), :], bc, ez, ALU.mult).then_inc(y_out, 1)
                dve.wait_ge(pg_used, i * GPSQ + (CS + GPSQ))
                v.tensor_copy(kcT[:, bass.ds(i, 1)].rearrange("p o g n -> p (o g n)"), ps[:, 6, 0:G * NBK]).then_inc(kc_out, 1)
            link.leave(B)

            for q in range(PIECES):
                rest(q, MIXED, mixed)
            with dve.Fori(0, 2) as i:
                for u in range(4):
                    dve.wait_ge(w_used, (i * 8 + (1 + U_MIX + 2 * u + 2)) * HALF)
                    x = xT[:, bass.ds(i * 8 + 2 * u, 2), :]
                    v.tensor_tensor(x, x, ps[:, 2 * (u % 2):2 * (u % 2) + 2, 0:NT], ALU.add).then_inc(x1_out, 1)
                    if u % 2 == 1:
                        sum_squares(2, i * 2 + u // 2)
            norm(2, 4, KT, NORM_KV)

            def head_norm(q, gain, outs_, before):
                dve.wait_ge(hs_full, q + 1)
                v.tensor_scalar(rs, ps[:, 4:6, 0:NT], 1.0 / HD, EPS, ALU.mult, ALU.add).then_inc(hv_out, 1)
                dve.wait_ge(hsd_out, q + 1)
                link(v.reciprocal(rs, rs))
                link(v.scalar_tensor_tensor(out=kn, in0=raw, scalar=gain, in1=rs, op0=ALU.mult, op1=ALU.mult))
                two = lambda a: a.unsqueeze(1).to_broadcast([a.shape[0], 2, NT])
                v.tensor_tensor(ra, kn, two(cosT[:]), ALU.mult)
                v.tensor_tensor(sq[0:64], kn[64:128], two(sinT[64:128]), ALU.mult)
                link(v.tensor_tensor(sq[64:128], kn[0:64], two(sinT[0:64]), ALU.mult))
                before()
                for o, sel in outs_[:-1]:
                    v.tensor_tensor(o, sel(ra), sel(sq), ALU.add)
                o, sel = outs_[-1]
                v.tensor_tensor(o, sel(ra), sel(sq), ALU.add).then_inc(rope_out, 1)

            with dve.Fori(0, 3) as i:
                link.enter(i, 6)
                for gp in range(2):
                    def before(gp=gp):
                        if gp == 0:
                            dve.wait_ge(kcp_out, i + 1)
                            dve.wait_ge(kt_full, i * 3 + 1)
                    head_norm(i * 2 + gp, vecT[:, bass.ds(i + 96, 1)], [(kro[:, 2 * gp:2 * gp + 2, :], lambda a: a)], before)
                dve.wait_ge(w_used, (i * 8 + (1 + U_KV + 8)) * HALF)
                for tt, (t0, nt) in enumerate(TOK):
                    v.tensor_copy(vto[0:nt, bass.ds(i, 1), tt, :].rearrange("p o c -> p (o c)"), ps[0:nt, VT_BANKS[tt], :]).then_inc(vt_out, 1)
            link.leave(3)
            dve.wait_ge(rope_out, 7)
            scale_rows(NORM_B, 2 * KT, hnf_b)
            dve.wait_ge(pc_full, 1)
            v.tensor_copy(pcK.rearrange("p g n -> p (g n)"), ps[:, 6, 0:G * PBK]).then_inc(pc_out, 1)
            v.tensor_copy(pcvT[:].rearrange("p g n -> p (g n)"), ps[:, 7, 0:G * PBK]).then_inc(pc_out, 1)
            dve.wait_ge(ge_out, 1)
            v.tensor_scalar(gd[0:GATES], gd[0:GATES], 1.0, None, ALU.add).then_inc(gd_out, 1)

            with dve.Fori(0, 2) as i:
                link.enter(i, 12)
                for u in range(4):
                    h = i * 8 + 2 * u
                    outs_ = [(qP[:, bass.ds(h, 2), :], lambda a: a[:, :, 0:NP])]
                    for t in range(2):
                        outs_.append((qS[:, :, bass.ds((h + t) * T, T)],
                                      lambda a, t=t: a[:, t, NP:NT].rearrange("p (b s) -> p b s", b=B)))
                    head_norm(i * 4 + 6 + u, vecT[:, 99:100], outs_, lambda: None)
            link.leave(2)
            dve.wait_ge(pv_full, 1)
            v.tensor_copy(pcV.rearrange("p g d -> p (g d)")[0:PBK], ps[0:PBK, 6, :]).then_inc(pv_out, 1)
            dve.wait_ge(gates_out, 16)
            dve.wait_ge(kv_store, 16 * 12)
            dve.wait_ge(x1_store, 16)
            dve.wait_ge(vts_out, 2)

            PER_MAIN = 28
            with dve.Fori(0, B) as i:
                link.enter(i, PER_MAIN)
                st = lambda a, n=1: stat[:, a:a + n]

                def m_copy(n, out, in_):
                    dve.wait_ge(m_full, i * NMU + n + 1)
                    v.tensor_copy(out, in_).then_inc(m_free, 1)
                    dve.wait_ge(m_free, i * NMU + n + 1)

                def negmax(a, src):
                    link(v.tensor_reduce(st(a), src, AX.X, ALU.max, negate=True))
                    return v.tensor_scalar(st(a), st(a), SCALE, None, ALU.mult)

                def normalise(a, probs):
                    link(v.reciprocal(st(a + 2), st(a + 1)))
                    return v.tensor_scalar(probs, probs, st(a + 2), None, ALU.mult)

                def output(n, br, total):
                    link(v.reciprocal(total, total))
                    dve.wait_ge(m_full, i * NMU + n + 1)
                    v.tensor_scalar(oS[:, br, bass.ds(i, 1), :].rearrange("p o c -> p (o c)"), ps[:, 7, 0:HD], total, None, ALU.mult).then_inc(m_free, 1)

                def z_unit(u):
                    dve.wait_ge(ze_out, i * 3 + u + 1)
                    dve.wait_ge(gb_full, i * 48 + 16 * (u + 1))
                    v.scalar_tensor_tensor(out=ezm, in0=ezm, scalar=1.0, in1=gbc, op0=ALU.add, op1=ALU.mult).then_inc(gb_used, 1)
                    dve.wait_ge(gb_used, i * 3 + u + 1)
                    link(v.reciprocal(ezm, ezm))
                    bank = 2 * (u % 2)
                    v.tensor_tensor(zgP[:, u], ezm[:, :, 0:NP], ps[:, bank:bank + 2, 0:NP], ALU.mult)
                    v.tensor_tensor(zS[:, u, bass.ds(i * 2, 2), :], ezm[:, :, NP:NT], ps[:, bank:bank + 2, NP:NT], ALU.mult).then_inc(zu_free, 1)

                def s_wait(n):
                    dve.wait_ge(s_full, i * NSU + n + 1)

                def sel_scores(c):
                    s_wait(c)
                    lo = 8 * (c - 1)
                    v.tensor_tensor(S[:, SL + lo * BLK:SL + (lo + 8) * BLK].rearrange("p (n l) -> p n l", l=BLK),
                                    ps[:, 6, :].rearrange("p (n l) -> p n l", l=BLK),
                                    bmask[:, lo:lo + 8].unsqueeze(2).to_broadcast([P, 8, BLK]), ALU.add).then_inc(s_free, 1)
                    dve.wait_ge(s_free, i * NSU + c + 2)
                    end = lo * BLK + 8 * BLK + (NS if c == 4 else 0)
                    link(v.tensor_reduce(st(SMAX + c - 1), S[:, SL + lo * BLK:SL + end], AX.X, ALU.max))

                m_copy(1, msb, ps[:, 7, 0:192])
                nm = newmask[:, bass.ds(i, 1), :].rearrange("p o s -> p (o s)")
                v.tensor_tensor(S[:, WN:WN + NS], msb[:, 64:128], nm, ALU.add)
                v.tensor_tensor(S[:, SN:SN + NS], msb[:, 128:192], nm, ALU.add)
                negmax(0, msb[:, 0:NBK]).then_inc(cexp_in, 1)
                dve.wait_ge(cexp_out, i + 1)
                normalise(0, pcm).then_inc(p_ready, 1)
                m_copy(2, psc, ps[:, 7, 0:NBK])
                m_copy(3, vcb[0:NBK], ps[0:NBK, 7, :])
                m_copy(4, pcT[0:NBK], ps[0:NBK, 7, 0:P])
                s_wait(0)
                v.tensor_tensor(S[:, 0:T], ps[:, 6, 0:T], winmask[:], ALU.add)
                v.tensor_copy(S[:, T:WIN], ps[:, 6, T:WIN]).then_inc(s_free, 1)
                dve.wait_ge(s_free, i * NSU + 2)
                m_copy(5, oS[:, 0, bass.ds(i, 1), :].rearrange("p o c -> p (o c)"), ps[:, 7, 0:H * T])
                negmax(3, S[:, 0:WIN + NS]).then_inc(wexp_in, 1)
                s_i = psc[:, 1:1 + MID].unsqueeze(1).to_broadcast([P, MID, MID])
                s_j = psc[:, 1:1 + MID].unsqueeze(2).to_broadcast([P, MID, MID])
                v.tensor_tensor(gt, s_i, s_j, ALU.is_gt)
                link(v.tensor_tensor(eq, s_i, s_j, ALU.is_equal))
                link(v.tensor_tensor(eq, eq, tri[:], ALU.mult))
                link(v.tensor_tensor(gt, gt, eq, ALU.add))
                v.memset(bmask[:, 0:1], 0.0)
                v.memset(bmask[:, NBK - 1:NBK], 0.0)
                link(v.tensor_reduce(bmask[:, 1:1 + MID], gt, AX.X, ALU.add))
                v.tensor_scalar(bmask[:, 1:1 + MID], bmask[:, 1:1 + MID], float(KEEP), NEG, ALU.is_ge, ALU.mult).then_inc(rank_out, 1)
                dve.wait_ge(rank_out, i + 1)
                sel_scores(1)
                m_copy(6, PTn[0:NS, 1, :], ps[0:NS, 7, 0:P])
                z_unit(0)
                sel_scores(2)
                dve.wait_ge(wexp_out, i + 1)
                output(7, 2, st(4))
                sel_scores(3)
                z_unit(1)
                sel_scores(4)
                negmax(6, st(SMAX, 4)).then_inc(sexp_in, 1)

                def prompt_scores(qt, t):
                    s_wait(CHUNKS + 2 * qt + t)
                    bank = ps[:, 6, :].rearrange("p (a k) -> p a k", a=2)
                    if qt:
                        v.tensor_copy(Sp[:, qt, 2 * t:2 * t + 2, 0:P], bank[:, :, 0:P])
                    v.tensor_tensor(Sp[:, qt, 2 * t:2 * t + 2, qt * P:(qt + 1) * P], bank[:, :, qt * P:(qt + 1) * P],
                                    causal[:].unsqueeze(1).to_broadcast([P, 2, P]), ALU.add).then_inc(s_free, 1)

                def prompt_max(qt):
                    dve.wait_ge(s_free, i * NSU + CHUNKS + 2 * qt + 3)
                    link(v.tensor_reduce(st(16 + 4 * qt, 4), Sp[:, qt, :, 0:(qt + 1) * P], AX.X, ALU.max, negate=True))
                    v.tensor_scalar(st(16 + 4 * qt, 4), st(16 + 4 * qt, 4), SCALE, None, ALU.mult).then_inc(pexp_in, 1)

                def prompt_scale(qt):
                    dve.wait_ge(pexp_out, i * 3 + qt + 1)
                    link(v.reciprocal(st(32 + 4 * qt, 4), st(24 + 4 * qt, 4)))
                    a = Sp[:, qt, :, 0:(qt + 1) * P]
                    v.tensor_tensor(a, a, st(32 + 4 * qt, 4).unsqueeze(2).to_broadcast([P, 4, (qt + 1) * P]), ALU.mult).then_inc(pp_ready, 1)

                prompt_scores(0, 0)
                prompt_scores(0, 1)
                prompt_max(0)
                prompt_scores(1, 0)
                prompt_scores(1, 1)
                prompt_max(1)
                dve.wait_ge(m_full, i * NMU + 8 + 1)
                four = lambda a: a.unsqueeze(2).to_broadcast([P, 4, PBK])
                mask = lambda a: a[:].unsqueeze(2).to_broadcast([P, 2, 2, PBK])
                pcs4 = pcs.rearrange("p (q t) n -> p q t n", t=2)
                v.tensor_tensor(pcs4, ps[:, 7, 0:4 * PBK].rearrange("p (q t n) -> p q t n", q=2, t=2), mask(pcmask), ALU.add).then_inc(m_free, 1)
                dve.wait_ge(m_free, i * NMU + 9)
                link(v.tensor_reduce(st(40, 4), pcs, AX.X, ALU.max))
                v.tensor_tensor(pcs, pcs, four(st(40, 4)), ALU.subtract).then_inc(pexp_in, 1)
                prompt_scale(0)
                z_unit(2)
                prompt_scale(1)
                dve.wait_ge(pexp_out, i * 3 + 3)
                link(v.tensor_reduce(st(44, 4), pcs, AX.X, ALU.add))
                link(v.reciprocal(st(48, 4), st(44, 4)))
                link(v.tensor_tensor(pcs, pcs, four(st(48, 4)), ALU.mult))
                v.tensor_tensor(pcs4, pcs4, mask(pckeep), ALU.mult).then_inc(pp_ready, 1)
                dve.wait_ge(sexp_out, i * 5 + 5)
                link(v.tensor_reduce(st(7), st(SSUM, 5), AX.X, ALU.add))
                output(9, 1, st(7))
                o = qP[:, bass.ds(i * 2, 2), :]
                for n, br in ((10, 1), (11, 2), (12, 0)):
                    dve.wait_ge(m_full, i * NMU + n + 1)
                    pso = ps[:, 7, :].rearrange("p (t q) -> p t q", t=2)
                    v.tensor_tensor(o if n == 10 else otmp, zgP[:, br], pso, ALU.mult).then_inc(m_free, 1)
                    dve.wait_ge(m_free, i * NMU + n + 1)
                    if n > 10:
                        link(v.tensor_tensor(o, o, otmp, ALU.add))
            link.leave(B)

            hbt = lambda a: a.rearrange("p h (b s) -> p b h s", s=T)
            dve.wait_ge(os_full, 1)
            for br in range(3):
                ins = None
                for b in range(B):
                    o3 = hbt(oTs if br == 0 else oadd)[:, b]
                    o = oS[:, 0, b, :] if br == 0 else ps[:, 2 * (br - 1) + b // 4, b % 4 * P:(b % 4 + 1) * P]
                    ins = v.tensor_tensor(o3, o.rearrange("p (h s) -> p h s", s=T), hbt(zS[:, br])[:, b], ALU.mult)
                link(ins)
                if br == 1:
                    link(v.tensor_tensor(oTs, oTs, oadd, ALU.add))
            v.tensor_tensor(oTs, oTs, oadd, ALU.add).then_inc(ots_out, 1)
            dve.wait_ge(ots_out, 1)
            for q in range(PIECES):
                rest(q, GATED, gated)

        @block.scalar
        def _(act):
            s = nc.scalar
            link = Chain(act, achain)

            for kt in range(1, KT, 2):
                act.wait_ge(tp_full, kt + 1)
                s.copy(xT[:, kt, :], ps[:, kt % 8, 0:NT]).then_inc(tpa_free, 1)

            def lead_w(i, before, lo, hi):
                for g in range(lo, hi):
                    if g % GPS == 0:
                        act.wait_ge(w_full[g // GPS % WS], i * (16 * 32 // (WS * GPS)) + 16 * ((before + g) // (WS * GPS) + 1))
                    act.wait_ge(w_used, i * 32 + (before + g + 1))
                    s.copy(w_hi[:, g % HS], slot[g // GPS % WS][:, g % GPS * GK:(g % GPS + 1) * GK, :]).then_inc(hi_out, 1)

            def lead(n, src, ready=None, beside=lambda q: None):
                for q in range(PIECES):
                    if ready:
                        act.wait_ge(ready[0], ready[1] + q + 1)
                    for d, x in src(q):
                        ins = s.copy(hn_hi[d], x)
                    ins.then_inc(hn_hid, 1)
                    beside(q)

            def raws(n):
                return hn_raw, PIECES * RAWS.index(n)

            def square(q):
                s.activation(xsq[:, bass.ds(q * 4, 4), :], xT[:, bass.ds(q * 4, 4), :], ACT.Square).then_inc(sq_out, 1)

            def norm(n):
                act.wait_ge(var_out, n)
                s.activation(rstd, rstd, ACT.Sqrt).then_inc(sd_out, 1)

            for q in range(4):
                act.wait_ge(tpd_free, 2 * q + 2)
                act.wait_ge(tpa_free, 2 * q + 2)
                square(q)
            lead_w(0, 0, 0, HS)
            norm(1)
            lead(NORM_A, normed(hnf), raws(NORM_A))

            with act.Fori(0, B) as i:
                lead_w(i, 0, HS, 12)
                act.wait_ge(w_used, (i * 8 + (1 + 2)) * HALF)
                act.wait_ge(w2_done, 2)
                act.wait_ge(h_used, i + 1)
                s.copy(csb, ps[:, 0:2, 0:NT]).then_inc(c_out, 1)
                lead_w(i, 0, 12, 28)
                act.wait_ge(w_used, (i * 8 + (1 + 6)) * HALF)
                act.wait_ge(y_out, i + 1)
                s.activation(ez, ps[:, 0:2, 0:NT], ACT.Exp, scale=-1.0).then_inc(e_out, 1)
                lead_w(i, 0, 28, 32 + HS)
                act.wait_ge(pg_used, i * GPSQ + (CS + GPSQ))
                s.copy(vcT[:, bass.ds(i, 1)].rearrange("p o g n -> p (o g n)"), ps[:, 7, 0:G * NBK]).then_inc(vc_out, 1)

            act.wait_ge(w_used, HS + U_MIX * HALF)
            lead(MIXED, mixed, (y_out, 1))
            with act.Fori(0, 2) as i:
                at = U_MIX * HALF
                lead_w(i, at, HS, 20)
                act.wait_ge(x1_out, i * 4 + 4)
                square(i * 2)
                lead_w(i, at, 20, 32 + HS)
                act.wait_ge(x1_out, i * 4 + 6)
                square(i * 2 + 1)
            norm(2)
            at = U_KV * HALF
            lead(NORM_KV, normed(hnf), raws(NORM_KV), lambda q: lead_w(0, at, q + 2, q + 3) if q >= 2 else None)
            for n in range(4):
                act.wait_ge(cs_full, n + 1)
                s.copy(crow[0:18, n * 512:(n + 1) * 512], ps[0:18, CS_BANKS[n], :]).then_inc(cs_out, 1)
            act.wait_ge(cs_out, 4)
            act.dma_start(conv_p.rearrange("l b w d -> (l b w) d"), crow[0:2, :]).then_inc(cs_store, 16)
            act.dma_start(conv_s.rearrange("l b w d -> (l b w) d"), crow[2:18, :]).then_inc(cs_store, 16)

            act.dma_start(x1_dram.rearrange("p (k t) -> p k t", k=KT), xT).then_inc(x1_store, 16)

            def squares(q, use, bank):
                act.wait_ge(w_used, use * HALF)
                act.wait_ge(rope_out, q + 1)
                s.copy(raw, ps[:, bank:bank + 2, 0:NT])
                s.activation(sq, ps[:, bank:bank + 2, 0:NT], ACT.Square).then_inc(sqr_out, 1)

            def root(q):
                act.wait_ge(hv_out, q + 1)
                s.activation(rs, rs, ACT.Sqrt).then_inc(hsd_out, 1)

            for i in range(3):
                lead_w(i, at, HS if i else PIECES + 2, 12)
                squares(i * 2, i * 8 + (1 + U_KV + 2), 0)
                lead_w(i, at, 12, 16)
                root(i * 2)
                lead_w(i, at, 16, 22)
                squares(i * 2 + 1, i * 8 + (1 + U_KV + 4), 2)
                lead_w(i, at, 22, 24)
                root(i * 2 + 1)
                lead_w(i, at, 24, 32)
                for tt, (t0, nt) in enumerate(TOK):
                    act.wait_ge(kt_full, i * 3 + tt + 1 + 1)
                    s.copy(kto[0:nt, bass.ds(i, 1), tt, :].rearrange("p o c -> p (o c)"), ps[0:nt, KT_BANKS[tt], :]).then_inc(kt_out, 1)
                if i < 2:
                    lead_w(i, at, 32, 32 + HS)
                act.wait_ge(cs_store, 32)
                s.copy(kTs[:, bass.ds(i // 2, 1)].rearrange("p o g t -> p (o g) t"), kro).then_inc(kcp_out, 1)
            act.wait_ge(wg_in, 16)
            act.wait_ge(w_used, HS + U_QUERY * HALF)
            s.copy(wg_hi, wgt).then_inc(wg_out, 1)
            lead(NORM_B, normed(hnf_b), raws(NORM_B))
            act.wait_ge(g_full, 1)
            lead_w(0, U_QUERY * HALF, 0, HS)
            s.activation(gd[0:GATES], ps[0:GATES, 5, 0:NT], ACT.Exp, scale=-1.0).then_inc(ge_out, 1)
            act.wait_ge(kt_out, 3 + 9)
            act.wait_ge(vt_out, 10)
            s.copy(vts[:, :, 0:2, :], vto[:, 1:3, 0:2, :]).then_inc(vts_out, 1)
            s.copy(vts[0:NS, :, 2, :], vto[0:NS, 1:3, 2, :]).then_inc(vts_out, 1)
            for br in range(3):
                for c, src in ((0, kto), (1, vto)):
                    if br < 2:
                        dp = rows_p[0, :, 2 * br + c].rearrange("(t p) g d -> p t (g d)", p=P)
                        ds_ = rows_s[:, :, 2 * br + c].rearrange("b t g d -> (b t) (g d)")
                        act.dma_start(dp, src[:, br, 0:2, :]).then_inc(kv_store, 16)
                        act.dma_start(ds_, src[0:NS, br, 2, :]).then_inc(kv_store, 16)
                    else:
                        dp = win_p[0, :, c].rearrange("(t p) g d -> p t (g d)", p=P)
                        act.dma_start(dp, src[:, br, 0:2, :]).then_inc(kv_store, 16)
                        act.dma_start(win_s[:, WIN - T:WIN, c].rearrange("b t g d -> b t (g d)"), src[0:NS, br, 2, :]).then_inc(kv_store, 16)

            for i in range(2):
                at, last = U_QUERY * HALF, i == 1
                lead_w(i, at, HS, 12)
                if i == 0:
                    act.wait_ge(gd_out, 1)
                    act.dma_start(gates_dram, gd[0:GATES]).then_inc(gates_out, 16)
                for u in range(4):
                    squares(i * 4 + 6 + u, i * 8 + (1 + U_QUERY + 2 * u + 2), 2 * (u % 2))
                    lead_w(i, at, 8 * u + 12, min(8 * u + 15, 32 if last else 32 + HS))
                    root(i * 4 + 6 + u)
                    lead_w(i, at, 8 * u + 15, min(8 * u + 20, 32 if last else 32 + HS))
            act.wait_ge(kv_store, 16 * 12)
            act.wait_ge(rope_out, 15)
            act.wait_ge(gates_out, 16)
            act.wait_ge(x1_store, 16)
            act.wait_ge(vts_out, 2)

            with act.Fori(0, B) as i:
                st = lambda a, n=1: stat[:, a:a + n]

                def empty(lo, hi):
                    for n in range(lo, hi):
                        if T_USES[n][0] == "probs_win":
                            act.wait_ge(rank_out, i + 1)
                        empty_t(act, s.copy, n, i)

                def exp_z(u):
                    act.wait_ge(w_used, i * ZG + (HS + G_Z + 8 * u + 8))
                    act.wait_ge(zu_free, i * 3 + u + 1)
                    s.activation(ezm, ps[:, 2 * (u % 2):2 * (u % 2) + 2, 0:NT], ACT.Exp, scale=-1.0).then_inc(ze_out, 1)

                def exp_prompt(qt):
                    act.wait_ge(pexp_in, i * 3 + qt + 1)
                    for a in range(4):
                        x = Sp[:, qt, a, 0:(qt + 1) * P]
                        ins = s.activation(x, x, ACT.Exp, bias=st(16 + 4 * qt + a), scale=SCALE, accum_out=st(24 + 4 * qt + a))
                    ins.then_inc(pexp_out, 1)

                empty(0, 1)
                act.wait_ge(cexp_in, i + 1)
                s.activation(pcm, msb[:, 0:NBK], ACT.Exp, bias=st(0), scale=SCALE, accum_out=st(1)).then_inc(cexp_out, 1)
                empty(1, 5)
                act.wait_ge(wexp_in, i + 1)
                s.activation(S[:, 0:WIN + NS], S[:, 0:WIN + NS], ACT.Exp, bias=st(3), scale=SCALE, accum_out=st(4)).then_inc(wexp_out, 1)
                empty(5, 9)
                exp_z(0)
                empty(9, 17)
                exp_z(1)
                empty(17, 21)
                act.wait_ge(sexp_in, i + 1)
                for c in range(5):
                    x = S[:, SL + c * 512:min(SL + (c + 1) * 512, SN + NS)]
                    s.activation(x, x, ACT.Exp, bias=st(6), scale=SCALE, accum_out=st(SSUM + c)).then_inc(sexp_out, 1)
                empty(21, 22)
                exp_prompt(0)
                empty(22, 23)
                exp_z(2)
                empty(23, 24)
                exp_prompt(1)
                empty(24, 25)
                act.wait_ge(pexp_in, i * 3 + 3)
                s.activation(pcs, pcs, ACT.Exp, scale=SCALE).then_inc(pexp_out, 1)
                empty(25, NTU)

            act.wait_ge(m_free, B * NMU + 1)
            act.wait_ge(w_used, HS + G_OUT)
            act.wait_ge(ots_out, 1)
            lead(GATED, gated)
            for n in range(8):
                act.wait_ge(y_full, n + 1)
                if n >= 2:
                    act.wait_ge(y_stored[n % 2], 32 * (n // 2))
                for tt, (t0, nt) in enumerate(TOK):
                    ins = s.copy(ysb[n % 2][0:nt, tt, :], ps[0:nt, 3 * (n % 2) + tt, 0:UNIT])
                ins.then_inc(y_free, 1)
                act.wait_ge(y_free, 2 + n + 1)
                cols = slice(n * UNIT, (n + 1) * UNIT)
                act.dma_start(y_p[0, :, cols].rearrange("(t p) c -> p t c", p=P), ysb[n % 2][:, 0:2, :]).then_inc(y_stored[n % 2], 16)
                act.dma_start(y_s[:, :, cols].rearrange("b t c -> (b t) c"), ysb[n % 2][0:NS, 2, :]).then_inc(y_stored[n % 2], 16)


_INS = ['x_prompt', 'x_sample', 'state_conv', 'cache_kv', 'state_win', 'page_table', 'g_a', 'w_in_a', 'conv_w', 'w_out_a',
        'g_kv', 'w_kv', 'g_k', 'w_cmp', 'g_b', 'w_qz', 'g_q', 'w_out_b']
_OUTS = [(1, NP, D), (B, T, D), (1, 1, 2, D), (1, B, 2, D), (1, NP, 4, G, HD), (B, T, 4, G, HD), (1, NP, 2, G, HD),
         (B, WIN, 2, G, HD)]


def tables():
    f = np.float32
    half = HD // 2
    inv = (10000.0 ** (-np.arange(half) / half)).astype(f)
    pos = np.concatenate([np.arange(NP), np.tile(PAST + np.arange(T), B)]).astype(f)
    ang = (pos[None, :] * inv[:, None]).astype(np.float64)
    row, t = np.arange(P), np.arange(P) % T
    new_b, new_t = np.arange(NS) // T, np.arange(NS) % T
    ok_new = (new_b[None, None] == np.arange(B)[None, :, None]) & (new_t[None, None] <= t[:, None, None])
    blk_end = np.arange(PBK) * BLK + BLK - 1
    ok_cmp = blk_end[None, None] <= row[:, None, None] + P * np.arange(2)[None, :, None]
    hide = lambda ok: np.where(ok, 0.0, NEG).astype(f)
    j = np.arange(MID)
    return {
        "ident": np.eye(P, dtype=f),
        "ones": np.ones((P, P), f),
        "inblk": (row[:, None] // (BLK // TPP) == np.arange(P // (BLK // TPP))[None]).astype(f),
        "group": ((row[:, None] // 32 == row[None] // 32) & (t[:, None] == t[None])).astype(f),
        "causal": hide(row[None] <= row[:, None]),
        "cosT": np.tile(np.cos(ang), (2, 1)).astype(f),
        "sinT": np.concatenate([np.sin(ang), -np.sin(ang)]).astype(f),
        "newmask": hide(ok_new),
        "winmask": hide(np.arange(T)[None] > t[:, None]),
        "tri": np.tile((j[None] < j[:, None]).astype(f)[None], (P, 1, 1)),
        "pcmask": hide(ok_cmp),
        "pckeep": ok_cmp.astype(f),
    }


def kernel(**inputs):
    import concourse.bacc as bacc
    from concourse.bass_utils import run_bass_kernel_spmd

    nc = bacc.Bacc("TRN2", target_bir_lowering=False, num_devices=1, dynamic_dma_scratch_size=1024)
    arrays, ins = {}, []
    for name in _INS:
        a = np.ascontiguousarray(inputs[name])
        arrays[f"in_{name}"] = a
        ins.append(nc.dram_tensor(f"in_{name}", a.shape, mybir.dt.from_np(a.dtype), kind="ExternalInput").ap())
    consts = {}
    for name, a in tables().items():
        arrays[f"table_{name}"] = a
        consts[name] = nc.dram_tensor(f"table_{name}", a.shape, F32, kind="ExternalInput").ap()
    outs = [nc.dram_tensor(f"out_{n}", shape, F32, kind="ExternalOutput").ap() for n, shape in enumerate(_OUTS)]
    scratch = [nc.dram_tensor("gates", (GATES, NT), F32, kind="Internal").ap(),
               nc.dram_tensor("x1", (P, KT * NT), F32, kind="Internal").ap()]
    build(nc, ins, consts, outs, scratch)
    r = run_bass_kernel_spmd(nc, [arrays], core_ids=[0])
    return tuple(r.results[0][f"out_{n}"] for n in range(len(_OUTS)))
```
